# Optimizing a Trainium2 kernel written in Bass

```python
import jax, jax.numpy as jnp
from jax import lax
import numpy as np
import math
import functools
import jax
import jax.numpy as jnp

D_MODEL = 1024
BATCH = 1
SEQ = 256
DEPTH = 2

POOL_WINDOWS = (2, 4, 8, 16)
POOL_GROUP = 64
POOL_WIDTH = POOL_GROUP * len(POOL_WINDOWS)
ATTN_HEADS = 4
ATTN_HEAD_DIM = 64
ATTN_WIDTH = ATTN_HEADS * ATTN_HEAD_DIM
IDX_HEADS = 8
IDX_DIM = 64
TOPK_MAX = 256
Q_BLOCK = 128
HGRN_HEADS = 4
HGRN_EXPAND = 128
HGRN_HEAD_V = 128
HGRN_KW = HGRN_HEADS * HGRN_EXPAND
HGRN_VW = HGRN_HEADS * HGRN_HEAD_V
HGRN_CHUNK = 64
KEY_MAX = 1.0 - 1e-6
REL_BUCKETS = 32
REL_MAX_DIST = 128
D_FF = 2816
N_SUB = 3
DN_ALPHA = (2 * DEPTH) ** 0.25
DN_BETA = (8 * DEPTH) ** -0.25
LN_EPS = 1e-5
RMS_EPS = 1e-6

MIX_WIDTH = POOL_WIDTH + ATTN_WIDTH + HGRN_VW
MIX_IN_WIDTHS = (POOL_WIDTH, ATTN_WIDTH, ATTN_WIDTH, ATTN_WIDTH, IDX_HEADS * IDX_DIM, IDX_DIM, IDX_HEADS,
                 HGRN_KW, HGRN_KW, HGRN_VW, HGRN_VW, 3 * D_MODEL)
MIX_IN_WIDTH = sum(MIX_IN_WIDTHS)
MIX_SPLITS = tuple(int(s) for s in np.cumsum(MIX_IN_WIDTHS)[:-1])


def layer_norm(x, g, b):
    x32 = x.astype(jnp.float32)
    mu = jnp.mean(x32, axis=-1, keepdims=True)
    var = jnp.mean(jnp.square(x32 - mu), axis=-1, keepdims=True)
    y = (x32 - mu) * lax.rsqrt(var + LN_EPS)
    return (y * g.astype(jnp.float32) + b.astype(jnp.float32)).astype(x.dtype)

def swiglu(h, w_in, w_out):
    gate, up = jnp.split(h @ w_in, 2, axis=-1)
    return (jax.nn.silu(gate) * up) @ w_out

def modulate(h, mod, j):
    return h * (1 + mod[:, j, 1][:, None, :]) + mod[:, j, 0][:, None, :]

def sub_gate(mod, j):
    return 1 + mod[:, j, 2][:, None, :]

def pool_mixer(a, pool_w, pool_scale):
    B, S, _ = a.shape
    a32 = a.astype(jnp.float32)
    P = jnp.pad(jnp.cumsum(a32, axis=1), ((0, 0), (1, 0), (0, 0)))
    pos1 = jnp.arange(1, S + 1)
    means = []
    for g, w in enumerate(POOL_WINDOWS):
        Pg = P[..., g * POOL_GROUP:(g + 1) * POOL_GROUP]
        lead = Pg[:, 1:]
        lag = jnp.concatenate([jnp.zeros_like(Pg[:, :w - 1]), Pg[:, :S + 1 - w]], axis=1)
        cnt = jnp.minimum(pos1, w).astype(jnp.float32)
        means.append((lead - lag) / cnt[None, :, None])
    pooled = jnp.stack(means, axis=2)
    d = (pooled - a32.reshape(B, S, len(POOL_WINDOWS), POOL_GROUP)).astype(a.dtype)
    y = jnp.einsum('bsgc,gcd->bsgd', d, pool_w)
    return y.reshape(B, S, POOL_WIDTH) * pool_scale

def t5_bucket(dist):
    max_exact = REL_BUCKETS // 2
    d32 = jnp.maximum(dist, 1).astype(jnp.float32)
    large = max_exact + (jnp.log(d32 / max_exact) / np.log(REL_MAX_DIST / max_exact)
                         * (REL_BUCKETS - max_exact)).astype(jnp.int32)
    large = jnp.minimum(large, REL_BUCKETS - 1)
    return jnp.where(dist < max_exact, dist, large)

def sparse_attention(q, k, v, q_idx, k_idx, w_idx, rel_bias):
    B, S, H, dh = q.shape
    top_k = min(TOPK_MAX, S // 4)
    n_blocks = S // Q_BLOCK
    scale = dh ** -0.5
    idx_scale = (IDX_DIM ** -0.5) * (IDX_HEADS ** -0.5)
    key_pos = jnp.arange(S)

    def block(i):
        q0 = i * Q_BLOCK
        qb = lax.dynamic_slice_in_dim(q, q0, Q_BLOCK, axis=1)
        qib = lax.dynamic_slice_in_dim(q_idx, q0, Q_BLOCK, axis=1)
        wb = lax.dynamic_slice_in_dim(w_idx, q0, Q_BLOCK, axis=1)
        qpos = q0 + jnp.arange(Q_BLOCK)
        logit_idx = jnp.einsum('bqhd,bsd->bqhs', qib, k_idx)
        score = jnp.einsum('bqh,bqhs->bqs', wb, jax.nn.relu(logit_idx)).astype(jnp.float32) * idx_scale
        causal = key_pos[None, :] <= qpos[:, None]
        score = jnp.where(causal[None], score, -jnp.inf)
        _, sel = lax.top_k(score, top_k)
        k_sel = jax.vmap(lambda kk, ii: kk[ii])(k, sel)
        v_sel = jax.vmap(lambda vv, ii: vv[ii])(v, sel)
        logits = jnp.einsum('bqhd,bqkhd->bhqk', qb, k_sel).astype(jnp.float32) * scale
        dist = qpos[None, :, None] - sel
        bias = rel_bias[t5_bucket(jnp.maximum(dist, 0))].astype(jnp.float32)
        logits = logits + jnp.transpose(bias, (0, 3, 1, 2))
        logits = jnp.where((dist >= 0)[:, None], logits, -jnp.inf)
        p = jax.nn.softmax(logits, axis=-1).astype(v.dtype)
        return jnp.einsum('bhqk,bqkhd->bqhd', p, v_sel)

    out = lax.map(block, jnp.arange(n_blocks))
    return jnp.transpose(out, (1, 0, 2, 3, 4)).reshape(B, S, H * dh)

def hgrn2(q, f_logit, i_val, g_out, lb, norm_g):
    B, S, _ = q.shape
    C = HGRN_CHUNK
    NC = S // C
    z = f_logit.astype(jnp.float32)
    lb = lb.astype(jnp.float32)
    key = (1 - lb) * jax.nn.sigmoid(-z)
    log_f = jnp.log1p(-jnp.minimum(key, KEY_MAX))
    qf = jax.nn.silu(q.astype(jnp.float32))

    def to_chunks(t, d):
        return jnp.transpose(t.reshape(B, NC, C, HGRN_HEADS, d), (1, 0, 3, 2, 4))

    qc = to_chunks(qf, HGRN_EXPAND)
    kc = to_chunks(key, HGRN_EXPAND)
    gc = to_chunks(log_f, HGRN_EXPAND)
    vc = to_chunks(i_val.astype(jnp.float32), HGRN_HEAD_V)
    tri = jnp.tril(jnp.ones((C, C), dtype=bool))

    def step(state, inp):
        qq, kk, vv, gg = inp
        A = jnp.cumsum(gg, axis=2)
        o_inter = jnp.einsum('bhtd,bhdv->bhtv', qq * jnp.exp(A), state)
        diff = A[:, :, :, None, :] - A[:, :, None, :, :]
        decay = jnp.exp(jnp.where(tri[None, None, :, :, None], diff, -jnp.inf))
        scores = jnp.einsum('bhtd,bhsd,bhtsd->bhts', qq, kk, decay)
        o_intra = jnp.einsum('bhts,bhsv->bhtv', scores, vv)
        k_dec = kk * jnp.exp(A[:, :, -1:, :] - A)
        new_state = jnp.exp(A[:, :, -1, :])[..., None] * state + jnp.einsum('bhsd,bhsv->bhdv', k_dec, vv)
        return new_state, o_inter + o_intra

    s0 = jnp.zeros((B, HGRN_HEADS, HGRN_EXPAND, HGRN_HEAD_V), jnp.float32)
    _, o = lax.scan(step, s0, (qc, kc, vc, gc))
    o = jnp.transpose(o, (1, 0, 3, 2, 4)).reshape(B, S, HGRN_HEADS, HGRN_HEAD_V)
    o = o * lax.rsqrt(jnp.mean(jnp.square(o), axis=-1, keepdims=True) + RMS_EPS)
    o = o.reshape(B, S, HGRN_VW).astype(q.dtype)
    return o * norm_g * jax.nn.silu(g_out)

def token_mixer(h, w_in, pool_w, pool_scale, rel_bias, lb, norm_g, w_branch, w_out):
    B, S, _ = h.shape
    proj = h @ w_in
    (a, q, k, v, qi, ki, wi, hq, hf, hi, hg, gates) = jnp.split(proj, MIX_SPLITS, axis=-1)
    y_a = pool_mixer(a, pool_w, pool_scale)
    y_b = sparse_attention(q.reshape(B, S, ATTN_HEADS, ATTN_HEAD_DIM),
                           k.reshape(B, S, ATTN_HEADS, ATTN_HEAD_DIM),
                           v.reshape(B, S, ATTN_HEADS, ATTN_HEAD_DIM),
                           qi.reshape(B, S, IDX_HEADS, IDX_DIM), ki, wi, rel_bias)
    y_c = hgrn2(hq, hf, hi, hg, lb, norm_g)
    g = jax.nn.sigmoid(gates.reshape(B, S, 3, D_MODEL))
    merged = (g[:, :, 0] * (y_a @ w_branch[:POOL_WIDTH])
              + g[:, :, 1] * (y_b @ w_branch[POOL_WIDTH:POOL_WIDTH + ATTN_WIDTH])
              + g[:, :, 2] * (y_c @ w_branch[POOL_WIDTH + ATTN_WIDTH:]))
    return merged @ w_out

def first_inputs(seed: int = 0) -> dict:
    key = jax.random.key(seed)
    ks = jax.random.split(key, 16)
    f32 = jnp.float32

    def n(k, shape):
        return jax.random.normal(k, shape, f32)

    x = n(ks[0], (BATCH, SEQ, D_MODEL))
    c = n(ks[1], (BATCH, D_MODEL))
    w_ada = n(ks[2], (DEPTH, D_MODEL, N_SUB * 3 * D_MODEL)) * (0.3 * D_MODEL ** -0.5)
    b_ada = 0.01 * n(ks[3], (DEPTH, N_SUB * 3 * D_MODEL))
    ln_g = 1.0 + 0.02 * n(ks[4], (DEPTH, N_SUB, D_MODEL))
    ln_b = 0.02 * n(ks[5], (DEPTH, N_SUB, D_MODEL))
    ffn_w_in = n(ks[6], (DEPTH, 2, D_MODEL, 2 * D_FF)) * D_MODEL ** -0.5
    ffn_w_out = n(ks[7], (DEPTH, 2, D_FF, D_MODEL)) * (DN_BETA * D_FF ** -0.5)
    mix_w_in = n(ks[8], (DEPTH, D_MODEL, MIX_IN_WIDTH)) * D_MODEL ** -0.5
    pool_w = n(ks[9], (DEPTH, len(POOL_WINDOWS), POOL_GROUP, POOL_GROUP)) * POOL_GROUP ** -0.5
    pool_scale = 1.0 + 0.02 * n(ks[10], (DEPTH, POOL_WIDTH))
    rel_bias = 0.5 * n(ks[11], (REL_BUCKETS, ATTN_HEADS))
    hgrn_lb = 1.0 + 0.1 * n(ks[12], (DEPTH, HGRN_KW))
    hgrn_norm_g = 1.0 + 0.02 * n(ks[13], (DEPTH, HGRN_VW))
    row_scale = jnp.concatenate([jnp.full((POOL_WIDTH,), POOL_WIDTH ** -0.5, f32),
                                 jnp.full((ATTN_WIDTH,), ATTN_WIDTH ** -0.5, f32),
                                 jnp.full((HGRN_VW,), HGRN_VW ** -0.5, f32)])
    w_branch = n(ks[14], (DEPTH, MIX_WIDTH, D_MODEL)) * row_scale[None, :, None]
    w_out = n(ks[15], (DEPTH, D_MODEL, D_MODEL)) * (DN_BETA * D_MODEL ** -0.5)
    return {'x': x, 'c': c, 'w_ada': w_ada, 'b_ada': b_ada, 'ln_g': ln_g, 'ln_b': ln_b,
            'ffn_w_in': ffn_w_in, 'ffn_w_out': ffn_w_out, 'mix_w_in': mix_w_in,
            'pool_w': pool_w, 'pool_scale': pool_scale, 'rel_bias': rel_bias,
            'hgrn_lb': hgrn_lb, 'hgrn_norm_g': hgrn_norm_g, 'w_branch': w_branch, 'w_out': w_out}

def first_block(x, c, w_ada, b_ada, ln_g, ln_b, ffn_w_in, ffn_w_out, mix_w_in, pool_w, pool_scale,
              rel_bias, hgrn_lb, hgrn_norm_g, w_branch, w_out):
    B = x.shape[0]
    lb_sm = jax.nn.softmax(hgrn_lb.astype(jnp.float32), axis=0)
    lbs = jnp.cumsum(lb_sm, axis=0) - lb_sm[0:1]
    cond = jax.nn.silu(c)
    for l in range(DEPTH):
        mod = (cond @ w_ada[l] + b_ada[l]).reshape(B, N_SUB, 3, D_MODEL)
        y = swiglu(modulate(x, mod, 0), ffn_w_in[l, 0], ffn_w_out[l, 0])
        x = layer_norm(DN_ALPHA * x + 0.5 * sub_gate(mod, 0) * y, ln_g[l, 0], ln_b[l, 0])
        y = token_mixer(modulate(x, mod, 1), mix_w_in[l], pool_w[l], pool_scale[l], rel_bias,
                        lbs[l], hgrn_norm_g[l], w_branch[l], w_out[l])
        x = layer_norm(DN_ALPHA * x + sub_gate(mod, 1) * y, ln_g[l, 1], ln_b[l, 1])
        y = swiglu(modulate(x, mod, 2), ffn_w_in[l, 1], ffn_w_out[l, 1])
        x = layer_norm(DN_ALPHA * x + 0.5 * sub_gate(mod, 2) * y, ln_g[l, 2], ln_b[l, 2])
    return x


GRID_W = 64
CTX_LEN = 256
N_EVEN = (DEPTH + 1) // 2
N_ODD = DEPTH // 2
EPS = 1e-6

GLA_HEADS = 4
GLA_DK = D_MODEL // 16
GLA_DV = D_MODEL // 8
GLA_RANK = 16
GLA_TAU = 16.0
GLA_CHUNK = 64

ML_HEADS = 4
ML_D = D_MODEL // 8
ML_CONV = 3
ML_CHUNK = 64

D_INNER = 2 * D_MODEL
SSD_HEADDIM = 64
SSD_HEADS = D_INNER // SSD_HEADDIM
SSD_GROUPS = 4
SSD_HPG = SSD_HEADS // SSD_GROUPS
SSD_STATE = 128
SSD_CONV = 3
SSD_CHUNK = 128

FFN_CONV = 3

GLA_QK = GLA_HEADS * GLA_DK
GLA_V = GLA_HEADS * GLA_DV
ML_W = ML_HEADS * ML_D
EVEN_SIZES = (GLA_QK, GLA_QK, GLA_V, GLA_V, ML_W, ML_W, ML_W, ML_W, 4 * ML_HEADS)
EVEN_IN = sum(EVEN_SIZES)
SSD_BC = SSD_GROUPS * SSD_STATE
SSD_CONV_CH = D_INNER + 2 * SSD_BC
ODD_SIZES = (D_INNER, SSD_CONV_CH, 2 * SSD_HEADS)
ODD_IN = sum(ODD_SIZES)


def _split(a, sizes):
    return jnp.split(a, [int(s) for s in np.cumsum(sizes)[:-1]], axis=-1)

def rmsnorm(x, g):
    xf = x.astype(jnp.float32)
    y = xf * lax.rsqrt(jnp.mean(xf * xf, axis=-1, keepdims=True) + EPS)
    return (y * g.astype(jnp.float32)).astype(x.dtype)

def modulate_2(x, g, shift, scale):
    return rmsnorm(x, g) * (1 + scale) + shift

def dwconv1d(x, w, b):
    k_w = w.shape[0]
    t = x.shape[1]
    pad = k_w // 2
    xp = jnp.pad(x, ((0, 0), (pad, pad), (0, 0)))
    return sum(xp[:, j:j + t] * w[j] for j in range(k_w)) + b

def dwconv2d_grid(x, w, b, rows):
    bsz, t, ch = x.shape
    y = lax.conv_general_dilated(x.reshape(bsz, rows, GRID_W, ch), w[:, :, None, :], (1, 1), 'SAME',
                                 dimension_numbers=('NHWC', 'HWIO', 'NHWC'), feature_group_count=ch)
    return y.reshape(bsz, t, ch) + b

def to_chunks(a, size):
    bsz, t = a.shape[:2]
    return jnp.moveaxis(a.reshape(bsz, t // size, size, *a.shape[2:]), 1, 0)

def from_chunks(a):
    a = jnp.moveaxis(a, 0, 1)
    return a.reshape(a.shape[0], a.shape[1] * a.shape[2], *a.shape[3:])

def gla_scan(q, k, v, log_a, s0, with_out):
    size = GLA_CHUNK
    tri = jnp.tril(jnp.ones((size, size), dtype=bool))[None, :, :, None, None]

    def step(s, inp):
        qc, kc, vc, lac = inp
        cum = jnp.cumsum(lac.astype(jnp.float32), axis=1)
        c_end = cum[:, -1]
        k_end = kc * jnp.exp(c_end[:, None] - cum)
        s_new = jnp.exp(c_end)[..., None] * s + jnp.einsum('bshk,bshv->bhkv', k_end, vc)
        if not with_out:
            return s_new, None
        rel = jnp.where(tri, cum[:, :, None] - cum[:, None, :], -jnp.inf)
        att = jnp.einsum('bthk,bshk,btshk->bhts', qc, kc, jnp.exp(rel))
        o = jnp.einsum('bhts,bshv->bthv', att, vc) + jnp.einsum('bthk,bhkv->bthv', qc * jnp.exp(cum), s)
        return s_new, o

    s, o = lax.scan(step, s0, tuple(to_chunks(a, size) for a in (q, k, v, log_a)))
    return (from_chunks(o) if with_out else None), s

def mlstm_scan(q, k, v, li, lf, state0, with_out):
    size = ML_CHUNK
    tri = jnp.tril(jnp.ones((size, size), dtype=bool))[None, :, :, None]

    def step(carry, inp):
        cmat, nvec, m = carry
        qc, kc, vc, lic, lfc = inp
        b = jnp.cumsum(lfc, axis=1)
        b_end = b[:, -1]
        w_end = b_end[:, None] - b + lic
        m_new = jnp.maximum(b_end + m, jnp.max(w_end, axis=1))
        decay = jnp.exp(b_end + m - m_new)
        ws = jnp.exp(w_end - m_new[:, None])
        c_new = decay[..., None, None] * cmat + jnp.einsum('bsh,bshk,bshv->bhkv', ws, kc, vc)
        n_new = decay[..., None] * nvec + jnp.einsum('bsh,bshk->bhk', ws, kc)
        if not with_out:
            return (c_new, n_new, m_new), None
        a_in = b + m[:, None]
        d_log = jnp.where(tri, b[:, :, None] - b[:, None, :] + lic[:, None, :], -jnp.inf)
        m_t = jnp.maximum(a_in, jnp.max(d_log, axis=2))
        dw = jnp.exp(d_log - m_t[:, :, None])
        aw = jnp.exp(a_in - m_t)
        sc = jnp.einsum('bthk,bshk->btsh', qc, kc) * dw
        num = aw[..., None] * jnp.einsum('bthk,bhkv->bthv', qc, cmat) + jnp.einsum('btsh,bshv->bthv', sc, vc)
        den = aw * jnp.einsum('bthk,bhk->bth', qc, nvec) + jnp.sum(sc, axis=2)
        h = num / jnp.maximum(jnp.abs(den), jnp.exp(-m_t))[..., None]
        return (c_new, n_new, m_new), h

    state, h = lax.scan(step, state0, tuple(to_chunks(a, size) for a in (q, k, v, li, lf)))
    return (from_chunks(h) if with_out else None), state

def ssd_scan(x, dt, bm, cm, s0, with_out, A):
    size = SSD_CHUNK
    tri = jnp.tril(jnp.ones((size, size), dtype=bool))[None, :, :, None, None]

    def step(s, inp):
        xc, dtc, bc, cc = inp
        cum = jnp.cumsum(dtc * A, axis=1)
        c_end = cum[:, -1]
        w_end = jnp.exp(c_end[:, None] - cum) * dtc
        s_new = jnp.exp(c_end)[..., None, None] * s + jnp.einsum('bsgh,bsgn,bsghp->bghpn', w_end, bc, xc)
        if not with_out:
            return s_new, None
        seg = jnp.where(tri, cum[:, :, None] - cum[:, None, :], -jnp.inf)
        cb = jnp.einsum('btgn,bsgn->btsg', cc, bc)
        w = jnp.exp(seg) * cb[..., None] * dtc[:, None]
        y = (jnp.einsum('btsgh,bsghp->btghp', w, xc)
             + jnp.exp(cum)[..., None] * jnp.einsum('btgn,bghpn->btghp', cc, s))
        return s_new, y

    s, y = lax.scan(step, s0, tuple(to_chunks(a, size) for a in (x, dt, bm, cm)))
    return (from_chunks(y) if with_out else None), s

def bidir_scan(scan_f, scan_b, ctx_f, lat_f, ctx_b, lat_b, init, ctx_out):
    def one_dir(scan_fn, ctx_args, lat_args):
        yc, s_ctx = scan_fn(*ctx_args, init, ctx_out)
        yl, _ = scan_fn(*lat_args, s_ctx, True)
        return yc, yl

    def rev(a):
        return jnp.flip(a, axis=1)

    yc_f, yl_f = one_dir(scan_f, ctx_f, lat_f)
    yc_b, yl_b = one_dir(scan_b, [rev(a) for a in ctx_b], [rev(a) for a in lat_b])
    yl = yl_f + rev(yl_b)
    yc = (yc_f + rev(yc_b)) if ctx_out else None
    return yc, yl

def even_features(h, w_in, a1, a2, ab, conv_w, conv_b, gate_b):
    bsz, t, _ = h.shape
    gq, gk, gv, gg, mq, mk, mv, mo, mg = _split(h @ w_in, EVEN_SIZES)
    log_a = [(jax.nn.log_sigmoid(((h @ a1[d]) @ a2[d] + ab[d]).astype(jnp.float32)) / GLA_TAU)
             .reshape(bsz, t, GLA_HEADS, GLA_DK) for d in range(2)]
    qk = jax.nn.silu(dwconv1d(jnp.concatenate([mq, mk], axis=-1), conv_w, conv_b))
    mq, mk = jnp.split(qk, 2, axis=-1)
    gates = (mg + gate_b).astype(jnp.float32).reshape(bsz, t, 4, ML_HEADS)
    return {
        'gla_q': gq.reshape(bsz, t, GLA_HEADS, GLA_DK) * GLA_DK ** -0.5,
        'gla_k': gk.reshape(bsz, t, GLA_HEADS, GLA_DK),
        'gla_v': gv.reshape(bsz, t, GLA_HEADS, GLA_DV),
        'gla_g': gg,
        'la_f': log_a[0], 'la_b': log_a[1],
        'ml_q': mq.reshape(bsz, t, ML_HEADS, ML_D),
        'ml_k': mk.reshape(bsz, t, ML_HEADS, ML_D) * ML_D ** -0.5,
        'ml_v': mv.reshape(bsz, t, ML_HEADS, ML_D),
        'ml_o': mo,
        'li_f': gates[:, :, 0], 'lf_f': jax.nn.log_sigmoid(gates[:, :, 1]),
        'li_b': gates[:, :, 2], 'lf_b': jax.nn.log_sigmoid(gates[:, :, 3]),
    }

def even_combine(f, o_gla, h_ml, gla_norm_g, ml_norm_g, w_out):
    bsz, t = o_gla.shape[:2]
    gla = rmsnorm(o_gla, gla_norm_g.reshape(GLA_HEADS, GLA_DV)).reshape(bsz, t, GLA_V) * jax.nn.silu(f['gla_g'])
    ml = jax.nn.sigmoid(f['ml_o']).reshape(bsz, t, ML_HEADS, ML_D) * h_ml
    ml = rmsnorm(ml, ml_norm_g.reshape(ML_HEADS, ML_D)).reshape(bsz, t, ML_W)
    return jnp.concatenate([gla, ml], axis=-1).astype(w_out.dtype) @ w_out

def even_mixer(hc, hl, w_in, a1, a2, ab, conv_w, conv_b, gate_b, gla_norm_g, ml_norm_g, w_out, ctx_out):
    fc = even_features(hc, w_in, a1, a2, ab, conv_w, conv_b, gate_b)
    fl = even_features(hl, w_in, a1, a2, ab, conv_w, conv_b, gate_b)
    bsz = hl.shape[0]

    def g_args(f, d):
        return (f['gla_q'], f['gla_k'], f['gla_v'], f['la_' + d])

    gla_init = jnp.zeros((bsz, GLA_HEADS, GLA_DK, GLA_DV), jnp.float32)
    oc_gla, ol_gla = bidir_scan(gla_scan, gla_scan, g_args(fc, 'f'), g_args(fl, 'f'),
                                g_args(fc, 'b'), g_args(fl, 'b'), gla_init, ctx_out)

    def m_args(f, d):
        return (f['ml_q'], f['ml_k'], f['ml_v'], f['li_' + d], f['lf_' + d])

    ml_init = (jnp.zeros((bsz, ML_HEADS, ML_D, ML_D), jnp.float32),
               jnp.zeros((bsz, ML_HEADS, ML_D), jnp.float32),
               jnp.zeros((bsz, ML_HEADS), jnp.float32))
    hc_ml, hl_ml = bidir_scan(mlstm_scan, mlstm_scan, m_args(fc, 'f'), m_args(fl, 'f'),
                              m_args(fc, 'b'), m_args(fl, 'b'), ml_init, ctx_out)
    yl = even_combine(fl, ol_gla, hl_ml, gla_norm_g, ml_norm_g, w_out)
    yc = even_combine(fc, oc_gla, hc_ml, gla_norm_g, ml_norm_g, w_out) if ctx_out else None
    return yc, yl

def odd_features(h, w_in, conv_w, conv_b, dt_bias):
    bsz, t, _ = h.shape
    z, xbc, dt = _split(h @ w_in, ODD_SIZES)
    xs, bm, cm = _split(jax.nn.silu(dwconv1d(xbc, conv_w, conv_b)), (D_INNER, SSD_BC, SSD_BC))
    dt = jax.nn.softplus(dt.astype(jnp.float32).reshape(bsz, t, 2, SSD_HEADS) + dt_bias.astype(jnp.float32))
    dt = dt.reshape(bsz, t, 2, SSD_GROUPS, SSD_HPG)
    return {
        'z': z,
        'x': xs.reshape(bsz, t, SSD_GROUPS, SSD_HPG, SSD_HEADDIM),
        'b': bm.reshape(bsz, t, SSD_GROUPS, SSD_STATE),
        'c': cm.reshape(bsz, t, SSD_GROUPS, SSD_STATE),
        'dt_f': dt[:, :, 0], 'dt_b': dt[:, :, 1],
    }

def odd_mixer(hc, hl, w_in, conv_w, conv_b, dt_bias, a_log, d_skip, norm_g, w_out, ctx_out):
    fc = odd_features(hc, w_in, conv_w, conv_b, dt_bias)
    fl = odd_features(hl, w_in, conv_w, conv_b, dt_bias)
    bsz = hl.shape[0]
    A = -jnp.exp(a_log.astype(jnp.float32)).reshape(2, SSD_GROUPS, SSD_HPG)
    scan_f = functools.partial(ssd_scan, A=A[0])
    scan_b = functools.partial(ssd_scan, A=A[1])

    def s_args(f, d):
        return (f['x'], f['dt_' + d], f['b'], f['c'])

    init = jnp.zeros((bsz, SSD_GROUPS, SSD_HPG, SSD_HEADDIM, SSD_STATE), jnp.float32)
    yc, yl = bidir_scan(scan_f, scan_b, s_args(fc, 'f'), s_args(fl, 'f'),
                        s_args(fc, 'b'), s_args(fl, 'b'), init, ctx_out)

    def combine(f, y):
        b_, t_ = y.shape[:2]
        y = (y + d_skip.reshape(SSD_GROUPS, SSD_HPG)[..., None] * f['x']).reshape(b_, t_, D_INNER)
        y = (y * jax.nn.silu(f['z'])).reshape(b_, t_, SSD_GROUPS, D_INNER // SSD_GROUPS)
        y = rmsnorm(y, norm_g.reshape(SSD_GROUPS, D_INNER // SSD_GROUPS)).reshape(b_, t_, D_INNER)
        return y.astype(w_out.dtype) @ w_out

    return (combine(fc, yc) if ctx_out else None), combine(fl, yl)

def conv_ffn(h, w_up, conv_w, conv_b, w_down, rows):
    u = h @ w_up
    if rows is None:
        u = dwconv1d(u, conv_w[1], conv_b)
    else:
        u = dwconv2d_grid(u, conv_w, conv_b, rows)
    a, g = jnp.split(u, 2, axis=-1)
    return (jax.nn.silu(g) * a) @ w_down

def second_inputs(seed: int = 0) -> dict:
    key = jax.random.key(seed)
    ks = list(jax.random.split(key, 40))
    f32 = jnp.float32

    def nrm(shape, scale):
        return scale * jax.random.normal(ks.pop(), shape, f32)

    def gain(shape):
        return 1.0 + 0.05 * jax.random.normal(ks.pop(), shape, f32)

    gate_base = jnp.concatenate([jnp.zeros((ML_HEADS,), f32), jnp.linspace(3.0, 6.0, ML_HEADS, dtype=f32)] * 2)
    dt0 = jnp.exp(jax.random.uniform(ks.pop(), (N_ODD, 2, SSD_HEADS), f32, math.log(1e-3), math.log(1e-1)))
    return {
        'x': nrm((BATCH, SEQ, D_MODEL), 1.0),
        'c': nrm((BATCH, D_MODEL), 1.0),
        'ctx': nrm((BATCH, CTX_LEN, D_MODEL), 1.0),
        'c_ctx': nrm((D_MODEL,), 1.0),
        'mod_w': nrm((DEPTH, D_MODEL, 6 * D_MODEL), 0.5 * D_MODEL ** -0.5),
        'mod_b': nrm((DEPTH, 6 * D_MODEL), 0.02),
        'norm_mix_g': gain((DEPTH, D_MODEL)),
        'norm_ffn_g': gain((DEPTH, D_MODEL)),
        'final_norm_g': gain((D_MODEL,)),
        'ffn_w_up': nrm((DEPTH, D_MODEL, 2 * D_FF), D_MODEL ** -0.5),
        'ffn_conv_w': nrm((DEPTH, FFN_CONV, FFN_CONV, 2 * D_FF), 1.0 / FFN_CONV),
        'ffn_conv_b': nrm((DEPTH, 2 * D_FF), 0.02),
        'ffn_w_down': nrm((DEPTH, D_FF, D_MODEL), D_FF ** -0.5),
        'even_w_in': nrm((N_EVEN, D_MODEL, EVEN_IN), D_MODEL ** -0.5),
        'gla_a1': nrm((N_EVEN, 2, D_MODEL, GLA_RANK), D_MODEL ** -0.5),
        'gla_a2': nrm((N_EVEN, 2, GLA_RANK, GLA_QK), GLA_RANK ** -0.5),
        'gla_ab': nrm((N_EVEN, 2, GLA_QK), 0.1),
        'ml_conv_w': nrm((N_EVEN, ML_CONV, 2 * ML_W), ML_CONV ** -0.5),
        'ml_conv_b': nrm((N_EVEN, 2 * ML_W), 0.02),
        'ml_gate_b': gate_base[None] + nrm((N_EVEN, 4 * ML_HEADS), 0.1),
        'gla_norm_g': gain((N_EVEN, GLA_V)),
        'ml_norm_g': gain((N_EVEN, ML_W)),
        'even_w_out': nrm((N_EVEN, GLA_V + ML_W, D_MODEL), (GLA_V + ML_W) ** -0.5),
        'ssd_w_in': nrm((N_ODD, D_MODEL, ODD_IN), D_MODEL ** -0.5),
        'ssd_conv_w': nrm((N_ODD, SSD_CONV, SSD_CONV_CH), SSD_CONV ** -0.5),
        'ssd_conv_b': nrm((N_ODD, SSD_CONV_CH), 0.02),
        'ssd_dt_bias': dt0 + jnp.log(-jnp.expm1(-dt0)),
        'ssd_a_log': jnp.log(jax.random.uniform(ks.pop(), (N_ODD, 2, SSD_HEADS), f32, 1.0, 16.0)),
        'ssd_d': gain((N_ODD, SSD_HEADS)),
        'ssd_norm_g': gain((N_ODD, D_INNER)),
        'ssd_w_out': nrm((N_ODD, D_INNER, D_MODEL), D_INNER ** -0.5),
    }

def second_block(x, c, ctx, c_ctx, mod_w, mod_b, norm_mix_g, norm_ffn_g, final_norm_g,
              ffn_w_up, ffn_conv_w, ffn_conv_b, ffn_w_down,
              even_w_in, gla_a1, gla_a2, gla_ab, ml_conv_w, ml_conv_b, ml_gate_b,
              gla_norm_g, ml_norm_g, even_w_out,
              ssd_w_in, ssd_conv_w, ssd_conv_b, ssd_dt_bias, ssd_a_log, ssd_d, ssd_norm_g, ssd_w_out):
    rows = x.shape[1] // GRID_W
    xl, xc = x, ctx
    for layer in range(DEPTH):
        last = layer == DEPTH - 1
        mod_l = (jax.nn.silu(c) @ mod_w[layer] + mod_b[layer])[:, None, :]
        mod_c = (jax.nn.silu(c_ctx) @ mod_w[layer] + mod_b[layer])[None, None, :]
        sh1l, sc1l, g1l, sh2l, sc2l, g2l = jnp.split(mod_l, 6, axis=-1)
        sh1c, sc1c, g1c, sh2c, sc2c, g2c = jnp.split(mod_c, 6, axis=-1)
        hl = modulate_2(xl, norm_mix_g[layer], sh1l, sc1l)
        hc = modulate_2(xc, norm_mix_g[layer], sh1c, sc1c)
        if layer % 2 == 0:
            e = layer // 2
            yc, yl = even_mixer(hc, hl, even_w_in[e], gla_a1[e], gla_a2[e], gla_ab[e], ml_conv_w[e], ml_conv_b[e],
                                ml_gate_b[e], gla_norm_g[e], ml_norm_g[e], even_w_out[e], not last)
        else:
            o = layer // 2
            yc, yl = odd_mixer(hc, hl, ssd_w_in[o], ssd_conv_w[o], ssd_conv_b[o], ssd_dt_bias[o], ssd_a_log[o],
                               ssd_d[o], ssd_norm_g[o], ssd_w_out[o], not last)
        xl = xl + g1l * yl
        hl = modulate_2(xl, norm_ffn_g[layer], sh2l, sc2l)
        xl = xl + g2l * conv_ffn(hl, ffn_w_up[layer], ffn_conv_w[layer], ffn_conv_b[layer], ffn_w_down[layer], rows)
        if not last:
            xc = xc + g1c * yc
            hc = modulate_2(xc, norm_ffn_g[layer], sh2c, sc2c)
            xc = xc + g2c * conv_ffn(hc, ffn_w_up[layer], ffn_conv_w[layer], ffn_conv_b[layer], ffn_w_down[layer], None)
    return rmsnorm(xl, final_norm_g)


def setup_inputs(seed=0):
    out = dict(first_inputs(seed))
    for name, value in second_inputs(seed + 1).items():
        if name != "x":
            out[name + "_2"] = value
    return out


def reference(
    x, c, w_ada, b_ada, ln_g, ln_b, ffn_w_in, ffn_w_out, mix_w_in, pool_w, pool_scale, rel_bias,
    hgrn_lb, hgrn_norm_g, w_branch, w_out, c_2, ctx_2, c_ctx_2, mod_w_2, mod_b_2, norm_mix_g_2,
    norm_ffn_g_2, final_norm_g_2, ffn_w_up_2, ffn_conv_w_2, ffn_conv_b_2, ffn_w_down_2,
    even_w_in_2, gla_a1_2, gla_a2_2, gla_ab_2, ml_conv_w_2, ml_conv_b_2, ml_gate_b_2,
    gla_norm_g_2, ml_norm_g_2, even_w_out_2, ssd_w_in_2, ssd_conv_w_2, ssd_conv_b_2,
    ssd_dt_bias_2, ssd_a_log_2, ssd_d_2, ssd_norm_g_2, ssd_w_out_2,
):
    x = first_block(
        x, c, w_ada, b_ada, ln_g, ln_b, ffn_w_in, ffn_w_out, mix_w_in, pool_w, pool_scale,
        rel_bias, hgrn_lb, hgrn_norm_g, w_branch, w_out,
    )
    return second_block(
        x, c_2, ctx_2, c_ctx_2, mod_w_2, mod_b_2, norm_mix_g_2, norm_ffn_g_2, final_norm_g_2,
        ffn_w_up_2, ffn_conv_w_2, ffn_conv_b_2, ffn_w_down_2, even_w_in_2, gla_a1_2, gla_a2_2,
        gla_ab_2, ml_conv_w_2, ml_conv_b_2, ml_gate_b_2, gla_norm_g_2, ml_norm_g_2,
        even_w_out_2, ssd_w_in_2, ssd_conv_w_2, ssd_conv_b_2, ssd_dt_bias_2, ssd_a_log_2,
        ssd_d_2, ssd_norm_g_2, ssd_w_out_2,
    )


_drawn_inputs = setup_inputs


def setup_inputs(seed=0):
    import zlib

    import numpy as np

    out = dict(_drawn_inputs(seed))
    spreads = {}
    factors = {'b_ada': 4.404,
     'pool_scale': 8.0,
     'hgrn_lb': 8.0,
     'hgrn_norm_g': 8.0,
     'norm_ffn_g_2': 3.151,
     'ffn_conv_b_2': 7.749,
     'gla_ab_2': 8.0,
     'ml_conv_b_2': 8.0,
     'gla_norm_g_2': 7.296,
     'ml_norm_g_2': 4.635,
     'ssd_conv_b_2': 7.152,
     'ssd_d_2': 8.0,
     'ssd_norm_g_2': 3.626}
    for name, (base, spread) in spreads.items():
        noise = np.random.default_rng([zlib.crc32(name.encode()), seed]).standard_normal(out[name].shape)
        drawn = base * np.exp(spread * noise) if base else spread * noise
        out[name] = jnp.asarray(drawn.astype(out[name].dtype))
    for name, factor in factors.items():
        out[name] = (out[name] * factor).astype(out[name].dtype)
    return out
```

```python
from contextlib import ExitStack

import concourse.bass as bass
from concourse import mybir
import numpy as np

F32 = mybir.dt.float32
ALU = mybir.AluOpType
ACT = mybir.ActivationFunctionType
AXX = mybir.AxisListType.X

P = 128
T = 256
D = 1024
KD = D // P
DEPTH = 2
D_FF = 2816
KF = D_FF // P
PANEL = 256
KSPLIT = KF // 2
SLOTS = BANKS = 4
SLOT_W = KSPLIT * PANEL
ALPHA = (2 * DEPTH) ** 0.25
LN_EPS, RMS_EPS = 1e-5, 1e-6
KEY_MAX = 1.0 - 1e-6
TOPK = 64
IDX_SCALE = (64 ** -0.5) * (8 ** -0.5)
NEG = -3.0e38
GONE = -3.3e38
MASKED = -1.0e30
POOL_WINDOWS = (2, 4, 8, 16)
PAD = 16
NLEV = 7
GRID_ROWS, GRID_W = 4, 64
LATPAD = (GRID_ROWS + 2) * (GRID_W + 2)
CTXPAD = T + 2

COL_SPEC = [("c", 8), ("b_ada", 2 * 72), ("ln_g", 48), ("ln_b", 48), ("pool_scale", 4), ("hgrn_lb", 8),
            ("hgrn_norm_g", 8), ("c_2", 8), ("c_ctx_2", 8), ("mod_b_2", 96), ("norm_mix_g_2", 16),
            ("norm_ffn_g_2", 16), ("final_norm_g_2", 8), ("ffn_conv_w_2", 2 * 9 * 44), ("ffn_conv_b_2", 88),
            ("gla_ab_2", 4), ("ml_conv_w_2", 24), ("ml_conv_b_2", 8), ("ml_gate_b_2", 1), ("gla_norm_g_2", 4),
            ("ml_norm_g_2", 4), ("ssd_conv_w_2", 72), ("ssd_conv_b_2", 24), ("ssd_dt_bias_2", 1),
            ("ssd_a_log_2", 1), ("ssd_d_2", 16), ("ssd_norm_g_2", 16)]
COL = {}
NCOL = 0
for _name, _n in COL_SPEC:
    COL[_name] = NCOL
    NCOL += _n

CONST_SPEC = [("ident", 128), ("flip", 128), ("tree_f", NLEV * 128), ("tree_b", NLEV * 128), ("causal", 256),
              ("mneg", 4 * 256), ("tri", 256), ("invcnt", 512), ("onehot", 384), ("eps", 4)]
CST = {}
NCST = 0
for _name, _n in CONST_SPEC:
    CST[_name] = NCST
    NCST += _n


class InOrder:

    def __init__(self, eng):
        self.eng = eng
        self.wait_ge, self.drain, self.Fori = eng.wait_ge, eng.drain, eng.Fori

    def activation(self, *a, **k):
        i = self.eng.activation(*a, **k)
        self.eng.drain()
        return i

    def tensor_scalar(self, *a, **k):
        i = self.eng.tensor_scalar(*a, **k)
        self.eng.drain()
        return i

    def tensor_tensor(self, *a, **k):
        i = self.eng.tensor_tensor(*a, **k)
        self.eng.drain()
        return i

    def scalar_tensor_tensor(self, *a, **k):
        i = self.eng.scalar_tensor_tensor(*a, **k)
        self.eng.drain()
        return i

    def tensor_copy(self, *a, **k):
        i = self.eng.tensor_copy(*a, **k)
        self.eng.drain()
        return i

    def tensor_reduce(self, *a, **k):
        i = self.eng.tensor_reduce(*a, **k)
        self.eng.drain()
        return i

    def tensor_tensor_scan(self, *a, **k):
        i = self.eng.tensor_tensor_scan(*a, **k)
        self.eng.drain()
        return i

    def reciprocal(self, *a, **k):
        i = self.eng.reciprocal(*a, **k)
        self.eng.drain()
        return i

    def memset(self, *a, **k):
        i = self.eng.memset(*a, **k)
        self.eng.drain()
        return i

    def max(self, *a, **k):
        i = self.eng.max(*a, **k)
        self.eng.drain()
        return i

    def match_replace(self, *a, **k):
        i = self.eng.match_replace(*a, **k)
        self.eng.drain()
        return i


class Gemm:

    def __init__(self, name, panels, accs_per_panel=1, wide=False, panels_per_acc=1):
        self.name, self.n, self.apa, self.wide, self.ppa = name, panels, accs_per_panel, wide, panels_per_acc


def plan():
    order = []
    for l in range(DEPTH):
        order += [Gemm(f"in{l}0", 22), Gemm(f"out{l}0", 8, wide=True, panels_per_acc=2),
                  Gemm(f"mix{l}", 15), Gemm(f"gate{l}", 12), Gemm(f"branch{l}", 4, 3), Gemm(f"mixout{l}", 4),
                  Gemm(f"in{l}1", 22), Gemm(f"out{l}1", 8, wide=True, panels_per_acc=2)]
    for l in range(DEPTH):
        both = 2 if l == 0 else 1
        if l == 0:
            order += [Gemm("even", 14, 2), Gemm("evengate", 1), Gemm("evenout", 4, 2)]
        else:
            order += [Gemm("dt", 1)]
            for g in range(4):
                order += [Gemm(f"ssdx{g}", 2, 2), Gemm(f"ssdbc{g}", 1, 2), Gemm(f"ssdz{g}", 2)]
            order += [Gemm("ssdout", 8, panels_per_acc=2)]
        order += [Gemm(f"up{l}", 22, both), Gemm(f"down{l}", 8, both, wide=True, panels_per_acc=2)]
    p = a = 0
    row = {False: 0, True: 0}
    finished = []
    halves = 0
    for g in order:
        g.p0, g.a0, g.row0 = p, a, row[g.wide]
        row[g.wide] += g.n
        for i in range(g.n):
            if g.ppa == 2 and i % 2 == 0:
                halves += 1
                finished.append(("half", 0, halves))
            else:
                last = a + g.apa * (i // g.ppa + 1) - 1
                finished.append(("ready", last % BANKS, last // BANKS + 1))
        p += g.n
        a += g.n // g.ppa * g.apa
    return {g.name: g for g in order}, order, finished, row


ADA, MOD = 36, 24
MOD0 = DEPTH * ADA
UNITS = DEPTH * (ADA + MOD)
HEAD = 8
CARRY = {"head": (0, HEAD), "in00": (HEAD, 22), "out00": (30, 6), "mix0": (36, 14), "in01": (50, 22),
         "in10": (72, 22), "mix1": (94, 4), "in11": (98, 22)}


def program(nc, io):
    G, order, finished, _ = plan()
    w8, w11, wc = io["w8"], io["w11"], io["wc"]
    with ExitStack() as ctx:
        def sb(name, shape):
            return ctx.enter_context(nc.sbuf_tensor(name, shape, F32))

        def sem(name):
            return ctx.enter_context(nc.semaphore(name))

        slots = [sb(f"panel{i}", [P, SLOT_W]) for i in range(SLOTS)]
        X = sb("residual", [P, KD, 2 * T])
        H = sb("normed", [P, KD, 2 * T])
        cst = sb("constants", [P, NCST])
        cols = sb("vectors", [P, NCOL])
        mods1 = sb("mods1", [P, DEPTH, 72])
        mods2 = sb("mods2", [P, DEPTH, 48, 2])
        cond_slot1 = sb("cond_panel1", [P, KD, PANEL])
        gain2 = sb("gain2", [P, KD, 2])
        cond = sb("cond", [P, KD])
        cond2 = sb("cond2", [P, KD, 2])
        ones_d = sb("ones_d", [P, P])
        ones_h = sb("ones_h", [P, P])
        biasC = sb("bias_causal", [P, 4, T])
        poolw = sb("pool_blocks", [P, DEPTH, 2, P])
        relb = sb("rel_table", [32, 4])
        one_lb = sb("one_minus_lb", [P, DEPTH, 4])
        std = sb("std", [P, 2 * T])
        small = sb("small", [P, 64])
        AW = 22656
        arena = sb("arena", [P, AW])
        acc = [ctx.enter_context(nc.psum_tensor(f"acc{i}", [P, 512], F32)) for i in range(BANKS)]
        mix = ctx.enter_context(nc.psum_tensor("mix", [P, 4, 512], F32))
        zrow_d = nc.dram_tensor("bias_rows", [4, 384], F32, kind="Internal")

        def region(off, *dims):
            n = int(np.prod(dims))
            assert off + n <= AW, (off, n)
            v = arena[:, off:off + n]
            if len(dims) == 2:
                v = v.rearrange("p (a b) -> p a b", a=dims[0])
            if len(dims) == 3:
                v = v.rearrange("p (a b c) -> p a b c", a=dims[0], b=dims[1])
            if len(dims) == 4:
                v = v.rearrange("p (a b c d) -> p a b c d", a=dims[0], b=dims[1], c=dims[2])
            return v

        def const(name, off=0, n=None):
            return cst[:, CST[name] + off:CST[name] + off + (n or dict(CONST_SPEC)[name])]

        def col(name, i, p0=0, p1=P):
            return cols[p0:p1, COL[name] + i:COL[name] + i + 1]

        ident = const("ident")
        a2w = const("onehot")[:, 0:T]
        eps_ln, eps_rms, one_col = (const("eps", i, 1) for i in range(3))
        lat = slice(T, 2 * T)
        both = slice(0, 2 * T)
        cond_slots = [H[:, :, 0:T], cond_slot1[:, :, :]]
        cond_part = [[const("mneg", PANEL * (2 * v + i), PANEL) for i in range(2)] for v in range(2)]
        hid = region(0, KF, 2 * T)
        squares = region(0, KD, 2 * T)
        apad = region(0, 2, PAD + T)
        qT, kT, qiT, kiT = region(544, 2, T), region(1056, 2, T), region(1568, 4, T), region(2592, T)
        vt, wi = region(2848, 2, T), region(3360, 2, 8)
        hi, qf, kk, hgs = region(3376, 2, 512), region(4400, 4, T), region(5424, 4, T), region(6448, 4, T)
        gates = region(7472, 24, T)
        ymix = region(13616, KD, T)
        TMP = 15664
        win = [region(TMP + 544 * i, 2, PAD + T) for i in range(4)]
        pdiff = region(TMP + 2176, 2, T)
        relu_s = region(TMP, 8, T)
        bias_rows = region(TMP + 3840, 384)
        score, work, addm = region(TMP + 2048, T), region(TMP + 2304, T), region(TMP + 2560, T)
        logit = region(TMP + 2816, 2, 4, T)
        probT = region(TMP + 4864, 2, 8, P)
        pref, suff = region(TMP, 4 * T), region(TMP + 1024, 4 * T)
        treeX = [region(TMP + 2048 + 1024 * i, 4 * T) for i in range(2)]
        pairs, offd, ptmp = region(TMP + 4096, 8, P), region(TMP + 5120, 4, P), region(TMP + 5632, 8, P)
        osq, onorm, ostd = region(TMP + 2048, 4 * T), region(TMP, 4, T), region(TMP + 1024, 4 * T)
        merged, mtmp = region(TMP, KD, T), region(TMP + 2048, 2, T)
        E_Q, E_K, E_V, E_MQ, E_MV, E_Y, E_T = 0, 1024, 2048, 4096, 8192, 10240, 14336
        gq, gk, gv = region(E_Q, 2, 512), region(E_K, 2, 512), region(E_V, 4, 512)
        mqk, mv = region(E_MQ, 8, 512), region(E_MV, 4, 512)
        ey = region(E_Y, 8, 512)
        logd = H[:, 0:4, :].rearrange("p a t -> p (a t)").rearrange("p (d n) -> p d n", d=2)
        gpref = H[:, 4:6, :].rearrange("p a t -> p (a t)")
        gsuff = H[:, 6:8, :].rearrange("p a t -> p (a t)")
        gX = [region(E_T + 1024 * i, 2, 512) for i in range(2)]
        gpairs = region(E_T + 2048, 16, P)
        goff = region(E_T + 4096, 16, P)
        gcross = region(E_T + 6144, 2, 4, T)
        gtmp = region(E_T + 6144, 8, P)
        qkc = region(0, 8, 512)
        rows16 = biasC[:, 0:2, :].rearrange("p a b -> p (a b)")
        bcol = biasC[:, 2, 0:64].rearrange("p (a b) -> p a b", a=4)
        ones_g = biasC[:, 3, 0:P]
        negid16 = sb("neg_ident", [16, 16])
        bwd_rows = const("eps", 3, 1)[0:16, :]
        lsg = region(E_T + 6144, 512)[0:16, :]
        cum16 = region(E_T + 6656, 512)[0:16, :]
        tmp16 = region(E_T + 7168, 512)[0:16, :]
        rall = H
        dlog = region(E_T, 8, 512)
        psum2 = region(E_T + 4096, 4, 512)
        mprobT = region(E_T + 6144, 4, 512)
        S_X, S_BC = region(0, 4, 512), region(2048, 2, 512)
        S_XC, S_BCC, S_Z = region(3072, 4, 512), region(5120, 2, 512), region(6144, 4, T)
        S_XT, S_BT = region(7168, 4, 512), region(9216, 2, P)
        S_XW, S_ST = region(9472, 2, 2, 512), region(11520, 2, 512)
        S_Y = region(12544, 16, T)
        S_CB = region(16640, 2, 384)
        S_ER, S_CW = region(17408, 2, T), region(17920, 2, T)
        S_DW = region(18432, 2, 384)
        dtr = region(19200, 512)
        dcum, dwe, dtmp = region(19712, 512), region(20224, T), region(20480, 512)
        dtT, dcT, dwT = region(20992, 2, 64), region(21120, 2, 64), region(21248, 2, 64)
        S_SQ = region(21376, 4, T)
        S_STD = region(22400, T)
        negA = small[0:64, 60:61]
        upad_l = region(11264, 2, 4, LATPAD)
        upad_c = region(11264 + 8 * LATPAD, 2, 4, CTXPAD)
        uconv = region(11264 + 8 * LATPAD + 8 * CTXPAD, 2, 4, 512)

        landed = [sem(f"panel_landed{i}") for i in range(SLOTS)]
        ready = [sem(f"acc_ready{i}") for i in range(BANKS)]
        free = [sem(f"acc_free{i}") for i in range(BANKS)]
        half_read = sem("half_read")
        cond_landed = [sem(f"cond_landed{i}") for i in range(2)]
        stage = sem("stage_end")
        named = {}

        def S(name):
            if name not in named:
                named[name] = sem(name)
            return named[name]


        def cond_bank(phase):
            return 3 if phase[:2] in ("he", "in") else 2

        block = ctx.enter_context(nc.Block())

        def stage_end(eng, count):
            count[0] += 1
            eng.drain().then_inc(stage, 1)
            eng.wait_ge(stage, 3 * count[0])

        def groups(eng, g, body):
            first = 0
            if g.p0 < SLOTS:
                for u in range(4):
                    body(0, u)
                first = 1
            with eng.Fori(first, g.n // 4) as it:
                for u in range(4):
                    body(it, u)
            for u in range(g.n % 4):
                body(g.n // 4, u)

        def wait_ready(eng, g, it, u, r=0):
            a = g.a0 + g.apa * u + r
            eng.wait_ge(ready[a % BANKS], it * g.apa + (a // BANKS + 1))
            return a % BANKS

        @block.sync
        def _(sp):
            m0, m1 = CST["mneg"], CST["tri"]
            sp.dma_start(cst[:, 0:m0], io["consts"][:, 0:m0]).then_inc(S("loaded"), 16)
            sp.dma_start(cst[:, m1:NCST], io["consts"][:, m1:NCST]).then_inc(S("consts_loaded"), 16)
            sp.dma_start(cols[:, :], io["cols"]).then_inc(S("loaded"), 16)
            sp.dma_start(X[:, :, :], io["xs"].rearrange("(k p) t -> p k t", p=P)).then_inc(S("loaded"), 16)
            sp.dma_start(poolw[:, :, :, :], io["poolw"]).then_inc(S("loaded"), 16)
            sp.dma_start(relb[:, :], io["rel_bias"]).then_inc(S("loaded"), 16)
            sp.wait_ge(S("consts_loaded"), 16)
            sp.dma_start(a2w[32:96, :], io["a2w"]).then_inc(S("loaded"), 16)

            def load(g, i, static_i):
                src = (w11 if g.wide else w8)[bass.ds(i + g.row0, 1), :, :].rearrange("a p n -> p (a n)")
                s = (g.p0 + static_i) % SLOTS
                width = SLOT_W if g.wide else KD * PANEL
                sp.dma_start(slots[s][:, 0:width], src).then_inc(landed[s], 16)

            def load_static(g, i):
                p = g.p0 + i
                if p >= SLOTS:
                    kind, b, v = finished[p - SLOTS]
                    sp.wait_ge(half_read if kind == "half" else ready[b], v)
                load(g, i, i)

            def load_cond(phase, i, u):
                n0, cnt = CARRY.get(phase, (0, 0))
                if isinstance(i, int) and i >= cnt:
                    return
                if not isinstance(i, int) or i + n0 >= 2:
                    sp.wait_ge(S("cond_part"), i + (n0 - 1))
                src = wc[bass.ds(i + n0, 1), :, :].rearrange("a p (k c) -> p (a k) c", k=KD)
                sp.dma_start(cond_slots[u % 2], src).then_inc(cond_landed[u % 2], 16)

            for i in range(HEAD):
                load_cond("head", i, i)
            for g in order:
                if g.n >= 12 and g.ppa == 1:
                    for i in range(4):
                        load_static(g, i)
                        load_cond(g.name, i, i)
                    with sp.Fori(1, g.n // 4) as it:
                        for u in range(4):
                            a = g.a0 + g.apa * (u + 1) - 1
                            sp.wait_ge(ready[a % BANKS], it * g.apa + (a // BANKS + 1 - g.apa))
                            load(g, it * 4 + u, u)
                            if CARRY.get(g.name, (0, 0))[1] >= g.n - g.n % 4:
                                load_cond(g.name, it * 4 + u, u)
                    for i in range(g.n - g.n % 4, g.n):
                        load_static(g, i)
                        load_cond(g.name, i, i)
                else:
                    for i in range(g.n):
                        load_static(g, i)
                        load_cond(g.name, i, i)
                if g.name == "out11":
                    sp.wait_ge(S("cond_summed"), UNITS)
                    sp.dma_start(const("mneg"), io["consts"][:, m0:m1]).then_inc(S("masks_loaded"), 16)
                if g.name == "in00":
                    sp.wait_ge(S("bias_rows"), 1)
                    sp.dma_start(zrow_d.ap(), bias_rows[0:4, :]).then_inc(S("bias_stored"), 16)
                    sp.wait_ge(S("bias_stored"), 16)
                    sp.dma_start(logit[:, 0, :, :],
                                 bass.AP(zrow_d, 0, [[1, P], [384, 4], [1, T]])).then_inc(S("hankel"), 16)
            sp.wait_ge(S("final"), 1)
            sp.dma_start(io["out"].rearrange("(k p) t -> p k t", p=P), H[:, :, lat]).then_inc(S("stored"), 16)
            sp.wait_ge(S("stored"), 16)

        @block.tensor
        def _(pe):
            count = [0]

            def panel_in(g, it, u):
                s = (g.p0 + u) % SLOTS
                pe.wait_ge(landed[s], it * 16 + 16 * ((g.p0 + u) // SLOTS + 1))
                return slots[s]

            def acc_open(g, it, u, r=0):
                a = g.a0 + g.apa * u + r
                if a >= BANKS or not isinstance(it, int) or it > 0:
                    pe.wait_ge(free[a % BANKS], it * g.apa + a // BANKS)
                return a % BANKS

            def features(g, it, u, rhs, ntok):
                w = panel_in(g, it, u)
                for j in range(2):
                    r = j if ntok == 512 else 0
                    if j == 0 or ntok == 512:
                        b = acc_open(g, it, u, r)
                    o = 0 if ntok == 512 else j * ntok
                    for k in range(KD):
                        mm = pe.matmul(acc[b][:, o:o + ntok], w[:, k * PANEL + j * P:k * PANEL + j * P + P], rhs(k),
                                       start=(k == 0), stop=(k == KD - 1))
                    if j == 1 or ntok == 512:
                        mm.then_inc(ready[b], 1)

            def tokens(g, u, lo, nblk, ncol=PANEL, off=0):
                w = panel_in(g, 0, u)
                for tb in range(nblk):
                    if tb % 2 == 0:
                        b = acc_open(g, 0, u, tb // 2)
                    for k in range(KD):
                        mm = pe.matmul(acc[b][:, tb % 2 * T:tb % 2 * T + ncol], H[:, k, lo + tb * P:lo + tb * P + P],
                                       w[:, k * PANEL + off:k * PANEL + off + ncol], start=(k == 0), stop=(k == KD - 1))
                    if tb % 2 == 1:
                        mm.then_inc(ready[b], 1)

            def cond_sum(phase, i, u):
                n0 = CARRY[phase][0]
                conds = 2 if n0 >= MOD0 else 1
                pe.wait_ge(S("cond_part"), i + (n0 + 1))
                for v in range(conds):
                    for j in range(2):
                        c = i * 2 + (T * v + j)
                        mm = pe.matmul(mix[:, cond_bank(phase), bass.ds(c, 1) if not isinstance(c, int) else slice(c, c + 1)],
                                       cond_part[v][u % 2][:, j * P:j * P + P], one_col, start=True, stop=True)
                mm.then_inc(S("cond_summed"), 1)

            def down(g, src, ntok, kper=KSPLIT, carry=0):
                for n in range(g.n // 2):
                    for part in range(2):
                        i = 2 * n + part
                        w = panel_in(g, 0, i)
                        for j in range(2):
                            a = g.a0 + g.apa * n + (j if ntok == 512 else 0)
                            if part == 0 and (j == 0 or ntok == 512) and a >= BANKS:
                                pe.wait_ge(free[a % BANKS], a // BANKS)
                            o = 0 if ntok == 512 else j * ntok
                            for k in range(kper):
                                first = part == 0 and k == 0 and (j == 0 or ntok == 512)
                                mm = pe.matmul(acc[a % BANKS][:, o:o + ntok],
                                               w[:, k * PANEL + j * P:k * PANEL + j * P + P],
                                               src(part * kper + k), start=first, stop=(part == 1 and k == kper - 1),
                                               skip_group_check=True)
                            if part == 1 and (j == 1 or ntok == 512):
                                mm.then_inc(ready[a % BANKS], 1)
                        if part == 0:
                            mm.then_inc(half_read, 1)
                        if i < carry:
                            cond_sum(g.name, i, i)

            def layer_norm(n, g):
                for i in range(4):
                    a = g.a0 + i
                    pe.wait_ge(free[a % BANKS], a // BANKS + 1)
                    for j in range(2):
                        k = 2 * i + j
                        mm = pe.matmul(mix[:, 0, 0:T], ones_d[:, :], X[:, k, lat], start=(k == 0), stop=(k == KD - 1))
                mm.then_inc(S("mean_ready"), 1)
                for k in range(KD):
                    pe.wait_ge(S("squared"), n * KD + k + 1)
                    mm = pe.matmul(mix[:, 1, 0:T], ones_d[:, :], squares[:, k, 0:T], start=(k == 0), stop=(k == KD - 1))
                mm.then_inc(S("var_ready"), 1)

            def rms_norm(n, sel):
                for k in range(KD):
                    pe.wait_ge(S("rms_sq"), n * KD + k + 1)
                    mm = pe.matmul(mix[:, 0, 0:sel.stop - sel.start], ones_d[:, :], squares[:, k, 0:sel.stop - sel.start],
                                   start=(k == 0), stop=(k == KD - 1))
                mm.then_inc(S("rms_ready"), 1)

            def pool(l):
                pe.wait_ge(S("pool_diff"), l + 1)
                for c in range(2):
                    mm = pe.matmul(mix[:, 0, c * T:c * T + T], poolw[:, l, c, :], pdiff[:, c, :], start=True, stop=True)
                mm.then_inc(S("pool_mm"), 1)

            def attention(l):
                for qb in range(2):
                    n = P * (qb + 1)
                    for b in range(4):
                        if qb == 1:
                            pe.wait_ge(S("idx_relu"), 8 * l + b + 1)
                        for i in range(2):
                            r = slice(64 * (b // 2), 64 * (b // 2) + 64)
                            mm = pe.matmul(mix[:, b, i * T:i * T + n], qiT[r, 2 * (b % 2) + i, qb * P:qb * P + P], kiT[r, 0:n],
                                           start=True, stop=True)
                        mm.then_inc(S("idx_mm"), 1)
                for qb in range(2):
                    n = P * (qb + 1)
                    pe.wait_ge(S("idx_relu"), 8 * l + 4 + 2 * qb + 2)
                    for h in range(4):
                        r = slice(64 * (h % 2), 64 * (h % 2) + 64)
                        mm = pe.matmul(mix[:, 2 * qb + h % 2, h // 2 * T:h // 2 * T + n],
                                       qT[r, h // 2, qb * P:qb * P + P], kT[r, h // 2, 0:n], start=True, stop=True)
                    mm.then_inc(S("logit_mm"), 1)
                for qb in range(2):
                    pe.wait_ge(S("prob_ready"), 2 * l + qb + 1)
                    for h in range(4):
                        for s in range(qb + 1):
                            i = h * (qb + 1) + s
                            mm = pe.transpose(mix[:, 2 * qb + i // 4, i % 4 * P:i % 4 * P + P],
                                              logit[:, qb, h, s * P:s * P + P], ident)
                    mm.then_inc(S("probT_mm"), 1)
                for qb in range(2):
                    pe.wait_ge(S("probT_ready"), 2 * l + qb + 1)
                    for i in range(4):
                        h = 2 * (i % 2) + i // 2
                        for s in range(qb + 1):
                            mm = pe.matmul(mix[64 * (h % 2):64 * (h % 2) + 64, 1, h // 2 * T + qb * P:h // 2 * T + qb * P + P],
                                           vt[:, s, h * 64:h * 64 + 64], probT[:, qb, i * (qb + 1) + s, :],
                                           start=(s == 0), stop=(s == qb))
                mm.then_inc(S("attn_mm"), 1)

            def hgrn(l):
                k4, q4 = kk, qf
                for i in range(9):
                    bank = 2 * (i % 2)
                    if i == 0:
                        pe.wait_ge(S("hg_key"), l + 1)
                    else:
                        pe.wait_ge(S("hg_x"), 8 * l + i)
                    if i >= 2:
                        pe.wait_ge(S("hg_acc"), 9 * l + i - 1)
                    xt = treeX[(i - 1) % 2].rearrange("p (h t) -> p h t", h=4)
                    if i < 8:
                        for b in range(2):
                            for h in range(4):
                                c = slice(b * P, b * P + P)
                                lhs, rhs = (k4[:, h, c], q4[:, h, c]) if i == 0 else (xt[:, h, c], xt[:, h, c])
                                mm = pe.matmul(mix[:, bank + b, h * P:h * P + P], lhs, rhs, start=True, stop=True)
                    else:
                        for h in range(4):
                            mm = pe.matmul(mix[:, bank, h * P:h * P + P], xt[:, h, 0:P], xt[:, h, P:T], start=True, stop=True)
                    mm.then_inc(S("hg_mm"), 1)
                pe.wait_ge(S("hg_acc"), 9 * l + 9)
                for h in range(4):
                    v = slice(h * P, h * P + P)
                    o = lambda t: mix[:, 2 + h // 2, h % 2 * T + t * P:h % 2 * T + t * P + P]
                    pe.matmul(o(0), hi[:, 0, v], pairs[:, h, :], start=True, stop=True)
                    pe.matmul(o(1), hi[:, 0, v], offd[:, h, :], start=True, stop=False)
                    mm = pe.matmul(o(1), hi[:, 1, v], pairs[:, 4 + h, :], start=False, stop=True)
                mm.then_inc(S("hg_o"), 1)
                pe.wait_ge(S("hg_sq"), l + 1)
                for i in range(2):
                    mm = pe.matmul(mix[:, i, :], ones_h[:, :], osq[:, i * 512:i * 512 + 512], start=True, stop=True)
                mm.then_inc(S("hg_ms"), 1)

            def even_tail(l):
                g = G["evengate"]
                w = panel_in(g, 0, 0)
                b = acc_open(g, 0, 0)
                for k in range(KD):
                    mm = pe.matmul(acc[b][0:96, :], w[:, k * PANEL:k * PANEL + 96], H[:, k, :], start=(k == 0), stop=(k == KD - 1))
                mm.then_inc(ready[b], 1)

            def gla():
                pe.wait_ge(S("rank_ready"), 1)
                for d in range(2):
                    r = slice(32 + 32 * d, 48 + 32 * d)
                    for c in range(2):
                        mm = pe.matmul(mix[:, 2 * d + c, :], a2w[r, c * P:c * P + P], rows16[r, :], start=True, stop=True)
                    mm.then_inc(S("decay_mm"), 1)
                n_mm = n_x = 0

                def heads(lhs, rhs, cs, ct, bank0, at):
                    for h in range(4):
                        r = slice(64 * (h % 2), 64 * (h % 2) + 64)
                        o = (2 * at + h // 2) * P
                        m = pe.matmul(mix[:, bank0 + h % 2, o:o + P], lhs[r, h // 2, cs * P:cs * P + P],
                                      rhs[r, h // 2, ct * P:ct * P + P], start=True, stop=True)
                    return m

                pe.wait_ge(S("decay_read"), 2)
                for hf in range(2):
                    for b in range(2):
                        mm = heads(gk, gq, 2 * hf + b, 2 * hf + b, 2 * hf, b)
                    mm.then_inc(S("gla_mm"), 1)
                    n_mm += 1
                for d in range(2):
                    for lv in range(9):
                        n_x += 1
                        pe.wait_ge(S("gla_x"), n_x)
                        xt = gX[d]
                        if lv < 7:
                            for hf in range(2):
                                pe.wait_ge(S("gla_acc"), n_mm if (d, lv, hf) == (1, 0, 0) else n_mm - 1)
                                for b in range(2):
                                    mm = heads(xt, xt, 2 * hf + b, 2 * hf + b, 2 * hf, b)
                                mm.then_inc(S("gla_mm"), 1)
                                n_mm += 1
                        elif lv == 7:
                            pe.wait_ge(S("gla_acc"), n_mm - 1)
                            for st in range(2):
                                s_, t_ = (0, 1) if d == 0 else (1, 0)
                                mm = heads(xt, xt, 2 * st + s_, 2 * st + t_, 0, st)
                            mm.then_inc(S("gla_mm"), 1)
                            n_mm += 1
                pe.wait_ge(S("gla_acc"), n_mm)
                for h in range(4):
                    r = slice(64 * (h % 2), 64 * (h % 2) + 64)
                    for s in range(2):
                        for d in range(2):
                            mm = pe.matmul(mix[:, h, s * T:s * T + T], gX[d][r, h // 2, s * P:s * P + P],
                                           gX[d][r, h // 2, T:2 * T], start=(d == 0), stop=(d == 1))
                mm.then_inc(S("gla_mm"), 1)
                n_mm += 1
                pe.wait_ge(S("gla_acc"), n_mm)
                for h in range(4):
                    for t in range(4):
                        o = mix[:, h, t * P:t * P + P]
                        st, tb = t // 2, t % 2
                        terms = [(2 * st + tb, gpairs[:, 8 * st + 4 * (h % 2) + 2 * tb + h // 2, :]),
                                 (2 * st + 1 - tb, goff[:, 8 * (1 - tb) + 4 * (h % 2) + 2 * st + h // 2, :])]
                        if st == 1:
                            terms += [(s, gcross[:, s, h, tb * P:tb * P + P]) for s in range(2)]
                        for i, (s, rhs) in enumerate(terms):
                            mm = pe.matmul(o, gv[:, s, h * P:h * P + P], rhs, start=(i == 0), stop=(i == len(terms) - 1))
                mm.then_inc(S("gla_o"), 1)
                head_norm(0)

            def head_norm(n):
                pe.wait_ge(S("head_sq"), n + 1)
                for h in range(4):
                    mm = pe.matmul(mix[:, h, :], ones_h[:, :], head_squares[n][:, h, :], start=True, stop=True)
                mm.then_inc(S("head_ms"), 1)

            head_squares = [region(E_T, 4, 512), region(E_T, 4, 512)]

            def mlstm():
                pe.wait_ge(S("ml_rows"), 1)
                for t in range(4):
                    mm = pe.transpose(mix[:, 0, t * 16:t * 16 + 16], cum16[:, t * P:t * P + P], ident[0:16, 0:16])
                mm.then_inc(S("ml_cols"), 1)
                for i in range(8):
                    h, d = i % 4, i // 4
                    if i >= 3:
                        pe.wait_ge(S("ml_rall"), i - 2)
                    li, lf = 8 * d + h, 8 * d + 4 + h
                    o = mix[:, 1 + i % 3, :]
                    pe.matmul(o, ident[0:16, li:li + 1].to_broadcast([16, P]), rows16[0:16, :], start=True, stop=False)
                    mm = pe.matmul(o, negid16[:, lf:lf + 1].to_broadcast([16, P]), cum16[:, :], start=False, stop=True)
                    mm.then_inc(S("ml_sel"), 1)
                pe.wait_ge(S("ml_qk"), 1)
                pe.wait_ge(S("ml_rall"), 8)
                for t in range(4):
                    w = T if t < 2 else 2 * T
                    if t >= 1:
                        pe.wait_ge(S("ml_h"), t)
                    for h in range(4):
                        mm = pe.matmul(mix[:, h, 0:w], qkc[:, h, t * P:t * P + P], qkc[:, 4 + h, 0:w], start=True, stop=True)
                    mm.then_inc(S("ml_scores"), 1)
                    pe.wait_ge(S("ml_prob"), t + 1)
                    for h in range(4):
                        for s in range(w // P):
                            mm = pe.transpose(mix[:, h, s * P:s * P + P], psum2[:, h, s * P:s * P + P], ident)
                    mm.then_inc(S("ml_probT"), 1)
                    pe.wait_ge(S("ml_probT_sb"), t + 1)
                    for h in range(4):
                        for s in range(w // P):
                            mm = pe.matmul(mix[:, h, 0:P], mv[:, s, h * P:h * P + P], mprobT[:, h, s * P:s * P + P],
                                           start=(s == 0), stop=(s == w // P - 1))
                    mm.then_inc(S("ml_hmm"), 1)
                head_norm(1)

            def ssd_rates():
                pe.wait_ge(S("dt_rows"), 1)
                for i in range(2):
                    pe.transpose(mix[:, 0, i * 64:i * 64 + 64], dtr[0:64, T + i * P:T + i * P + P], ident[0:64, 0:64])
                    pe.transpose(mix[:, 0, 128 + i * 64:192 + i * 64], dcum[0:64, T + i * P:T + i * P + P], ident[0:64, 0:64])
                    mm = pe.transpose(mix[:, 0, 256 + i * 64:320 + i * 64], dwe[0:64, i * P:i * P + P], ident[0:64, 0:64])
                mm.then_inc(S("dt_cols"), 1)

            def ssd_group(g):
                for u in range(2):
                    features(G[f"ssdx{g}"], 0, u, lambda k: H[:, k, :], 512)
                features(G[f"ssdbc{g}"], 0, 0, lambda k: H[:, k, :], 512)
                for u in range(2):
                    features(G[f"ssdz{g}"], 0, u, lambda k: H[:, k, lat], T)
                pe.wait_ge(S("ssd_conv"), g + 1)
                for s in range(4):
                    for c in range(4):
                        mm = pe.transpose(mix[:, s, c * P:c * P + P], S_XC[:, c, s * P:s * P + P], ident)
                mm.then_inc(S("ssd_xT"), 1)
                pe.wait_ge(S("ssd_xT_sb"), g + 1)
                for s in range(2):
                    pe.transpose(mix[:, 0, s * P:s * P + P], S_BCC[:, 0, s * P:s * P + P], ident)
                for s in range(2):
                    mm = pe.matmul(mix[:, 1, s * T:s * T + T], S_BCC[:, 0, T + s * P:T + s * P + P], S_BCC[:, 1, lat],
                                   start=True, stop=True)
                mm.then_inc(S("ssd_cb"), 1)
                pe.wait_ge(S("ssd_cb_sb"), g + 1)
                pe.wait_ge(S("ssd_xw"), g + 1)
                for d in range(2):
                    for s in range(2):
                        mm = pe.matmul(mix[:, 2 + d, :], S_BT[:, s, :], S_XW[:, d, s, :], start=(s == 0), stop=(s == 1))
                mm.then_inc(S("ssd_state"), 1)
                pe.wait_ge(S("ssd_state_sb"), g + 1)
                for i in range(16):
                    pr, hh, d = i // 4, i // 2 % 2, i % 2
                    n = 16 * g + i
                    h = 2 * pr + hh
                    row = 32 * d + 8 * g + h
                    if n >= 2:
                        pe.wait_ge(S("ssd_dmin"), n - 1)
                    pe.matmul(mix[:, i % 2, 0:T], ident[0:64, row:row + 1].to_broadcast([64, P]), dcum[0:64, lat],
                              start=True, stop=True).then_inc(S("ssd_row"), 1)
                    if i >= 1:
                        ssd_out(g, i - 1, n - 1)
                ssd_out(g, 15, 16 * g + 15)
                pe.wait_ge(S("ssd_gsq"), g + 1)
                for c in range(4):
                    mm = pe.matmul(mix[:, 0, 0:T], ones_g[:, :], S_SQ[:, c, :], start=(c == 0), stop=(c == 3))
                mm.then_inc(S("ssd_gms"), 1)

            def ssd_out(g, i, n):
                pr, hh, d = i // 4, i // 2 % 2, i % 2
                h = 2 * pr + hh
                r = slice(64 * hh, 64 * hh + 64)
                v = slice(h * 64, h * 64 + 64)
                y = mix[:, 2 + pr % 2, :]
                first, last = i % 2 == 0, i % 2 == 1
                if i % 4 == 0 and i >= 8:
                    pe.wait_ge(S("ssd_y"), 4 * g + pr - 1)
                pe.wait_ge(S("ssd_w"), n + 1)
                w = S_DW[:, n % 2, :]
                pe.matmul(y[r, 0:T], S_ST[:, d, v], S_CW[:, n % 2, :], start=first, stop=False, skip_group_check=True)
                if d == 0:
                    pe.matmul(y[r, 0:T], S_XT[:, 2, v], w[:, 0:T], start=False, stop=False, skip_group_check=True)
                    mm = pe.matmul(y[r, P:T], S_XT[:, 3, v], w[:, T:T + P], start=False, stop=last, skip_group_check=True)
                else:
                    pe.matmul(y[r, 0:T], S_XT[:, 3, v], w[:, P:P + T], start=False, stop=False, skip_group_check=True)
                    mm = pe.matmul(y[r, 0:P], S_XT[:, 2, v], w[:, 0:P], start=False, stop=last, skip_group_check=True)
                mm.then_inc(S("ssd_ymm"), 1)

            pe.wait_ge(S("loaded"), 96)
            pe.matmul(mix[0:4, 0, 0:384], relb[:, :], const("onehot")[0:32, :], start=True, stop=True).then_inc(S("bias_mm"), 1)
            for i in range(HEAD):
                cond_sum("head", i, i)
            stage_end(pe, count)
            norms = 0
            for l in range(DEPTH):
                for f in range(2):
                    if f == 1:
                        if l == 0:
                            pe.wait_ge(S("hankel"), 16)
                            for i in range(2):
                                mm = pe.matmul(mix[:, i, :], const("flip"), logit[:, 0, 2 * i:2 * i + 2, :], start=True, stop=True)
                            mm.then_inc(S("bias_flip"), 1)
                        pe.wait_ge(S("h_ready"), 3 * l + 2)
                        g = G[f"mix{l}"]
                        rhs = lambda k: H[:, k, lat]
                        for u in range(15):
                            if u == 5:
                                w = panel_in(g, 0, u)
                                b = acc_open(g, 0, u)
                                for k in range(KD):
                                    pe.matmul(acc[b][:, 0:T], w[:, k * PANEL:k * PANEL + P], rhs(k), start=(k == 0), stop=(k == KD - 1))
                                for tb in range(2):
                                    for k in range(KD):
                                        mm = pe.matmul(acc[b][:, T + 8 * tb:T + 8 * tb + 8], H[:, k, T + tb * P:T + tb * P + P],
                                                       w[:, k * PANEL + P:k * PANEL + P + 8], start=(k == 0), stop=(k == KD - 1))
                                mm.then_inc(ready[b], 1)
                            elif u in (6, 7, 8):
                                tokens(g, u, T, 2)
                            else:
                                features(g, 0, u, rhs, T)
                            if u < CARRY[f"mix{l}"][1]:
                                cond_sum(f"mix{l}", u, u)
                        groups(pe, G[f"gate{l}"], lambda it, u, g=G[f"gate{l}"]: features(g, it, u, rhs, T))
                        stage_end(pe, count)
                        pool(l)
                        stage_end(pe, count)
                        attention(l)
                        stage_end(pe, count)
                        hgrn(l)
                        stage_end(pe, count)
                        g = G[f"branch{l}"]
                        for u in range(4):
                            w = panel_in(g, 0, u)
                            for r, ks in enumerate((range(0, 2), range(2, 4), range(4, 8))):
                                b = acc_open(g, 0, u, r)
                                for j in range(2):
                                    for k in ks:
                                        mm = pe.matmul(acc[b][:, j * T:j * T + T], w[:, k * PANEL + j * P:k * PANEL + j * P + P],
                                                       ymix[:, k, :], start=(k == ks[0]), stop=(k == ks[-1]))
                                mm.then_inc(ready[b], 1)
                        stage_end(pe, count)
                        g = G[f"mixout{l}"]
                        for u in range(4):
                            features(g, 0, u, lambda k: merged[:, k, :], T)
                        layer_norm(norms, g)
                        norms += 1
                        stage_end(pe, count)
                    pe.wait_ge(S("h_ready"), 3 * l + 1 + 2 * f)

                    def up_panel(it, u, name=f"in{l}{f}"):
                        features(G[name], it, u, lambda k: H[:, k, lat], T)
                        cond_sum(name, it * 4 + u, u)

                    groups(pe, G[f"in{l}{f}"], up_panel)
                    pe.wait_ge(S("hid_ready"), 2 * l + f + 1)
                    down(G[f"out{l}{f}"], lambda k: hid[:, k, 0:T], T, carry=CARRY.get(f"out{l}{f}", (0, 0))[1])
                    layer_norm(norms, G[f"out{l}{f}"])
                    norms += 1
                    stage_end(pe, count)
            rms = 0
            for l in range(DEPTH):
                rms_norm(rms, both)
                rms += 1
                stage_end(pe, count)
                if l == 0:
                    for u in range(14):
                        if u in (2, 3, 10, 11):
                            tokens(G["even"], u, 0, 4)
                        else:
                            features(G["even"], 0, u, lambda k: H[:, k, :], 512)
                    even_tail(l)
                    stage_end(pe, count)
                    gla()
                    stage_end(pe, count)
                    mlstm()
                    stage_end(pe, count)
                    for u in range(4):
                        features(G["evenout"], 0, u, lambda k: ey[:, k, :], 512)
                else:
                    g = G["dt"]
                    w = panel_in(g, 0, 0)
                    b = acc_open(g, 0, 0)
                    for k in range(KD):
                        mm = pe.matmul(acc[b][0:64, :], w[:, k * PANEL:k * PANEL + 64], H[:, k, :], start=(k == 0), stop=(k == KD - 1))
                    mm.then_inc(ready[b], 1)
                    ssd_rates()
                    stage_end(pe, count)
                    for g in range(4):
                        ssd_group(g)
                        stage_end(pe, count)
                    down(G["ssdout"], lambda k: S_Y[:, k, :], T, KD)
                stage_end(pe, count)
                sel = both if l == 0 else lat
                rms_norm(rms, sel)
                rms += 1
                stage_end(pe, count)
                ntok = 512 if l == 0 else T
                groups(pe, G[f"up{l}"], lambda it, u, g=G[f"up{l}"]: features(g, it, u, lambda k: H[:, k, sel], ntok))
                pe.wait_ge(S("ffn_hid"), l + 1)
                down(G[f"down{l}"], lambda k: hid[:, k, 0:ntok], ntok)
                stage_end(pe, count)
            rms_norm(rms, lat)

        @block.scalar
        def _(act):
            act = InOrder(act)
            count = [0]

            def evac(g, it, u, r, dst, src_cols, func, scale=1.0):
                b = wait_ready(act, g, it, u, r)
                src = acc[b][:, src_cols]
                if len(dst.shape) == 3:
                    src = src.rearrange("p (a b) -> p a b", a=dst.shape[1])
                act.activation(dst, src, func, scale=scale).then_inc(free[b], 1)

            def layer_norm(n, l, j):
                for k in range(KD):
                    act.wait_ge(S("centred"), n * KD + k + 1)
                    act.activation(squares[:, k, 0:T], X[:, k, lat], ACT.Square).then_inc(S("squared"), 1)
                act.wait_ge(S("var_ready"), n + 1)
                act.activation(std[:, 0:T], mix[:, 1, 0:T], ACT.Sqrt, bias=eps_ln).then_inc(S("std_ready"), 1)
                for k in range(KD):
                    act.wait_ge(S("scaled"), n * KD + k + 1)
                    c = (3 * l + j) * KD + k
                    act.activation(X[:, k, lat], X[:, k, lat], ACT.Identity, scale=col("ln_g", c), bias=col("ln_b", c))\
                       .then_inc(S("x_ready"), 1)

            def rms_norm(n, sel):
                w = sel.stop - sel.start
                for k in range(KD):
                    act.activation(squares[:, k, 0:w], X[:, k, sel], ACT.Square).then_inc(S("rms_sq"), 1)
                act.wait_ge(S("rms_ready"), n + 1)
                act.activation(std[:, 0:w], mix[:, 0, 0:w], ACT.Sqrt, bias=eps_rms).then_inc(S("rms_std"), 1)

            def pool(l):
                act.wait_ge(S("pool_mm"), l + 1)
                for c in range(2):
                    act.activation(ymix[:, c, :], mix[:, 0, c * T:c * T + T], ACT.Identity, scale=col("pool_scale", 2 * l + c))

            def attention(l):
                for qb in range(2):
                    n = P * (qb + 1)
                    for pr in range(4):
                        act.wait_ge(S("idx_mm"), 8 * l + 4 * qb + pr + 1)
                        if qb == 1 and pr == 0:
                            act.wait_ge(S("idx_sum"), 2 * l + 1)
                        act.activation(relu_s[:, 2 * pr:2 * pr + 2, 0:n],
                                       mix[:, pr, :].rearrange("p (a t) -> p a t", a=2)[:, :, 0:n], ACT.Relu)\
                           .then_inc(S("idx_relu"), 1)
                for qb in range(2):
                    n = P * (qb + 1)
                    act.wait_ge(S("logit_ready"), 2 * l + qb + 1)
                    for h in range(4):
                        e = act.activation(logit[:, qb, h, 0:n], logit[:, qb, h, 0:n], ACT.Exp,
                                           bias=small[:, 8 * qb + h:8 * qb + h + 1],
                                           accum_out=small[:, 8 * qb + 4 + h:8 * qb + 5 + h])
                    act.drain().then_inc(S("exp_ready"), 1)
                for qb in range(2):
                    act.wait_ge(S("probT_mm"), 2 * l + qb + 1)
                    m = 4 * (qb + 1)
                    act.activation(probT[:, qb, 0:m, :].rearrange("p a b -> p (a b)"),
                                   mix[:, 2 * qb:2 * qb + qb + 1, :].rearrange("p a b -> p (a b)"), ACT.Copy)\
                       .then_inc(S("probT_ready"), 1)
                act.wait_ge(S("attn_mm"), l + 1)
                act.activation(ymix[:, 2:4, :].rearrange("p a b -> p (a b)"), mix[:, 1, :], ACT.Copy)

            def halves(v, m):
                return v.rearrange("p (n two m) -> p n two m", two=2, m=m)

            def hgrn(l):
                act.wait_ge(S("hg_key"), l + 1)
                act.activation(pref, pref, ACT.Ln, bias=one_col)
                act.drain()
                for lv in range(8):
                    m = 1 << lv
                    if lv >= 1:
                        act.wait_ge(S("hg_sums"), 7 * l + lv)
                    else:
                        act.wait_ge(S("hg_zero"), l + 1)
                    if lv >= 2:
                        act.wait_ge(S("hg_mm"), 9 * l + lv)
                    x = halves(treeX[lv % 2], m)
                    act.activation(x[:, :, 0, :], halves(suff, m)[:, :, 0, :], ACT.Exp)
                    act.activation(x[:, :, 1, :], halves(pref, m)[:, :, 1, :], ACT.Exp).then_inc(S("hg_exp"), 1)
                act.wait_ge(S("hg_o"), l + 1)
                act.activation(osq, mix[:, 2:4, :].rearrange("p a b -> p (a b)"), ACT.Square).then_inc(S("hg_sq"), 1)
                act.wait_ge(S("hg_ms"), l + 1)
                act.activation(ostd, mix[:, 0:2, :].rearrange("p a b -> p (a b)"), ACT.Sqrt, bias=eps_rms)\
                   .then_inc(S("hg_std"), 1)

            def gla():
                for d in range(2):
                    act.wait_ge(S("decay_mm"), d + 1)
                    for c in range(2):
                        act.activation(gX[0][:, c, :], mix[:, 2 * d + c, :], ACT.Identity, bias=col("gla_ab_2", 2 * d + c))
                    act.drain().then_inc(S("decay_read"), 1)
                    act.activation(gX[1][:, :, :], gX[0][:, :, :], ACT.Abs)
                    act.drain()
                    act.activation(gX[1][:, :, :], gX[1][:, :, :], ACT.Exp, scale=-1.0)
                    act.drain()
                    act.activation(gX[1][:, :, :], gX[1][:, :, :], ACT.Ln, bias=one_col).then_inc(S("decay_ln"), 1)
                    act.wait_ge(S("decay_log"), d + 1)
                for d in range(2):
                    for lv in range(9):
                        m = 1 << lv
                        n = 9 * d + lv
                        act.wait_ge(S("gla_sums"), n + 1)
                        if lv >= 1:
                            act.wait_ge(S("gla_mm"), gla_read(d, lv))
                        x = halves(gX[d].rearrange("p c t -> p (c t)"), m)
                        e, o = (0, 1) if (d == 0 or lv == 8) else (1, 0)
                        act.activation(x[:, :, e, :], halves(gsuff, m)[:, :, e, :], ACT.Exp)
                        act.activation(x[:, :, o, :], halves(gpref, m)[:, :, o, :], ACT.Exp).then_inc(S("gla_exp"), 1)
                act.wait_ge(S("gla_o"), 1)
                act.activation(gv[:, :, :], mix[:, :, :], ACT.Copy)
                act.activation(region(E_T, 4, 512), mix[:, :, :], ACT.Square)
                act.drain().then_inc(S("head_sq"), 1)
                act.wait_ge(S("head_ms"), 1)
                act.activation(region(E_T, 4, 512), mix[:, :, :], ACT.Sqrt, bias=eps_rms).then_inc(S("head_std"), 1)

            def gla_read(d, lv):
                return 2 + 15 * d + 2 * min(lv, 7) + (1 if lv == 8 else 0)

            def mlstm():
                act.activation(tmp16[:, :], rows16[0:16, :], ACT.Abs)
                act.drain()
                act.activation(tmp16[:, :], tmp16[:, :], ACT.Exp, scale=-1.0)
                act.drain()
                act.activation(tmp16[:, :], tmp16[:, :], ACT.Ln, bias=one_col[0:16, :]).then_inc(S("ml_ln"), 1)
                for c in range(8):
                    act.wait_ge(S("ml_conv"), c + 1)
                    i = act.activation(qkc[:, c, :], qkc[:, c, :], ACT.Silu)
                i.then_inc(S("ml_qk"), 1)
                act.wait_ge(S("ml_cols"), 1)
                act.activation(bcol[:, :, :], mix[:, 0, 0:64].rearrange("p (a b) -> p a b", a=4), ACT.Copy).then_inc(S("ml_bcol"), 1)
                for i in range(8):
                    act.wait_ge(S("ml_sel"), i + 1)
                    act.activation(rall[:, i, :], mix[:, 1 + i % 3, :], ACT.Copy).then_inc(S("ml_rall"), 1)
                for t in range(4):
                    w = T if t < 2 else 2 * T
                    act.wait_ge(S("ml_max"), t + 1)
                    for i in range(8):
                        act.activation(dlog[:, i, 0:w], dlog[:, i, 0:w], ACT.Exp, bias=small[:, i:i + 1])
                    act.activation(small[:, 8:16], small[:, 0:8], ACT.Exp)
                    act.drain().then_inc(S("ml_exp"), 1)
                    act.wait_ge(S("ml_probT"), t + 1)
                    act.activation(mprobT[:, :, 0:w], mix[:, :, 0:w], ACT.Copy).then_inc(S("ml_probT_sb"), 1)
                    act.wait_ge(S("ml_hmm"), t + 1)
                    act.activation(mqk[:, 0:4, t * P:t * P + P], mix[:, :, 0:P], ACT.Copy).then_inc(S("ml_h"), 1)
                act.wait_ge(S("ml_gated"), 1)
                act.activation(region(E_T, 4, 512), mqk[:, 0:4, :], ACT.Square).then_inc(S("head_sq"), 1)
                act.wait_ge(S("head_ms"), 2)
                act.activation(region(E_T, 4, 512), mix[:, :, :], ACT.Sqrt, bias=eps_rms).then_inc(S("head_std"), 1)

            def ssd_rates():
                b = wait_ready(act, G["dt"], 0, 0)
                act.activation(dtr[0:64, :], acc[b][0:64, :], ACT.Identity, bias=col("ssd_dt_bias_2", 0, 0, 64)).then_inc(free[b], 1)
                act.activation(negA, col("ssd_a_log_2", 0, 0, 64), ACT.Exp)
                act.drain()
                act.activation(dcum[0:64, :], dtr[0:64, :], ACT.Abs)
                act.drain()
                act.activation(dcum[0:64, :], dcum[0:64, :], ACT.Exp, scale=-1.0).then_inc(S("dt_exp"), 1)
                act.wait_ge(S("dt_onep"), 1)
                act.activation(dtmp[0:64, :], dtmp[0:64, :], ACT.Ln).then_inc(S("dt_ln"), 1)
                act.wait_ge(S("dt_end"), 1)
                act.activation(dwe[0:64, :], dwe[0:64, :], ACT.Exp).then_inc(S("dt_wend"), 1)
                act.wait_ge(S("dt_cols"), 1)
                for dst, o in ((dtT, 0), (dcT, 128), (dwT, 256)):
                    act.activation(dst[:, :, :], mix[:, 0, o:o + 128].rearrange("p (a b) -> p a b", a=2), ACT.Copy)

            def ssd_group(g):
                for u in range(2):
                    for r in range(2):
                        evac(G[f"ssdx{g}"], 0, u, r, S_X[:, 2 * u + r, :], both, ACT.Copy)
                for r in range(2):
                    evac(G[f"ssdbc{g}"], 0, 0, r, S_BC[:, r, :], both, ACT.Copy)
                act.drain().then_inc(S("ssd_raw"), 1)
                for u in range(2):
                    evac(G[f"ssdz{g}"], 0, u, 0, S_Z[:, 2 * u:2 * u + 2, :], both, ACT.Silu)
                act.wait_ge(S("ssd_cv"), g + 1)
                act.activation(S_XC[:, :, :], S_XC[:, :, :], ACT.Silu)
                act.activation(S_BCC[:, :, :], S_BCC[:, :, :], ACT.Silu)
                act.drain().then_inc(S("ssd_conv"), 1)
                act.wait_ge(S("ssd_xT"), g + 1)
                act.activation(S_XT[:, :, :], mix[:, :, :], ACT.Copy).then_inc(S("ssd_xT_sb"), 1)
                act.wait_ge(S("ssd_cb"), g + 1)
                act.activation(S_BT[:, :, :], mix[:, 0, 0:T].rearrange("p (a b) -> p a b", a=2), ACT.Copy).then_inc(S("ssd_bt"), 1)
                act.wait_ge(S("ssd_state"), g + 1)
                act.activation(S_ST[:, :, :], mix[:, 2:4, :], ACT.Copy).then_inc(S("ssd_state_sb"), 1)
                for i in range(16):
                    n = 16 * g + i
                    act.wait_ge(S("ssd_row"), n + 1)
                    if n >= 2:
                        act.wait_ge(S("ssd_cw"), n - 1)
                    act.activation(S_ER[:, n % 2, :], mix[:, i % 2, 0:T], ACT.Exp).then_inc(S("ssd_erow"), 1)
                    act.wait_ge(S("ssd_dmin"), n + 1)
                    act.activation(S_DW[:, n % 2, :], S_DW[:, n % 2, :], ACT.Exp).then_inc(S("ssd_edec"), 1)
                act.wait_ge(S("ssd_yz"), g + 1)
                act.activation(S_SQ[:, :, :], S_Y[:, 4 * g:4 * g + 4, :], ACT.Square).then_inc(S("ssd_gsq"), 1)
                act.wait_ge(S("ssd_gms"), g + 1)
                act.activation(S_STD, mix[:, 0, 0:T], ACT.Sqrt, bias=eps_rms).then_inc(S("ssd_gstd"), 1)

            def ffn_up(l):
                g = G[f"up{l}"]

                def body(it, u):
                    par = u // 2
                    for j in range(2):
                        r = j if l == 0 else 0
                        c = 2 * (u % 2) + j
                        if j == 0 or l == 0:
                            b = wait_ready(act, g, it, u, r)
                        if j == 0 and u % 2 == 0:
                            conv_wait(act, l, it, par)
                        o = j * T if l == 1 else T
                        last = act.activation(
                            upad_l[:, par, c, :].rearrange("p (r w) -> p r w", r=GRID_ROWS + 2)[:, 1:GRID_ROWS + 1, 1:GRID_W + 1],
                            acc[b][:, o:o + T].rearrange("p (r w) -> p r w", r=GRID_ROWS), ACT.Copy)
                        if l == 0:
                            last = act.activation(upad_c[:, par, c, 1:T + 1], acc[b][:, 0:T], ACT.Copy)
                        if j == 1 or l == 0:
                            last.then_inc(free[b], 1)
                    if u % 2 == 1:
                        act.drain().then_inc(S("up_raw"), 1)
                        w = 512 if l == 0 else T
                        act.wait_ge(S("up_conv"), it * 2 + (11 * l + par + 1))
                        act.activation(uconv[:, par, 2:4, 0:w], uconv[:, par, 2:4, 0:w], ACT.Silu).then_inc(S("up_silu"), 1)

                groups(act, g, body)

            def conv_wait(eng, l, it, par):
                eng.wait_ge(S("up_read"), it * 2 + (13 * l + par + 1))

            act.wait_ge(S("loaded"), 96)
            act.activation(cond[:, :], cols[:, COL["c"]:COL["c"] + 8], ACT.Silu)
            act.activation(cond2[:, :, 0], cols[:, COL["c_2"]:COL["c_2"] + 8], ACT.Silu)
            act.activation(cond2[:, :, 1], cols[:, COL["c_ctx_2"]:COL["c_ctx_2"] + 8], ACT.Silu)
            act.drain().then_inc(S("cond_ready"), 1)
            act.wait_ge(S("bias_mm"), 1)
            act.activation(bias_rows[0:4, :], mix[0:4, 0, 0:384], ACT.Copy).then_inc(S("bias_rows"), 1)
            act.wait_ge(S("lb_diff"), 1)
            act.activation(small[:, 0:8], small[:, 0:8], ACT.Exp).then_inc(S("lb_exp"), 1)
            n = 0
            stage_end(act, count)
            for l in range(DEPTH):
                for f in range(2):
                    if f == 1:
                        g = G[f"mix{l}"]
                        for u in range(15):
                            if u == 0:
                                evac(g, 0, u, 0, apad[:, :, PAD:PAD + T], both, ACT.Copy)
                            elif u == 5:
                                b = wait_ready(act, g, 0, u)
                                act.activation(kiT, acc[b][:, 0:T], ACT.Copy)
                                act.activation(wi[:, :, :], acc[b][:, T:T + 16].rearrange("p (a b) -> p a b", a=2), ACT.Copy)\
                                   .then_inc(free[b], 1)
                            else:
                                dst, func, scale = {
                                    1: (qT[:, :, :], ACT.Copy, 1.0), 2: (kT[:, :, :], ACT.Copy, 1.0),
                                    3: (qiT[:, 0:2, :], ACT.Copy, 1.0), 4: (qiT[:, 2:4, :], ACT.Copy, 1.0),
                                    6: (vt[:, :, :], ACT.Copy, 1.0), 7: (hi[:, :, 0:T], ACT.Copy, 1.0),
                                    8: (hi[:, :, T:512], ACT.Copy, 1.0), 9: (qf[:, 0:2, :], ACT.Silu, 1.0),
                                    10: (qf[:, 2:4, :], ACT.Silu, 1.0), 11: (hgs[:, 0:2, :], ACT.Silu, 1.0),
                                    12: (hgs[:, 2:4, :], ACT.Silu, 1.0), 13: (kk[:, 0:2, :], ACT.Sigmoid, -1.0),
                                    14: (kk[:, 2:4, :], ACT.Sigmoid, -1.0)}[u]
                                evac(g, 0, u, 0, dst, both, func, scale)
                        groups(act, G[f"gate{l}"],
                               lambda it, u, g=G[f"gate{l}"]: evac(g, it, u, 0, gates[:, bass.ds(it * 8 + 2 * u, 2), :], both, ACT.Sigmoid))
                        stage_end(act, count)
                        pool(l)
                        stage_end(act, count)
                        attention(l)
                        stage_end(act, count)
                        hgrn(l)
                        stage_end(act, count)
                        stage_end(act, count)
                        layer_norm(n, l, 1)
                        n += 1
                        stage_end(act, count)
                    groups(act, G[f"in{l}{f}"],
                           lambda it, u, g=G[f"in{l}{f}"]: evac(g, it, u, 0, hid[:, bass.ds(it * 4 + u, 2), 0:T], both, ACT.Silu)
                           if u % 2 == 0 else None)
                    layer_norm(n, l, 2 * f)
                    n += 1
                    stage_end(act, count)
            rms = 0
            for l in range(DEPTH):
                rms_norm(rms, both)
                rms += 1
                stage_end(act, count)
                if l == 0:
                    g = G["even"]
                    feat = {0: gq, 1: gk, 4: ey[:, 0:2, :], 5: ey[:, 2:4, :], 6: mqk[:, 0:2, :], 7: mqk[:, 2:4, :],
                            8: mqk[:, 4:6, :], 9: mqk[:, 6:8, :], 12: ey[:, 4:6, :], 13: ey[:, 6:8, :]}
                    func = {4: ACT.Silu, 5: ACT.Silu, 12: ACT.Sigmoid, 13: ACT.Sigmoid}
                    for u in range(14):
                        for r in range(2):
                            if u in (2, 3, 10, 11):
                                dst = gv if u < 4 else mv
                                evac(g, 0, u, r, dst[:, 2 * r:2 * r + 2, u % 2 * T:u % 2 * T + T], both, ACT.Copy)
                            else:
                                evac(g, 0, u, r, feat[u][:, r, :], both, func.get(u, ACT.Copy), 0.125 if u == 0 else 1.0)
                    b = wait_ready(act, G["evengate"], 0, 0)
                    act.activation(rows16[0:16, :], acc[b][0:16, :], ACT.Identity, bias=col("ml_gate_b_2", 0, 0, 16))
                    act.activation(rows16[32:64, :], acc[b][32:64, :], ACT.Copy)
                    act.activation(rows16[64:96, :], acc[b][64:96, :], ACT.Copy).then_inc(free[b], 1)
                    act.drain().then_inc(S("rank_ready"), 1)
                    stage_end(act, count)
                    gla()
                    stage_end(act, count)
                    mlstm()
                    stage_end(act, count)
                else:
                    ssd_rates()
                    stage_end(act, count)
                    for g in range(4):
                        ssd_group(g)
                        stage_end(act, count)
                stage_end(act, count)
                rms_norm(rms, both if l == 0 else lat)
                rms += 1
                stage_end(act, count)
                ffn_up(l)
                stage_end(act, count)
            rms_norm(rms, lat)

        @block.vector
        def _(dve):
            dve = InOrder(dve)
            count = [0]

            def stt(out, a, s, b, op0, op1, **kw):
                return dve.scalar_tensor_tensor(out=out, in0=a, scalar=s, in1=b, op0=op0, op1=op1, **kw)

            def bc(v, n):
                return v.unsqueeze(1).to_broadcast([v.shape[0], n, v.shape[1]])

            def cond_weigh(phase, i, u):
                n0 = CARRY[phase][0]
                conds = [cond2[:, :, 0], cond2[:, :, 1]] if n0 >= MOD0 else [cond]
                w, parts = cond_slots[u % 2], [p[u % 2] for p in cond_part]
                dve.wait_ge(cond_landed[u % 2], i * 8 + (8 * (n0 - u % 2) + 16))
                if not isinstance(i, int) or i + n0 >= 2:
                    dve.wait_ge(S("cond_summed"), i + (n0 - 1))
                for k in range(KD):
                    for c, part in zip(conds, parts):
                        if k == 0:
                            dve.eng.tensor_tensor(part, w[:, 0, :], c[:, 0:1].to_broadcast([P, PANEL]), ALU.mult)
                        else:
                            dve.eng.scalar_tensor_tensor(out=part, in0=w[:, k, :], scalar=c[:, k:k + 1], in1=part, op0=ALU.mult, op1=ALU.add)
                    if k < KD - 1:
                        dve.drain()
                dve.drain().then_inc(S("cond_part"), 1)

            def cond_take(phase):
                n0, cnt = CARRY[phase]
                dve.wait_ge(S("cond_summed"), n0 + cnt)
                src = mix[:, cond_bank(phase), :]
                for first, size, table in [(l * ADA, ADA, mods1[:, l, :]) for l in range(DEPTH)] + \
                                          [(MOD0 + l * MOD, MOD, mods2[:, l, :, :]) for l in range(DEPTH)]:
                    a, b = max(n0, first), min(n0 + cnt, first + size)
                    if a >= b:
                        continue
                    t0, t1, s0, s1 = 2 * (a - first), 2 * (b - first), 2 * (a - n0), 2 * (b - n0)
                    if n0 >= MOD0:
                        bias = cols[:, COL["mod_b_2"] + 2 * (a - MOD0):COL["mod_b_2"] + 2 * (b - MOD0)]
                        for v in range(2):
                            dve.tensor_tensor(table[:, t0:t1, v], src[:, T * v + s0:T * v + s1], bias, ALU.add)
                    else:
                        bias = cols[:, COL["b_ada"] + 2 * a:COL["b_ada"] + 2 * b]
                        dve.tensor_tensor(table[:, t0:t1], src[:, s0:s1], bias, ALU.add)
                        for j in (0, 2):
                            if t0 <= 24 * j + 16 and 24 * j + 24 <= t1:
                                gt = table[:, 24 * j + 16:24 * j + 24]
                                dve.tensor_scalar(gt, gt, 0.5, None, ALU.mult)

            def modulated(l, j):
                mod1 = mods1[:, l, :]
                for k in range(KD):
                    i = dve.tensor_scalar(H[:, k, lat], X[:, k, lat], mod1[:, 24 * j + 8 + k:24 * j + 9 + k],
                                          mod1[:, 24 * j + k:24 * j + k + 1], ALU.mult, ALU.add)
                i.then_inc(S("h_ready"), 1)
                dve.tensor_scalar(X[:, :, lat], X[:, :, lat], float(ALPHA), None, ALU.mult)
                dve.drain()

            def residual(g, l, gate0):
                mod1 = mods1[:, l, :]
                for n in range(4):
                    b = wait_ready(dve, g, 0, n)
                    for j in range(2):
                        k = 2 * n + j
                        i = stt(X[:, k, lat], acc[b][:, j * T:j * T + T], mod1[:, gate0 + k:gate0 + k + 1], X[:, k, lat], ALU.mult, ALU.add)
                    i.then_inc(free[b], 1)

            def layer_norm(n):
                dve.wait_ge(S("mean_ready"), n + 1)
                for k in range(KD):
                    dve.tensor_tensor(X[:, k, lat], X[:, k, lat], mix[:, 0, 0:T], ALU.subtract).then_inc(S("centred"), 1)
                dve.wait_ge(S("std_ready"), n + 1)
                dve.reciprocal(std[:, 0:T], std[:, 0:T])
                dve.drain()
                for k in range(KD):
                    dve.tensor_tensor(X[:, k, lat], X[:, k, lat], std[:, 0:T], ALU.mult).then_inc(S("scaled"), 1)
                dve.wait_ge(S("x_ready"), KD * (n + 1))

            def rms_norm(n, sel, gain, shift, streams):
                w = sel.stop - sel.start
                dve.wait_ge(S("rms_std"), n + 1)
                dve.reciprocal(std[:, 0:w], std[:, 0:w])
                dve.drain()
                dve.tensor_tensor(H[:, :, sel], X[:, :, sel], bc(std[:, 0:w], KD), ALU.mult)
                dve.drain()
                for k in range(KD):
                    for v in streams:
                        t = lat if v == 0 else slice(0, T)
                        if shift is None:
                            i = dve.tensor_scalar(H[:, k, t], H[:, k, t], gain(k, v), None, ALU.mult)
                        else:
                            i = dve.tensor_scalar(H[:, k, t], H[:, k, t], gain(k, v), shift[:, k, v:v + 1], ALU.mult, ALU.add)
                return i

            def pool(l):
                src = apad
                for i, w in enumerate((1, 2, 4, 8)):
                    dve.tensor_copy(win[i][:, :, 0:w], src[:, :, 0:w])
                    dve.tensor_tensor(win[i][:, :, w:PAD + T], src[:, :, w:PAD + T], src[:, :, 0:PAD + T - w], ALU.add)
                    dve.drain()
                    src = win[i]
                cnt = const("invcnt").rearrange("p (a t) -> p a t", a=2)
                for i in range(4):
                    r = slice(64 * (i % 2), 64 * (i % 2) + 64)
                    dve.tensor_tensor(pdiff[r, i // 2, :], win[i][r, i // 2, PAD:PAD + T], cnt[r, i // 2, :], ALU.mult)
                dve.drain()
                dve.tensor_tensor(pdiff[:, :, :], pdiff[:, :, :], apad[:, :, PAD:PAD + T], ALU.subtract).then_inc(S("pool_diff"), 1)

            def attention(l):
                for qb in range(2):
                    n = P * (qb + 1)
                    off = 0 if qb == 1 else P
                    for h in range(8):
                        if h % 2 == 0:
                            dve.wait_ge(S("idx_relu"), 8 * l + 4 * qb + h // 2 + 1)
                        head = 2 * (2 * (h // 2 % 2) + h % 2) + h // 4
                        w = wi[:, qb, head:head + 1]
                        if h == 0:
                            i = dve.tensor_scalar(score[:, 0:n], relu_s[:, h, 0:n], w, None, ALU.mult)
                        else:
                            i = stt(score[:, 0:n], relu_s[:, h, 0:n], w, score[:, 0:n], ALU.mult, ALU.add)
                        if h == 7:
                            i.then_inc(S("idx_sum"), 1)
                        dve.drain()
                    stt(score[:, 0:n], score[:, 0:n], IDX_SCALE, const("causal")[:, off:off + n], ALU.mult, ALU.add)
                    dve.drain()
                    src = score
                    for r in range(TOPK // 8):
                        dve.max(small[:, 16:24], src[:, 0:n])
                        dve.drain()
                        dve.match_replace(work[:, 0:n], small[:, 16:24], src[:, 0:n], GONE)
                        dve.drain()
                        src = work
                    dve.tensor_tensor(addm[:, 0:n], work[:, 0:n], score[:, 0:n], ALU.is_equal)
                    dve.drain()
                    dve.tensor_scalar(addm[:, 0:n], addm[:, 0:n], MASKED, None, ALU.mult)
                    dve.drain()
                    dve.wait_ge(S("logit_mm"), 2 * l + qb + 1)
                    lg = logit[:, qb, :, 0:n]
                    src = mix[:, 2 * qb:2 * qb + 2, :].rearrange("p a (b t) -> p (a b) t", b=2)[:, :, 0:n]
                    stt(lg, src, 64 ** -0.5, biasC[:, :, off:off + n], ALU.mult, ALU.add)
                    dve.drain()
                    dve.tensor_tensor(lg, lg, bc(addm[:, 0:n], 4), ALU.add)
                    dve.drain()
                    dve.tensor_reduce(small[:, 8 * qb:8 * qb + 4], lg, AXX, ALU.max, negate=True).then_inc(S("logit_ready"), 1)
                for qb in range(2):
                    n = P * (qb + 1)
                    dve.wait_ge(S("exp_ready"), 2 * l + qb + 1)
                    r = small[:, 8 * qb + 4:8 * qb + 8]
                    dve.reciprocal(r, r)
                    dve.drain()
                    dve.tensor_tensor(logit[:, qb, :, 0:n], logit[:, qb, :, 0:n],
                                      r.unsqueeze(2).to_broadcast([P, 4, n]), ALU.mult).then_inc(S("prob_ready"), 1)

            def halves(v, m):
                return v.rearrange("p (n two m) -> p n two m", two=2, m=m)

            def last_bc(v, e, edge, m):
                return halves(v, m)[:, :, e, edge:edge + 1].to_broadcast([P, v.shape[1] // (2 * m), m])

            def hgrn(l):
                for h in range(4):
                    dve.tensor_scalar(kk[:, h, :], kk[:, h, :], one_lb[:, l, h:h + 1], None, ALU.mult)
                dve.drain()
                dve.tensor_scalar(pref, kk[:, :, :].rearrange("p a b -> p (a b)"), KEY_MAX, -1.0, ALU.min, ALU.mult)
                dve.drain().then_inc(S("hg_key"), 1)
                dve.memset(suff, 0.0).then_inc(S("hg_zero"), 1)
                mask = const("tree_f")
                kf, qq = kk[:, :, :].rearrange("p a b -> p (a b)"), qf[:, :, :].rearrange("p a b -> p (a b)")

                def take(i):
                    bank = 2 * (i % 2)
                    dve.wait_ge(S("hg_mm"), 9 * l + i + 1)
                    src = mix[:, bank:bank + 2, :].rearrange("p a (h t) -> p (a h) t", h=4)
                    if i == 0:
                        dve.tensor_tensor(pairs[:, :, :], src, bc(ident, 8), ALU.mult).then_inc(S("hg_acc"), 1)
                    elif i < 8:
                        dve.tensor_tensor(ptmp[:, :, :], src, bc(mask[:, (i - 1) * P:i * P], 8), ALU.mult).then_inc(S("hg_acc"), 1)
                        dve.drain()
                        dve.tensor_tensor(pairs[:, :, :], pairs[:, :, :], ptmp[:, :, :], ALU.add)
                    else:
                        dve.tensor_copy(offd[:, :, :], src[:, 0:4, :])
                        dve.drain().then_inc(S("hg_acc"), 1)

                for lv in range(8):
                    m = 1 << lv
                    x = halves(treeX[lv % 2], m)
                    dve.wait_ge(S("hg_exp"), 8 * l + lv + 1)
                    if lv < 7:
                        dve.tensor_tensor(halves(suff, m)[:, :, 0, :], halves(suff, m)[:, :, 0, :], last_bc(pref, 1, m - 1, m), ALU.add)
                        dve.drain()
                        dve.tensor_tensor(halves(pref, m)[:, :, 1, :], halves(pref, m)[:, :, 1, :], last_bc(pref, 0, m - 1, m), ALU.add)
                        dve.drain().then_inc(S("hg_sums"), 1)
                    dve.tensor_tensor(x[:, :, 0, :], x[:, :, 0, :], halves(kf, m)[:, :, 0, :], ALU.mult)
                    dve.tensor_tensor(x[:, :, 1, :], x[:, :, 1, :], halves(qq, m)[:, :, 1, :], ALU.mult)
                    dve.drain().then_inc(S("hg_x"), 1)
                    take(lv)
                take(8)
                dve.wait_ge(S("hg_std"), l + 1)
                dve.reciprocal(ostd, ostd)
                dve.drain()
                dve.tensor_tensor(onorm[:, :, :].rearrange("p a b -> p (a b)"), mix[:, 2:4, :].rearrange("p a b -> p (a b)"), ostd, ALU.mult)
                dve.drain()
                for h in range(4):
                    stt(ymix[:, 4 + h, :], onorm[:, h, :], col("hgrn_norm_g", 4 * l + h), hgs[:, h, :], ALU.mult, ALU.mult)

            def branch(l):
                g = G[f"branch{l}"]
                for u in range(4):
                    for r in range(3):
                        b = wait_ready(dve, g, 0, u, r)
                        src = acc[b][:, :].rearrange("p (a t) -> p a t", a=2)
                        dst = merged[:, 2 * u:2 * u + 2, :]
                        gt = gates[:, 8 * r + 2 * u:8 * r + 2 * u + 2, :]
                        if r == 0:
                            dve.tensor_tensor(dst, src, gt, ALU.mult).then_inc(free[b], 1)
                        else:
                            dve.tensor_tensor(mtmp[:, :, :], src, gt, ALU.mult).then_inc(free[b], 1)
                            dve.drain()
                            dve.tensor_tensor(dst, dst, mtmp[:, :, :], ALU.add)
                        dve.drain()

            def gla():
                for d in range(2):
                    dve.wait_ge(S("decay_ln"), d + 1)
                    v = gX[0][:, :, :].rearrange("p a b -> p (a b)")
                    stt(logd[:, d, :], v, 0.0, gX[1][:, :, :].rearrange("p a b -> p (a b)"), ALU.min, ALU.subtract)
                    dve.drain()
                    dve.tensor_scalar(logd[:, d, :], logd[:, d, :], 1.0 / 16.0, None, ALU.mult)
                    dve.drain().then_inc(S("decay_log"), 1)
                n_mm = 0

                def take(d, lv, hf):
                    nonlocal n_mm
                    n_mm += 1
                    dve.wait_ge(S("gla_mm"), n_mm)
                    src = mix[:, 2 * hf:2 * hf + 2, :].rearrange("p a (h t) -> p (a h) t", h=4)
                    dst = gpairs[:, 8 * hf:8 * hf + 8, :]
                    if lv < 0:
                        stt(dst, src, 2.0, bc(ident, 8), ALU.mult, ALU.mult).then_inc(S("gla_acc"), 1)
                    else:
                        mask = const("tree_f" if d == 0 else "tree_b", lv * P, P)
                        dve.tensor_tensor(gtmp[:, :, :], src, bc(mask, 8), ALU.mult).then_inc(S("gla_acc"), 1)
                        dve.drain()
                        dve.tensor_tensor(dst, dst, gtmp[:, :, :], ALU.add)
                    dve.drain()

                for hf in range(2):
                    take(0, -1, hf)
                kf, qq = gk[:, :, :].rearrange("p a b -> p (a b)"), gq[:, :, :].rearrange("p a b -> p (a b)")
                for d in range(2):
                    if d == 1:
                        dve.wait_ge(S("gla_exp"), 9)
                    dve.tensor_copy(gpref, logd[:, d, :])
                    dve.memset(gsuff, 0.0)
                    dve.drain().then_inc(S("gla_sums"), 1)
                    for lv in range(9):
                        m = 1 << lv
                        x = halves(gX[d].rearrange("p c t -> p (c t)"), m)
                        e, o = (0, 1) if (d == 0 or lv == 8) else (1, 0)
                        edge = m - 1 if d == 0 else 0
                        dve.wait_ge(S("gla_exp"), 9 * d + lv + 1)
                        if lv < 8:
                            dve.tensor_tensor(halves(gsuff, m)[:, :, e, :], halves(gsuff, m)[:, :, e, :], last_bc(gpref, o, edge, m), ALU.add)
                            dve.drain()
                            dve.tensor_tensor(halves(gpref, m)[:, :, o, :], halves(gpref, m)[:, :, o, :], last_bc(gpref, e, edge, m), ALU.add)
                            dve.drain().then_inc(S("gla_sums"), 1)
                        dve.tensor_tensor(x[:, :, e, :], x[:, :, e, :], halves(kf, m)[:, :, e, :], ALU.mult)
                        dve.tensor_tensor(x[:, :, o, :], x[:, :, o, :], halves(qq, m)[:, :, o, :], ALU.mult)
                        dve.drain().then_inc(S("gla_x"), 1)
                        if lv < 7:
                            take(d, lv, 0)
                            take(d, lv, 1)
                        elif lv == 7:
                            n_mm += 1
                            dve.wait_ge(S("gla_mm"), n_mm)
                            dve.tensor_copy(goff[:, 8 * d:8 * d + 8, :].rearrange("p a t -> p (a t)"), mix[:, 0:2, :].rearrange("p a t -> p (a t)"))
                            dve.drain().then_inc(S("gla_acc"), 1)
                n_mm += 1
                dve.wait_ge(S("gla_mm"), n_mm)
                dve.tensor_copy(gcross[:, :, :, :], mix[:, :, :].rearrange("p h (s t) -> p s h t", s=2))
                dve.drain().then_inc(S("gla_acc"), 1)
                dve.wait_ge(S("head_std"), 1)
                rs = region(E_T, 4, 512)
                dve.reciprocal(rs, rs)
                dve.drain()
                dve.tensor_tensor(rs, rs, gv[:, :, :], ALU.mult)
                dve.drain()
                for h in range(4):
                    stt(ey[:, h, :], rs[:, h, :], col("gla_norm_g_2", h), ey[:, h, :], ALU.mult, ALU.mult)

            def conv3(dst, src, w, b, c, nch, nst):
                s2 = src.rearrange("p (s t) -> p s t", s=nst)
                d2 = dst.rearrange("p (s t) -> p s t", s=nst)
                dve.tensor_scalar(dst, src, col(w, nch + c), col(b, c), ALU.mult, ALU.add)
                dve.drain()
                stt(d2[:, :, 1:T], s2[:, :, 0:T - 1], col(w, c), d2[:, :, 1:T], ALU.mult, ALU.add)
                dve.drain()
                return stt(d2[:, :, 0:T - 1], s2[:, :, 1:T], col(w, 2 * nch + c), d2[:, :, 0:T - 1], ALU.mult, ALU.add)

            def mlstm():
                for c in range(8):
                    conv3(qkc[:, c, :], mqk[:, c, :], "ml_conv_w_2", "ml_conv_b_2", c, 8, 2).then_inc(S("ml_conv"), 1)
                dve.wait_ge(S("ml_ln"), 1)
                stt(lsg[:, :], rows16[0:16, :], 0.0, tmp16[:, :], ALU.min, ALU.subtract)
                dve.memset(tmp16[:, :], 1.0)
                dve.drain()
                dve.tensor_tensor_scan(cum16[:, :], tmp16[:, :], lsg[:, :], 0.0, ALU.mult, ALU.add)
                dve.drain()
                dve.tensor_tensor(tmp16[:, :], lsg[:, :], cum16[:, :], ALU.subtract)
                dve.drain()
                dve.tensor_scalar(tmp16[:, 0:T], tmp16[:, 0:T], cum16[:, T - 1:T], None, ALU.add)
                dve.tensor_scalar(tmp16[:, T:512], tmp16[:, T:512], cum16[:, 511:512], cum16[:, T - 1:T], ALU.add, ALU.add)
                dve.drain()
                dve.tensor_tensor(tmp16[:, :], tmp16[:, :], cum16[:, :], ALU.subtract)
                dve.drain()
                stt(cum16[:, :], tmp16[:, :], bwd_rows, cum16[:, :], ALU.mult, ALU.add)
                dve.drain().then_inc(S("ml_rows"), 1)
                dve.wait_ge(S("masks_loaded"), 16)
                dve.wait_ge(S("ml_bcol"), 1)
                dve.wait_ge(S("ml_rall"), 8)
                scale = 128 ** -0.5
                for t in range(4):
                    w = T if t < 2 else 2 * T
                    o = 0 if t < 2 else T
                    for i in range(8):
                        h, d = i % 4, i // 4
                        b = bcol[:, t, 8 * d + 4 + h:8 * d + 5 + h]
                        mask = const("mneg", (2 * d + t % 2) * T, T)
                        stt(dlog[:, i, o:o + T], rall[:, i, o:o + T], b, mask, ALU.add, ALU.add)
                        if t >= 2:
                            dve.tensor_scalar(dlog[:, i, 0:T], rall[:, i, 0:T], b, None, ALU.add)
                    dve.drain()
                    dve.tensor_reduce(small[:, 0:8], dlog[:, :, 0:w], AXX, ALU.max)
                    dve.drain()
                    dve.tensor_scalar(small[:, 0:8], small[:, 0:8], 0.0, -1.0, ALU.max, ALU.mult)
                    dve.drain().then_inc(S("ml_max"), 1)
                    dve.wait_ge(S("ml_exp"), t + 1)
                    dve.wait_ge(S("ml_scores"), t + 1)
                    for i in range(8):
                        stt(dlog[:, i, 0:w], dlog[:, i, 0:w], scale, mix[:, i % 4, 0:w], ALU.mult, ALU.mult,
                            accum_out=small[:, 16 + i:17 + i])
                    dve.drain()
                    stt(small[:, 16:24], small[:, 16:24], -1.0, small[:, 16:24], ALU.mult, ALU.max)
                    dve.drain()
                    dve.tensor_tensor(small[:, 16:24], small[:, 16:24], small[:, 8:16], ALU.max)
                    dve.drain()
                    dve.reciprocal(small[:, 16:24], small[:, 16:24])
                    dve.drain()
                    for h in range(4):
                        dve.tensor_scalar(psum2[:, h, 0:w], dlog[:, h, 0:w], small[:, 16 + h:17 + h], None, ALU.mult)
                    dve.drain()
                    for h in range(4):
                        stt(psum2[:, h, 0:w], dlog[:, 4 + h, 0:w], small[:, 20 + h:21 + h], psum2[:, h, 0:w], ALU.mult, ALU.add)
                    dve.drain().then_inc(S("ml_prob"), 1)
                dve.wait_ge(S("ml_h"), 4)
                dve.tensor_tensor(mqk[:, 0:4, :], mqk[:, 0:4, :], ey[:, 4:8, :], ALU.mult).then_inc(S("ml_gated"), 1)
                dve.wait_ge(S("head_std"), 2)
                rs = region(E_T, 4, 512)
                dve.reciprocal(rs, rs)
                dve.drain()
                for h in range(4):
                    stt(ey[:, 4 + h, :], mqk[:, h, :], col("ml_norm_g_2", h), rs[:, h, :], ALU.mult, ALU.mult)

            def ssd_rates():
                dve.wait_ge(S("dt_exp"), 1)
                e, u, d64 = dcum[0:64, :], dtmp[0:64, :], dtr[0:64, :]
                dve.tensor_scalar(u, e, 1.0, None, ALU.add)
                dve.drain().then_inc(S("dt_onep"), 1)
                sp_q, sp_m = S_X[0:64, 0, :], S_X[0:64, 1, :]
                dve.tensor_scalar(sp_q, e, 1.0, -1.0, ALU.add, ALU.add)
                dve.drain()
                dve.tensor_scalar(sp_m, sp_q, 0.0, None, ALU.is_equal)
                dve.drain()
                dve.tensor_tensor(sp_q, sp_q, sp_m, ALU.add)
                dve.drain()
                dve.reciprocal(sp_q, sp_q)
                dve.drain()
                dve.wait_ge(S("dt_ln"), 1)
                dve.tensor_tensor(u, u, sp_q, ALU.mult)
                dve.drain()
                dve.tensor_tensor(u, u, sp_m, ALU.add)
                dve.drain()
                dve.tensor_tensor(u, u, e, ALU.mult)
                dve.drain()
                stt(d64, d64, 0.0, u, ALU.max, ALU.add)
                dve.tensor_scalar(negA, negA, -1.0, None, ALU.mult)
                dve.drain()
                dta = u
                dve.tensor_scalar(dta, d64, negA, None, ALU.mult)
                dve.memset(sp_q, 1.0)
                dve.drain()
                f = dcum[0:64, :]
                for s in range(2):
                    dve.tensor_tensor_scan(f[:, s * T:s * T + T], sp_q[:, 0:T], dta[:, s * T:s * T + T], 0.0, ALU.mult, ALU.add)
                dve.drain()
                we = dwe[0:64, :]
                dve.tensor_scalar(we[0:32, :], f[0:32, 0:T], -1.0, f[0:32, T - 1:T], ALU.mult, ALU.add)
                dve.tensor_tensor(we[32:64, :], f[32:64, 0:T], dta[32:64, 0:T], ALU.subtract)
                dve.tensor_tensor(sp_m[32:64, 0:T], dta[32:64, lat], f[32:64, lat], ALU.subtract)
                dve.tensor_copy(sp_m[32:64, T:T + 1], f[32:64, 511:512])
                dve.drain().then_inc(S("dt_end"), 1)
                dve.tensor_scalar(f[32:64, lat], sp_m[32:64, 0:T], sp_m[32:64, T:T + 1], None, ALU.add)
                dve.drain()
                dve.wait_ge(S("dt_wend"), 1)
                dve.tensor_tensor(we, we, d64[:, 0:T], ALU.mult)
                dve.drain().then_inc(S("dt_rows"), 1)

            def ssd_group(g):
                dve.wait_ge(S("ssd_raw"), g + 1)
                for c in range(4):
                    i = conv3(S_XC[:, c, :], S_X[:, c, :], "ssd_conv_w_2", "ssd_conv_b_2", 4 * g + c, 24, 2)
                for c in range(2):
                    i = conv3(S_BCC[:, c, :], S_BC[:, c, :], "ssd_conv_w_2", "ssd_conv_b_2", 16 + 4 * c + g, 24, 2)
                dve.drain().then_inc(S("ssd_cv"), 1)
                dve.wait_ge(S("ssd_xT_sb"), g + 1)
                for d in range(2):
                    for s in range(2):
                        w = dwT[:, s, 32 * d + 8 * g:32 * d + 8 * g + 8].unsqueeze(2).to_broadcast([P, 8, 64])
                        dve.tensor_tensor(S_XW[:, d, s, :].rearrange("p (h q) -> p h q", h=8),
                                          S_XT[:, s, :].rearrange("p (h q) -> p h q", h=8), w, ALU.mult)
                dve.drain().then_inc(S("ssd_xw"), 1)
                dve.wait_ge(S("ssd_cb"), g + 1)
                dve.wait_ge(S("ssd_bt"), g + 1)
                up, dn = const("tri", 0, P), const("tri", P, P)
                dve.tensor_tensor(S_CB[:, 0, 0:P], mix[:, 1, 0:P], up, ALU.mult)
                dve.tensor_copy(S_CB[:, 0, P:T], mix[:, 1, P:T])
                dve.tensor_tensor(S_CB[:, 0, T:T + P], mix[:, 1, T + P:512], up, ALU.mult)
                dve.tensor_tensor(S_CB[:, 1, 0:P], mix[:, 1, 0:P], dn, ALU.mult)
                dve.tensor_copy(S_CB[:, 1, P:T], mix[:, 1, T:T + P])
                dve.tensor_tensor(S_CB[:, 1, T:T + P], mix[:, 1, T + P:512], dn, ALU.mult)
                dve.drain().then_inc(S("ssd_cb_sb"), 1)
                for i in range(16):
                    pr, hh, d = i // 4, i // 2 % 2, i % 2
                    n = 16 * g + i
                    row = 32 * d + 8 * g + 2 * pr + hh
                    R = mix[:, i % 2, :]
                    W = S_DW[:, n % 2, :]
                    if n >= 2:
                        dve.wait_ge(S("ssd_ymm"), n - 1)
                    dve.wait_ge(S("ssd_erow"), n + 1)
                    cs = [dcT[:, s, row:row + 1] for s in range(2)]
                    spans = ((0, T, 0, T), (T, T + P, P, T)) if d == 0 else ((0, P, 0, P), (P, P + T, 0, T))
                    for s, (a, b, t0, t1) in enumerate(spans):
                        dve.tensor_scalar(W[:, a:b], R[:, t0:t1], cs[s], 0.0, ALU.subtract, ALU.min)
                    dve.drain().then_inc(S("ssd_dmin"), 1)
                    dve.tensor_tensor(S_CW[:, n % 2, :], S_ER[:, n % 2, :], S_BCC[:, 1, lat], ALU.mult)
                    dve.drain().then_inc(S("ssd_cw"), 1)
                    dve.wait_ge(S("ssd_edec"), n + 1)
                    for s, (a, b, t0, t1) in enumerate(spans):
                        stt(W[:, a:b], W[:, a:b], dtT[:, s, row:row + 1], S_CB[:, d, a:b], ALU.mult, ALU.mult)
                    dve.drain().then_inc(S("ssd_w"), 1)
                    if i % 4 == 1 and i >= 4:
                        ssd_take(g, i // 4 - 1)
                ssd_take(g, 3)
                dve.drain()
                dve.tensor_tensor(S_Y[:, 4 * g:4 * g + 4, :], S_Y[:, 4 * g:4 * g + 4, :], S_Z[:, :, :], ALU.mult)\
                   .then_inc(S("ssd_yz"), 1)
                dve.wait_ge(S("ssd_gstd"), g + 1)
                dve.reciprocal(S_STD, S_STD)
                dve.drain()
                for c in range(4):
                    k = 4 * g + c
                    stt(S_Y[:, k, :], S_Y[:, k, :], col("ssd_norm_g_2", k), S_STD, ALU.mult, ALU.mult)

            def ssd_take(g, pr):
                dve.wait_ge(S("ssd_ymm"), 16 * g + 4 * pr + 4)
                k = 4 * g + pr
                stt(S_Y[:, k, :], S_XC[:, pr, lat], col("ssd_d_2", k), mix[:, 2 + pr % 2, 0:T], ALU.mult, ALU.add)\
                    .then_inc(S("ssd_y"), 1)

            def ffn_up(l):
                g = G[f"up{l}"]
                dve.memset(upad_l[:, :, :, :].rearrange("p a b c -> p (a b c)"), 0.0)
                dve.memset(upad_c[:, :, :, :].rearrange("p a b c -> p (a b c)"), 0.0)
                dve.drain().then_inc(S("up_read"), 2)

                def wcol(it, tap, half, j, u):
                    base = COL["ffn_conv_w_2"] + (l * 9 + tap) * 44 + half * 22
                    return cols[:, bass.ds(it * 4 + (base + 2 * (u // 2) + j), 1)]

                def body(it, u):
                    if u % 2 == 0:
                        return
                    par = u // 2
                    dve.wait_ge(S("up_raw"), it * 2 + (11 * l + par + 1))
                    lo = T if l == 0 else 0
                    for tap in range(-1, 9):
                        for half in range(2):
                            for j in range(2):
                                c = 2 * half + j
                                pad = upad_l[:, par, c, :].rearrange("p (r w) -> p r w", r=GRID_ROWS + 2)
                                out = uconv[:, par, c, lo:lo + T].rearrange("p (r w) -> p r w", r=GRID_ROWS)
                                oc = uconv[:, par, c, 0:T]
                                if tap == -1:
                                    base = COL["ffn_conv_b_2"] + l * 44 + half * 22
                                    b = cols[:, bass.ds(it * 4 + (base + 2 * par + j), 1)]
                                    dve.tensor_scalar(out, pad[:, 1:5, 1:65], wcol(it, 4, half, j, u), b, ALU.mult, ALU.add)
                                    if l == 0:
                                        dve.tensor_scalar(oc, upad_c[:, par, c, 1:T + 1], wcol(it, 4, half, j, u), b, ALU.mult, ALU.add)
                                elif tap != 4:
                                    dr, dc = tap // 3, tap % 3
                                    stt(out, pad[:, dr:dr + 4, dc:dc + 64], wcol(it, tap, half, j, u), out, ALU.mult, ALU.add)
                                    if l == 0 and dr == 1:
                                        stt(oc, upad_c[:, par, c, dc:dc + T], wcol(it, tap, half, j, u), oc, ALU.mult, ALU.add)
                        dve.drain()
                    dve.drain().then_inc(S("up_conv"), 1)
                    dve.drain().then_inc(S("up_read"), 1)
                    w = 512 if l == 0 else T
                    dve.wait_ge(S("up_silu"), it * 2 + (11 * l + par + 1))
                    dve.tensor_tensor(hid[:, bass.ds(it * 4 + 2 * par, 2), 0:w], uconv[:, par, 0:2, 0:w], uconv[:, par, 2:4, 0:w], ALU.mult)

                groups(dve, g, body)
                dve.drain().then_inc(S("ffn_hid"), 1)

            def add_branch(g, gate, streams):
                for u in range(g.n // g.ppa):
                    for j in range(2):
                        k = 2 * u + j
                        if len(streams) == 2 or j == 0:
                            b = wait_ready(dve, g, 0, u, j if len(streams) == 2 else 0)
                        for v in streams:
                            t = lat if v == 0 else slice(0, T)
                            src = acc[b][:, t] if len(streams) == 2 else acc[b][:, j * T:j * T + T]
                            i = stt(X[:, k, t], src, gate[:, k, v:v + 1], X[:, k, t], ALU.mult, ALU.add)
                        if len(streams) == 2 or j == 1:
                            i.then_inc(free[b], 1)
                dve.drain()

            dve.memset(ones_d[:, :], 1.0 / D)
            dve.memset(ones_h[:, :], 1.0 / P)
            dve.wait_ge(S("loaded"), 96)
            lb = [cols[:, COL["hgrn_lb"] + 4 * i:COL["hgrn_lb"] + 4 * i + 4] for i in range(DEPTH)]
            dve.tensor_tensor(small[:, 8:12], lb[0], lb[1], ALU.max)
            dve.drain()
            for i in range(DEPTH):
                dve.tensor_tensor(small[:, 4 * i:4 * i + 4], lb[i], small[:, 8:12], ALU.subtract)
            dve.drain().then_inc(S("lb_diff"), 1)
            dve.tensor_scalar(negid16[:, :], ident[0:16, 0:16], -1.0, None, ALU.mult)
            dve.wait_ge(S("lb_exp"), 1)
            dve.tensor_tensor(small[:, 8:12], small[:, 0:4], small[:, 4:8], ALU.add)
            dve.drain()
            dve.reciprocal(small[:, 8:12], small[:, 8:12])
            dve.drain()
            for i in range(DEPTH):
                dve.tensor_tensor(small[:, 4 * i:4 * i + 4], small[:, 4 * i:4 * i + 4], small[:, 8:12], ALU.mult)
            dve.memset(one_lb[:, 0, :], 0.0)
            dve.drain()
            dve.tensor_tensor(one_lb[:, 1, :], small[:, 0:4], small[:, 4:8], ALU.add)
            dve.drain()
            dve.tensor_tensor(one_lb[:, 1, :], one_lb[:, 1, :], small[:, 0:4], ALU.subtract)
            dve.drain()
            dve.tensor_scalar(one_lb[:, :, :], one_lb[:, :, :], -1.0, 1.0, ALU.mult, ALU.add)
            for l in range(DEPTH):
                b3 = cols[:, COL["b_ada"] + 72 * l:COL["b_ada"] + 72 * l + 72].rearrange("p (j w) -> p j w", j=3)
                dve.tensor_scalar(b3[:, :, 8:24], b3[:, :, 8:24], 1.0, None, ALU.add)
            dve.drain()
            dve.wait_ge(S("cond_ready"), 1)
            for i in range(HEAD):
                cond_weigh("head", i, i)
            cond_take("head")
            stage_end(dve, count)
            n = 0
            for l in range(DEPTH):
                modulated(l, 0)
                for f in range(2):
                    if f == 1:
                        modulated(l, 1)
                        if l == 0:
                            dve.wait_ge(S("bias_flip"), 1)
                            dve.tensor_tensor(biasC[:, :, :], mix[:, 0:2, :].rearrange("p a (b t) -> p (a b) t", b=2), bc(const("causal"), 4), ALU.add)
                        for i in range(CARRY[f"mix{l}"][1]):
                            cond_weigh(f"mix{l}", i, i)
                        cond_take(f"mix{l}")
                        dve.memset(apad[:, :, 0:PAD], 0.0)
                        stage_end(dve, count)
                        pool(l)
                        stage_end(dve, count)
                        attention(l)
                        stage_end(dve, count)
                        hgrn(l)
                        stage_end(dve, count)
                        branch(l)
                        stage_end(dve, count)
                        residual(G[f"mixout{l}"], l, 24 + 16)
                        layer_norm(n)
                        n += 1
                        stage_end(dve, count)
                        modulated(l, 2)

                    def gate_up(it, u, g=G[f"in{l}{f}"]):
                        cond_weigh(g.name, it * 4 + u, u)
                        if u % 2 == 0:
                            return
                        b = wait_ready(dve, g, it, u)
                        a = g.a0 + u - 1
                        dve.wait_ge(free[a % BANKS], it + (a // BANKS + 1))
                        h = hid[:, bass.ds(it * 4 + u - 1, 2), 0:T]
                        dve.tensor_tensor(h, h, acc[b][:, :].rearrange("p (a t) -> p a t", a=2), ALU.mult).then_inc(free[b], 1)

                    groups(dve, G[f"in{l}{f}"], gate_up)
                    dve.drain().then_inc(S("hid_ready"), 1)
                    cond_take(f"in{l}{f}")
                    for i in range(CARRY.get(f"out{l}{f}", (0, 0))[1]):
                        cond_weigh(f"out{l}{f}", i, i)
                    residual(G[f"out{l}{f}"], l, 48 * f + 16)
                    if f"out{l}{f}" in CARRY:
                        cond_take(f"out{l}{f}")
                    layer_norm(n)
                    n += 1
                    stage_end(dve, count)
            rms = 0
            for l in range(DEPTH):
                mod2 = mods2[:, l, :, :]

                def gains(name, s0):
                    for v in range(2):
                        stt(gain2[:, :, v], mod2[:, s0:s0 + 8, v], 1.0, cols[:, COL[name] + 8 * l:COL[name] + 8 * l + 8], ALU.add, ALU.mult)
                    dve.drain()

                gains("norm_mix_g_2", 8)
                if l == 0:
                    dve.memset(ones_g, 1.0 / 512)
                by = lambda k, v: gain2[:, k, v:v + 1]
                rms_norm(rms, both, by, mod2[:, 0:8, :], (0, 1))
                rms += 1
                stage_end(dve, count)
                if l == 0:
                    stage_end(dve, count)
                    gla()
                    stage_end(dve, count)
                    mlstm()
                    stage_end(dve, count)
                    add_branch(G["evenout"], mod2[:, 16:24, :], (0, 1))
                else:
                    ssd_rates()
                    stage_end(dve, count)
                    for g in range(4):
                        ssd_group(g)
                        stage_end(dve, count)
                    add_branch(G["ssdout"], mod2[:, 16:24, :], (0,))
                gains("norm_ffn_g_2", 32)
                stage_end(dve, count)
                streams = (0, 1) if l == 0 else (0,)
                rms_norm(rms, both if l == 0 else lat, by, mod2[:, 24:32, :], streams)
                rms += 1
                stage_end(dve, count)
                ffn_up(l)
                add_branch(G[f"down{l}"], mod2[:, 40:48, :], streams)
                stage_end(dve, count)
            rms_norm(rms, lat, lambda k, v: col("final_norm_g_2", k), None, (0,))
            dve.drain().then_inc(S("final"), 1)


def bucket_of(dist):
    if dist < 16:
        return dist
    large = 16 + int(np.float32(np.log(np.float32(dist) / np.float32(16)) / np.log(128 / 16)) * np.float32(16))
    return min(large, 31)


def constants():
    c = np.zeros((P, NCST), np.float32)

    def put(name, v, off=0):
        c[:v.shape[0], CST[name] + off:CST[name] + off + v.shape[1]] = v

    i = np.arange(P)
    s, t = i[:, None], i[None, :]
    put("ident", (s == t).astype(np.float32))
    put("flip", (s + t == P - 1).astype(np.float32))
    for lv in range(NLEV):
        m = 1 << lv
        f = ((s // (2 * m) == t // (2 * m)) & (s // m % 2 == 0) & (t // m % 2 == 1)).astype(np.float32)
        put("tree_f", f, lv * P)
        put("tree_b", f.T, lv * P)
    j = np.arange(T)[None, :]
    put("causal", np.where(P + s - j < 0, NEG, 0).astype(np.float32))
    for d in range(2):
        for par in range(2):
            ok = j <= P * par + s if d == 0 else j >= P * par + s
            put("mneg", np.where(ok, 0, MASKED).astype(np.float32), (2 * d + par) * T)
    put("tri", (t >= s).astype(np.float32))
    put("tri", (t <= s).astype(np.float32), P)
    for c_ in range(2):
        w = np.array([POOL_WINDOWS[2 * c_ + h] for h in range(2)]).repeat(64)[:, None]
        put("invcnt", (1.0 / np.minimum(j + 1, w)).astype(np.float32), c_ * T)
    dist = np.maximum(T - 1 - np.arange(384), 0)
    put("onehot", (np.arange(32)[:, None] == np.array([bucket_of(int(x)) for x in dist])[None, :]).astype(np.float32))
    put("eps", np.array([[LN_EPS, RMS_EPS, 1.0]], np.float32).repeat(P, 0))
    put("eps", ((i >= 8) & (i < 16)).astype(np.float32)[:, None], 3)
    return c


def panels(w, starts):
    k = w.shape[0]
    out = np.zeros((len(starts), P, k // P, PANEL), w.dtype)
    for n, a in enumerate(starts):
        b = w[:, a:a + PANEL]
        out[n, :, :, :b.shape[1]] = b.reshape(k // P, P, -1).transpose(1, 0, 2)
    return out.reshape(len(starts), P, -1)


def down_panels(w, rows):
    out = [panels(w[r:r + rows], [a]) for a in range(0, w.shape[1], PANEL) for r in range(0, w.shape[0], rows)]
    return np.concatenate(out)


def custom_panel(pieces):
    out = np.zeros((1, P, KD, PANEL), np.float32)
    for w, at in pieces:
        out[0, :, :, at:at + w.shape[1]] = w.reshape(KD, P, -1).transpose(1, 0, 2)
    return out.reshape(1, P, -1)


def weight_stream(x):
    w8, w11, wc = [], [], []
    step = lambda a, n: [a + PANEL * i for i in range(n)]
    for l in range(DEPTH):
        wc.append(panels(x["w_ada"][l], step(0, ADA)))
        pairs = [c for i in range(11) for c in (PANEL * i, D_FF + PANEL * i)]
        m = x["mix_w_in"][l]
        for f in range(2):
            if f == 1:
                w8.append(panels(m, [0, 256, 512, 1024, 1280]))
                w8.append(custom_panel([(m[:, 1536:1600], 0), (m[:, 1536:1600], 64), (m[:, 1600:1608], 128)]))
                w8.append(panels(m, [768, 2632, 2888, 1608, 1864, 3144, 3400, 2120, 2376] + step(3656, 12)))
                w8.append(panels(x["w_branch"][l], step(0, 4)))
                w8.append(panels(x["w_out"][l], step(0, 4)))
            w8.append(panels(x["ffn_w_in"][l, f], pairs))
            w11.append(down_panels(x["ffn_w_out"][l, f], KSPLIT * P))
    for l in range(DEPTH):
        wc.append(panels(x["mod_w_2"][l], step(0, MOD)))
        if l == 0:
            e = x["even_w_in_2"][0]
            w8.append(panels(e, step(0, 14)))
            w8.append(custom_panel([(e[:, 3584:3600], 0), (x["gla_a1_2"][0, 0], 32), (x["gla_a1_2"][0, 1], 64)]))
            w8.append(panels(x["even_w_out_2"][0], step(0, 4)))
        else:
            o = x["ssd_w_in_2"][0]
            w8.append(custom_panel([(o[:, 5120:5184], 0)]))
            for g in range(4):
                w8.append(panels(o, step(2048 + 512 * g, 2)))
                w8.append(custom_panel([(o[:, 4096 + P * g:4096 + P * g + P], 0), (o[:, 4608 + P * g:4608 + P * g + P], P)]))
                w8.append(panels(o, step(512 * g, 2)))
            w8.append(down_panels(x["ssd_w_out_2"][0], KD * P))
        w8.append(panels(x["ffn_w_up_2"][l], pairs))
        w11.append(down_panels(x["ffn_w_down_2"][l], KSPLIT * P))
    return np.concatenate(w8), np.concatenate(w11), np.concatenate(wc)


def vectors(x):
    c = np.zeros((P, NCOL), np.float32)
    for name, n in COL_SPEC:
        v = x[name].reshape(-1)
        if name == "ssd_d_2":
            v = v.repeat(64)
        if n == 1:
            c[:v.size, COL[name]] = v
        else:
            c[:, COL[name]:COL[name] + n] = v.reshape(n, P).T
    return c


def kernel(**inputs):
    import concourse.bacc as bacc
    from concourse.bass_utils import run_bass_kernel_spmd

    x = {k: np.asarray(v) for k, v in inputs.items()}
    arrays = {}
    arrays["w8"], arrays["w11"], arrays["wc"] = weight_stream(x)
    arrays["consts"] = constants()
    arrays["cols"] = vectors(x)
    arrays["xs"] = np.ascontiguousarray(np.concatenate([x["ctx_2"][0].T, x["x"][0].T], axis=1))
    pw = np.zeros((P, DEPTH, 2, P), np.float32)
    for g in range(4):
        r = slice(64 * (g % 2), 64 * (g % 2) + 64)
        pw[r, :, g // 2, r] = x["pool_w"][:, g].transpose(1, 0, 2)
    arrays["poolw"] = pw
    a2 = np.zeros((64, T), np.float32)
    a2[0:16], a2[32:48] = x["gla_a2_2"][0, 0], x["gla_a2_2"][0, 1]
    arrays["a2w"] = a2
    arrays["rel_bias"] = np.ascontiguousarray(x["rel_bias"][:, [0, 2, 1, 3]])
    nc = bacc.Bacc("TRN2", target_bir_lowering=False, num_devices=1)
    io = {}
    for name, a in arrays.items():
        io[name] = nc.dram_tensor(name, a.shape, mybir.dt.from_np(a.dtype), kind="ExternalInput").ap()
    io["out"] = nc.dram_tensor("out", (D, T), F32, kind="ExternalOutput").ap()
    program(nc, io)
    r = run_bass_kernel_spmd(nc, [arrays], core_ids=[0])
    return np.ascontiguousarray(r.results[0]["out"].T)[None]
```

```python
from contextlib import ExitStack

import concourse.bass as bass
from concourse import mybir
import numpy as np

F32 = mybir.dt.float32
F32R = mybir.dt.float32r
ALU = mybir.AluOpType
ACT = mybir.ActivationFunctionType
AXX = mybir.AxisListType.X

P = 128
T = 256
D = 1024
KD = D // P
DEPTH = 2
D_FF = 2816
KF = D_FF // P
PANEL = 256
KSPLIT = KF // 2
SLOTS = BANKS = 4
SLOT_W = KSPLIT * PANEL
ALPHA = (2 * DEPTH) ** 0.25
LN_EPS, RMS_EPS = 1e-5, 1e-6
KEY_MAX = 1.0 - 1e-6
TOPK = 64
IDX_SCALE = (64 ** -0.5) * (8 ** -0.5)
NEG = -3.0e38
GONE = -3.3e38
MASKED = -1.0e30
POOL_WINDOWS = (2, 4, 8, 16)
PAD = 16
NLEV = 7
GRID_ROWS, GRID_W = 4, 64
LATPAD = (GRID_ROWS + 2) * (GRID_W + 2)
CTXPAD = T + 2

COL_SPEC = [("c", 8), ("b_ada", 2 * 72), ("ln_g", 48), ("ln_b", 48), ("pool_scale", 4), ("hgrn_lb", 8),
            ("hgrn_norm_g", 8), ("c_2", 8), ("c_ctx_2", 8), ("mod_b_2", 96), ("norm_mix_g_2", 16),
            ("norm_ffn_g_2", 16), ("final_norm_g_2", 8), ("ffn_conv_w_2", 2 * 9 * 44), ("ffn_conv_b_2", 88),
            ("gla_ab_2", 4), ("ml_conv_w_2", 24), ("ml_conv_b_2", 8), ("ml_gate_b_2", 1), ("gla_norm_g_2", 4),
            ("ml_norm_g_2", 4), ("ssd_conv_w_2", 72), ("ssd_conv_b_2", 24), ("ssd_dt_bias_2", 1),
            ("ssd_a_log_2", 1), ("ssd_d_2", 16), ("ssd_norm_g_2", 16)]
COL = {}
NCOL = 0
for _name, _n in COL_SPEC:
    COL[_name] = NCOL
    NCOL += _n

CONST_SPEC = [("ident", 128), ("flip", 128), ("tree_f", NLEV * 128), ("tree_b", NLEV * 128), ("causal", 256),
              ("mneg", 4 * 256), ("tri", 256), ("invcnt", 512), ("onehot", 384), ("eps", 4)]
CST = {}
NCST = 0
for _name, _n in CONST_SPEC:
    CST[_name] = NCST
    NCST += _n


class InOrder:

    def __init__(self, eng):
        self.eng = eng
        self.wait_ge, self.drain, self.Fori = eng.wait_ge, eng.drain, eng.Fori

    def activation(self, *a, **k):
        i = self.eng.activation(*a, **k)
        self.eng.drain()
        return i

    def tensor_scalar(self, *a, **k):
        i = self.eng.tensor_scalar(*a, **k)
        self.eng.drain()
        return i

    def tensor_tensor(self, *a, **k):
        i = self.eng.tensor_tensor(*a, **k)
        self.eng.drain()
        return i

    def scalar_tensor_tensor(self, *a, **k):
        i = self.eng.scalar_tensor_tensor(*a, **k)
        self.eng.drain()
        return i

    def tensor_copy(self, *a, **k):
        i = self.eng.tensor_copy(*a, **k)
        self.eng.drain()
        return i

    def tensor_reduce(self, *a, **k):
        i = self.eng.tensor_reduce(*a, **k)
        self.eng.drain()
        return i

    def tensor_tensor_scan(self, *a, **k):
        i = self.eng.tensor_tensor_scan(*a, **k)
        self.eng.drain()
        return i

    def reciprocal(self, *a, **k):
        i = self.eng.reciprocal(*a, **k)
        self.eng.drain()
        return i

    def memset(self, *a, **k):
        i = self.eng.memset(*a, **k)
        self.eng.drain()
        return i

    def max(self, *a, **k):
        i = self.eng.max(*a, **k)
        self.eng.drain()
        return i

    def match_replace(self, *a, **k):
        i = self.eng.match_replace(*a, **k)
        self.eng.drain()
        return i


class Gemm:

    def __init__(self, name, panels, accs_per_panel=1, wide=False, panels_per_acc=1, split=False):
        self.name, self.n, self.apa, self.wide, self.ppa = name, panels, accs_per_panel, wide, panels_per_acc
        self.split = split


def plan():
    order = []
    for l in range(DEPTH):
        order += [Gemm(f"in{l}0", 22, split=True), Gemm(f"out{l}0", 8, wide=True, panels_per_acc=2, split=True),
                  Gemm(f"mix{l}", 15), Gemm(f"gate{l}", 12), Gemm(f"branch{l}", 4, 3), Gemm(f"mixout{l}", 4),
                  Gemm(f"in{l}1", 22, split=True), Gemm(f"out{l}1", 8, wide=True, panels_per_acc=2, split=True)]
    for l in range(DEPTH):
        both = 2 if l == 0 else 1
        if l == 0:
            order += [Gemm("even", 14, 2), Gemm("evengate", 1), Gemm("evenout", 4, 2)]
        else:
            order += [Gemm("dt", 1)]
            for g in range(4):
                order += [Gemm(f"ssdx{g}", 2, 2), Gemm(f"ssdbc{g}", 1, 2), Gemm(f"ssdz{g}", 2)]
            order += [Gemm("ssdout", 8, panels_per_acc=2)]
        order += [Gemm(f"up{l}", 22, both), Gemm(f"down{l}", 8, both, wide=True, panels_per_acc=2)]
    p = a = splits = 0
    row = {False: 0, True: 0}
    finished = []
    halves = 0
    for g in order:
        g.p0, g.a0, g.row0, g.s0, g.h0 = p, a, row[g.wide], splits, halves
        row[g.wide] += g.n
        for i in range(g.n):
            if g.ppa == 2 and i % 2 == 0:
                halves += 1
            last = a + g.apa * (i // g.ppa + 1) - 1
            if g.split:
                splits += 1
                finished.append(("low_made", 0, 2 * splits))
            elif g.ppa == 2 and i % 2 == 0:
                finished.append(("half_read", 0, halves))
            else:
                finished.append(("ready", last % BANKS, last // BANKS + 1))
        p += g.n
        a += g.n // g.ppa * g.apa
    return {g.name: g for g in order}, order, finished, row


ADA, MOD = 36, 24
MOD0 = DEPTH * ADA
UNITS = DEPTH * (ADA + MOD)
HEAD = 8
CARRY = {"head": (0, HEAD), "in00": (8, 11), "out00": (19, 6), "mix0": (25, 15), "in01": (40, 11), "out01": (51, 6),
         "in10": (57, 11), "out10": (68, 4), "mix1": (72, 13), "in11": (85, 11), "even": (96, MOD)}


def carried(phase, it, u):
    if phase not in CARRY:
        return []
    if phase[:2] == "in":
        units = [(it * 2 + u // 2, u // 2)] if u % 2 == 1 else []
    elif phase == "even":
        units = [(it * 8 + (2 * u + e), e) for e in range(2)]
    else:
        units = [(it * 4 + u, u % 2)]
    return [(i, e) for i, e in units if not isinstance(it, int) or i < CARRY[phase][1]]


def program(nc, io):
    G, order, finished, _ = plan()
    w8, w11, wc = io["w8"], io["w11"], io["wc"]
    with ExitStack() as ctx:
        def sb(name, shape):
            return ctx.enter_context(nc.sbuf_tensor(name, shape, F32))

        def sem(name):
            return ctx.enter_context(nc.semaphore(name))

        slots = [sb(f"panel{i}", [P, SLOT_W]) for i in range(SLOTS)]
        X = sb("residual", [P, KD, 2 * T])
        with nc.sbuf_tensor("normed_r", [P, KD, 2 * T], F32R) as H_r:
            pass
        H = sb("normed", [P, KD, 2 * T])
        cst = sb("constants", [P, NCST])
        cols = sb("vectors", [P, NCOL])
        mods1 = sb("mods1", [P, DEPTH, 72])
        mods2 = sb("mods2", [P, DEPTH, 48, 2])
        cond_slot1 = sb("cond_panel1", [P, KD, PANEL])
        gain2 = sb("gain2", [P, KD, 2])
        cond = sb("cond", [P, KD])
        cond2 = sb("cond2", [P, KD, 2])
        ones_d = sb("ones_d", [P, P])
        ones_h = sb("ones_h", [P, P])
        biasC = sb("bias_causal", [P, 4, T])
        poolw = sb("pool_blocks", [P, DEPTH, 2, P])
        relb = sb("rel_table", [32, 4])
        one_lb = sb("one_minus_lb", [P, DEPTH, 4])
        std = sb("std", [P, 2 * T])
        small = sb("small", [P, 64])
        AW = 22656
        with nc.sbuf_tensor("arena_r", [P, AW], F32R) as arena_r:
            pass
        arena = sb("arena", [P, AW])
        accs = ctx.enter_context(nc.psum_tensor("accs", [P, BANKS, 512], F32))
        acc = [accs[:, i, :] for i in range(BANKS)]
        mix = ctx.enter_context(nc.psum_tensor("mix", [P, 4, 512], F32))
        zrow_d = nc.dram_tensor("bias_rows", [4, 384], F32, kind="Internal")

        def region(off, *dims, of=arena):
            n = int(np.prod(dims))
            assert off + n <= AW, (off, n)
            v = of[:, off:off + n]
            if len(dims) == 2:
                v = v.rearrange("p (a b) -> p a b", a=dims[0])
            if len(dims) == 3:
                v = v.rearrange("p (a b c) -> p a b c", a=dims[0], b=dims[1])
            if len(dims) == 4:
                v = v.rearrange("p (a b c d) -> p a b c d", a=dims[0], b=dims[1], c=dims[2])
            return v

        def const(name, off=0, n=None):
            return cst[:, CST[name] + off:CST[name] + off + (n or dict(CONST_SPEC)[name])]

        def col(name, i, p0=0, p1=P):
            return cols[p0:p1, COL[name] + i:COL[name] + i + 1]

        ident = const("ident")
        a2w = const("onehot")[:, 0:T]
        eps_ln, eps_rms, one_col = (const("eps", i, 1) for i in range(3))
        lat = slice(T, 2 * T)
        both = slice(0, 2 * T)
        cond_slots = {False: [H[:, :, 0:T], cond_slot1[:, :, :]],
                      True: [region(14336, KD, PANEL), cond_slot1[:, :, :]]}
        cond_part = [[const("mneg", PANEL * (2 * v + i), PANEL) for i in range(2)] for v in range(2)]
        hid = region(0, KF, 2 * T)
        squares = region(0, KD, 2 * T)
        hid_hi, hid_lo = region(0, KF, T, of=arena_r), region(KF * T, KF, T, of=arena_r)
        hid_raw = region(KF * T, KF, T)
        h_hi, h_lo, h_raw = H_r[:, :, T:2 * T], region(2 * KF * T, KD, T, of=arena_r), region(2 * KF * T, KD, T)
        SPLIT = 2 * KF * T + KD * T
        up_hi = [region(SPLIT + i * KD * P, KD, P, of=arena_r) for i in range(4)]
        up_lo = [region(SPLIT + (4 + i) * KD * P, KD, P, of=arena_r) for i in range(4)]
        down_hi = [region(SPLIT + i * KSPLIT * P, KSPLIT, P, of=arena_r) for i in range(4)]
        down_lo = [region(SPLIT + (4 + i) * KSPLIT * P, KSPLIT, P, of=arena_r) for i in range(2)]
        apad = region(0, 2, PAD + T)
        qT, kT, qiT, kiT = region(544, 2, T), region(1056, 2, T), region(1568, 4, T), region(2592, T)
        vt, wi = region(2848, 2, T), region(3360, 2, 8)
        hi, qf, kk, hgs = region(3376, 2, 512), region(4400, 4, T), region(5424, 4, T), region(6448, 4, T)
        gates = region(7472, 24, T)
        ymix = region(13616, KD, T)
        TMP = 15664
        win = [region(TMP + 544 * i, 2, PAD + T) for i in range(4)]
        pdiff = region(TMP + 2176, 2, T)
        relu_s = region(TMP, 8, T)
        bias_rows = region(SPLIT + 6 * KSPLIT * P, 384)
        score, work, addm = region(TMP + 2048, T), region(TMP + 2304, T), region(TMP + 2560, T)
        logit = region(TMP + 2816, 2, 4, T)
        probT = region(TMP + 4864, 2, 8, P)
        pref, suff = region(TMP, 4 * T), region(TMP + 1024, 4 * T)
        treeX = [region(TMP + 2048 + 1024 * i, 4 * T) for i in range(2)]
        pairs, offd, ptmp = region(TMP + 4096, 8, P), region(TMP + 5120, 4, P), region(TMP + 5632, 8, P)
        osq, onorm, ostd = region(TMP + 2048, 4 * T), region(TMP, 4, T), region(TMP + 1024, 4 * T)
        merged, mtmp = region(TMP, KD, T), region(TMP + 2048, 2, T)
        E_Q, E_K, E_V, E_MQ, E_MV, E_Y, E_T = 0, 1024, 2048, 4096, 8192, 10240, 14336
        gq, gk, gv = region(E_Q, 2, 512), region(E_K, 2, 512), region(E_V, 4, 512)
        mqk, mv = region(E_MQ, 8, 512), region(E_MV, 4, 512)
        ey = region(E_Y, 8, 512)
        logd = H[:, 0:4, :].rearrange("p a t -> p (a t)").rearrange("p (d n) -> p d n", d=2)
        gpref = logd
        gsuff = H[:, 4:8, :].rearrange("p a t -> p (a t)").rearrange("p (d n) -> p d n", d=2)
        gX = [region(E_T + 1024 * i, 2, 512) for i in range(2)]
        gpairs = region(E_T + 2048, 16, P)
        goff = region(E_T + 4096, 16, P)
        gla_banks = [mix, accs]
        gcross = region(E_T + 6144, 2, 4, T)
        gtmp = region(E_T + 6144, 8, P)
        qkc = region(0, 8, 512)
        rows16 = biasC[:, 0:2, :].rearrange("p a b -> p (a b)")
        bcol = biasC[:, 2, 0:64].rearrange("p (a b) -> p a b", a=4)
        ones_g = biasC[:, 3, 0:P]
        negid16 = sb("neg_ident", [16, 16])
        bwd_rows = const("eps", 3, 1)[0:16, :]
        lsg = region(E_T + 6144, 512)[0:16, :]
        cum16 = region(E_T + 6656, 512)[0:16, :]
        tmp16 = region(E_T + 7168, 512)[0:16, :]
        rall = H
        dlog = region(E_T, 8, 512)
        psum2 = region(E_T + 4096, 4, 512)
        mprobT = region(E_T + 6144, 4, 512)
        S_X, S_BC = region(0, 4, 512), region(2048, 2, 512)
        S_XC = [region(3072, 4, 512), cond_slot1[:, :, :].rearrange("p a b -> p (a b)").rearrange("p (a b) -> p a b", a=4)]
        S_BCC = [[region(5120, 512), region(5632, 512)], [region(19200, 512), region(20224, 512)]]
        S_Z = [region(6144, 4, T), region(21376, 4, T)]
        S_XT, S_BT = region(7168, 4, 512), region(9216, 2, P)
        S_XW, S_ST = region(9472, 2, 2, 512), region(11520, 2, 512)
        S_Y = region(12544, 16, T)
        S_CB = region(16640, 2, 384)
        S_ER, S_CW = region(17408, 2, T), region(17920, 2, T)
        S_DW = region(18432, 2, 384)
        dtr = region(19200, 512)
        dcum, dwe, dtmp = region(19712, 512), region(20224, T), region(20480, 512)
        dtT, dcT, dwT = region(20992, 2, 64), region(21120, 2, 64), region(21248, 2, 64)
        S_SQ = region(9472, 4, T)
        S_STD = region(22400, T)
        negA = small[0:64, 60:61]
        upad_l = region(11264, 2, 4, LATPAD)
        upad_c = region(11264 + 8 * LATPAD, 2, 4, CTXPAD)
        uconv = region(11264 + 8 * LATPAD + 8 * CTXPAD, 2, 4, 512)

        landed = [sem(f"panel_landed{i}") for i in range(SLOTS)]
        ready = [sem(f"acc_ready{i}") for i in range(BANKS)]
        free = [sem(f"acc_free{i}") for i in range(BANKS)]
        half_read = sem("half_read")
        first_used = sem("first_half_used")
        cond_landed = [sem(f"cond_landed{i}") for i in range(2)]
        stage = sem("stage_end")
        named = {}

        def S(name):
            if name not in named:
                named[name] = sem(name)
            return named[name]


        def ffn_tap(l, it, tap, half, j, par):
            base = COL["ffn_conv_w_2"] + (l * 9 + tap) * 44 + half * 22
            return cols[:, bass.ds(it * 4 + (base + 2 * par + j), 1)]

        def ffn_bias(l, it, half, j, par):
            return cols[:, bass.ds(it * 4 + (COL["ffn_conv_b_2"] + l * 44 + half * 22 + 2 * par + j), 1)]

        def ssd_channel(g, q):
            return 4 * g + q if q < 4 else 16 + 4 * (q - 4) + g

        def cond_bank(phase):
            return 3 if phase[:2] in ("he", "in") else 2

        block = ctx.enter_context(nc.Block())

        def stage_end(eng, count):
            count[0] += 1
            eng.drain().then_inc(stage, 1)
            eng.wait_ge(stage, 3 * count[0])

        def groups(eng, g, body, peel=False):
            first = 0
            if peel or g.p0 < SLOTS:
                for u in range(4):
                    body(0, u)
                first = 1
            with eng.Fori(first, g.n // 4) as it:
                for u in range(4):
                    body(it, u)
            for u in range(g.n % 4):
                body(g.n // 4, u)

        def half_panel(g, u, j):
            k = KSPLIT if g.wide else KD
            return slots[(g.p0 + u) % SLOTS][:, 0:k * PANEL].rearrange("p (k c) -> p k c", k=k)[:, :, j * P:j * P + P]

        def split_parts(g, u, j):
            return (down_hi[(2 * u + j) % 4], down_lo[j]) if g.wide else (up_hi[(2 * u + j) % 4], up_lo[(2 * u + j) % 4])

        def split_count(g, it, u, j):
            return it * 8 + (2 * (g.s0 + u) + j + 1)

        def wait_used(eng, g, it, u, j):
            if j == 0:
                eng.wait_ge(first_used, it * 4 + (g.s0 + u + 1))
            elif g.ppa == 1:
                a = g.a0 + u
                eng.wait_ge(ready[a % BANKS], it + (a // BANKS + 1))
            elif u % 2 == 0:
                eng.wait_ge(half_read, g.h0 + u // 2 + 1)
            else:
                a = g.a0 + u // 2
                eng.wait_ge(ready[a % BANKS], a // BANKS + 1)

        def wait_ready(eng, g, it, u, r=0):
            a = g.a0 + g.apa * u + r
            eng.wait_ge(ready[a % BANKS], it * g.apa + (a // BANKS + 1))
            return a % BANKS

        @block.sync
        def _(sp):
            m0, m1 = CST["mneg"], CST["tri"]
            sp.dma_start(cst[:, 0:m0], io["consts"][:, 0:m0]).then_inc(S("loaded"), 16)
            sp.dma_start(cst[:, m1:NCST], io["consts"][:, m1:NCST]).then_inc(S("consts_loaded"), 16)
            sp.dma_start(cols[:, :], io["cols"]).then_inc(S("loaded"), 16)
            sp.dma_start(X[:, :, :], io["xs"].rearrange("(k p) t -> p k t", p=P)).then_inc(S("loaded"), 16)
            sp.dma_start(poolw[:, :, :, :], io["poolw"]).then_inc(S("loaded"), 16)
            sp.dma_start(relb[:, :], io["rel_bias"]).then_inc(S("loaded"), 16)
            sp.wait_ge(S("consts_loaded"), 16)
            sp.dma_start(a2w[32:96, :], io["a2w"]).then_inc(S("loaded"), 16)

            def load(g, i, static_i):
                src = (w11 if g.wide else w8)[bass.ds(i + g.row0, 1), :, :].rearrange("a p n -> p (a n)")
                s = (g.p0 + static_i) % SLOTS
                width = SLOT_W if g.wide else KD * PANEL
                sp.dma_start(slots[s][:, 0:width], src).then_inc(landed[s], 16)

            def load_static(g, i):
                p = g.p0 + i
                if p >= SLOTS:
                    kind, b, v = finished[p - SLOTS]
                    sp.wait_ge({"half_read": half_read, "low_made": S("low_made")}.get(kind, ready[b]), v)
                load(g, i, i)

            def load_cond(phase, it, u):
                for i, e in carried(phase, it, u):
                    n0 = CARRY[phase][0]
                    slot = (n0 + e) % 2
                    if not isinstance(i, int) or i + n0 >= 2:
                        sp.wait_ge(S("cond_part"), i + (n0 - 1))
                    if phase == "even" and isinstance(i, int) and i == 0:
                        sp.wait_ge(S("rms_std"), 1)
                    src = wc[bass.ds(i + n0, 1), :, :].rearrange("a p (k c) -> p (a k) c", k=KD)
                    sp.dma_start(cond_slots[phase == "even"][slot], src).then_inc(cond_landed[slot], 16)

            for i in range(HEAD):
                load_cond("head", 0, i)
            for g in order:
                if g.n >= 12 and g.ppa == 1:
                    for i in range(4):
                        load_static(g, i)
                        load_cond(g.name, 0, i)
                    with sp.Fori(1, g.n // 4) as it:
                        for u in range(4):
                            a = g.a0 + g.apa * (u + 1) - 1
                            if g.split:
                                sp.wait_ge(S("low_made"), split_count(g, it, u - SLOTS, 1))
                            else:
                                sp.wait_ge(ready[a % BANKS], it * g.apa + (a // BANKS + 1 - g.apa))
                            load(g, it * 4 + u, u)
                            load_cond(g.name, it, u)
                    for i in range(g.n - g.n % 4, g.n):
                        load_static(g, i)
                        load_cond(g.name, 0, i)
                else:
                    for i in range(g.n):
                        load_static(g, i)
                        load_cond(g.name, 0, i)
                if g.name == "even":
                    sp.wait_ge(S("cond_summed"), UNITS)
                    sp.dma_start(const("mneg"), io["consts"][:, m0:m1]).then_inc(S("masks_loaded"), 16)
                if g.name == "in00":
                    sp.wait_ge(S("bias_rows"), 1)
                    sp.dma_start(zrow_d.ap(), bias_rows[0:4, :]).then_inc(S("bias_stored"), 16)
                    sp.wait_ge(S("bias_stored"), 16)
                    sp.dma_start(biasC[:, :, :],
                                 bass.AP(zrow_d, 0, [[1, P], [384, 4], [1, T]])).then_inc(S("hankel"), 16)
            sp.wait_ge(S("final"), 1)
            sp.dma_start(io["out"].rearrange("(k p) t -> p k t", p=P), H[:, :, lat]).then_inc(S("stored"), 16)
            sp.wait_ge(S("stored"), 16)

        @block.tensor
        def _(pe):
            count = [0]

            def panel_in(g, it, u):
                s = (g.p0 + u) % SLOTS
                pe.wait_ge(landed[s], it * 16 + 16 * ((g.p0 + u) // SLOTS + 1))
                return slots[s]

            def acc_open(g, it, u, r=0):
                a = g.a0 + g.apa * u + r
                if a >= BANKS or not isinstance(it, int) or it > 0:
                    pe.wait_ge(free[a % BANKS], it * g.apa + a // BANKS)
                return a % BANKS

            def features(g, it, u, rhs, ntok):
                w = panel_in(g, it, u)
                for j in range(2):
                    r = j if ntok == 512 else 0
                    if j == 0 or ntok == 512:
                        b = acc_open(g, it, u, r)
                    o = 0 if ntok == 512 else j * ntok
                    for k in range(KD):
                        mm = pe.matmul(acc[b][:, o:o + ntok], w[:, k * PANEL + j * P:k * PANEL + j * P + P], rhs(k),
                                       start=(k == 0), stop=(k == KD - 1))
                    if j == 1 or ntok == 512:
                        mm.then_inc(ready[b], 1)

            def split_half(g, it, u, j, out, src_hi, src_lo, clear, last, done):
                pe.wait_ge(S("low_made"), split_count(g, it, u, j))
                hi, lo = split_parts(g, u, j)
                n = hi.shape[1]
                for k in range(n):
                    pe.matmul(out, hi[:, k, :], src_hi(k), start=clear and k == 0, stop=False, skip_group_check=True)
                    pe.matmul(out, hi[:, k, :], src_lo(k), start=False, stop=False, skip_group_check=True)
                    mm = pe.matmul(out, lo[:, k, :], src_hi(k), start=False, stop=last and k == n - 1, skip_group_check=True)
                mm.then_inc(done, 1)

            def split_up(g, it, u):
                b = acc_open(g, it, u)
                for j in range(2):
                    split_half(g, it, u, j, acc[b][:, j * T:j * T + T], lambda k: h_hi[:, k, :], lambda k: h_lo[:, k, :],
                               j == 0, True, (first_used, ready[b])[j])

            def split_down(g):
                for i in range(g.n):
                    a, part = g.a0 + i // 2, i % 2
                    b = a % BANKS
                    if part == 0:
                        pe.wait_ge(free[b], a // BANKS)
                    for j in range(2):
                        split_half(g, 0, i, j, acc[b][:, j * T:j * T + T],
                                   lambda k: hid_hi[:, part * KSPLIT + k, :], lambda k: hid_lo[:, part * KSPLIT + k, :],
                                   part == 0 and j == 0, part == 1, (first_used, ready[b] if part else half_read)[j])
                    cond_sum(g.name, 0, i)

            def tokens(g, u, lo, nblk, ncol=PANEL, off=0):
                w = panel_in(g, 0, u)
                for tb in range(nblk):
                    if tb % 2 == 0:
                        b = acc_open(g, 0, u, tb // 2)
                    for k in range(KD):
                        mm = pe.matmul(acc[b][:, tb % 2 * T:tb % 2 * T + ncol], H[:, k, lo + tb * P:lo + tb * P + P],
                                       w[:, k * PANEL + off:k * PANEL + off + ncol], start=(k == 0), stop=(k == KD - 1))
                    if tb % 2 == 1:
                        mm.then_inc(ready[b], 1)

            def cond_sum(phase, it, u):
                for i, e in carried(phase, it, u):
                    n0 = CARRY[phase][0]
                    pe.wait_ge(S("cond_part"), i + (n0 + 1))
                    for v in range(2 if n0 >= MOD0 else 1):
                        for j in range(2):
                            c = i * 2 + (T * v + j)
                            mm = pe.matmul(mix[:, cond_bank(phase), bass.ds(c, 1) if not isinstance(c, int) else slice(c, c + 1)],
                                           cond_part[v][(n0 + e) % 2][:, j * P:j * P + P], one_col, start=True, stop=True)
                    mm.then_inc(S("cond_summed"), 1)

            def down(g, src, ntok, kper=KSPLIT):
                for n in range(g.n // 2):
                    for part in range(2):
                        i = 2 * n + part
                        w = panel_in(g, 0, i)
                        for j in range(2):
                            a = g.a0 + g.apa * n + (j if ntok == 512 else 0)
                            if part == 0 and (j == 0 or ntok == 512) and a >= BANKS:
                                pe.wait_ge(free[a % BANKS], a // BANKS)
                            o = 0 if ntok == 512 else j * ntok
                            for k in range(kper):
                                first = part == 0 and k == 0 and (j == 0 or ntok == 512)
                                mm = pe.matmul(acc[a % BANKS][:, o:o + ntok],
                                               w[:, k * PANEL + j * P:k * PANEL + j * P + P],
                                               src(part * kper + k), start=first, stop=(part == 1 and k == kper - 1),
                                               skip_group_check=True)
                            if part == 1 and (j == 1 or ntok == 512):
                                mm.then_inc(ready[a % BANKS], 1)
                        if part == 0:
                            mm.then_inc(half_read, 1)

            def layer_norm(n, g):
                for i in range(4):
                    a = g.a0 + i
                    pe.wait_ge(free[a % BANKS], a // BANKS + 1)
                    for j in range(2):
                        k = 2 * i + j
                        mm = pe.matmul(mix[:, 0, 0:T], ones_d[:, :], X[:, k, lat], start=(k == 0), stop=(k == KD - 1))
                mm.then_inc(S("mean_ready"), 1)
                for k in range(KD):
                    pe.wait_ge(S("squared"), n * KD + k + 1)
                    mm = pe.matmul(mix[:, 1, 0:T], ones_d[:, :], squares[:, k, 0:T], start=(k == 0), stop=(k == KD - 1))
                mm.then_inc(S("var_ready"), 1)

            def rms_norm(n, sel):
                for k in range(KD):
                    pe.wait_ge(S("rms_sq"), n * KD + k + 1)
                    mm = pe.matmul(mix[:, 0, 0:sel.stop - sel.start], ones_d[:, :], squares[:, k, 0:sel.stop - sel.start],
                                   start=(k == 0), stop=(k == KD - 1))
                mm.then_inc(S("rms_ready"), 1)

            def gate(l, *panels):
                for u in panels:
                    features(G[f"gate{l}"], 0, u, lambda k: H[:, k, lat], T)

            def pool(l):
                gate(l, 0, 1)
                pe.wait_ge(S("pool_diff"), l + 1)
                for c in range(2):
                    mm = pe.matmul(mix[:, 0, c * T:c * T + T], poolw[:, l, c, :], pdiff[:, c, :], start=True, stop=True)
                mm.then_inc(S("pool_mm"), 1)

            def attention(l):
                for qb in range(2):
                    n = P * (qb + 1)
                    for b in range(4):
                        if qb == 1:
                            pe.wait_ge(S("idx_relu"), 8 * l + b + 1)
                        for i in range(2):
                            r = slice(64 * (b // 2), 64 * (b // 2) + 64)
                            mm = pe.matmul(mix[:, b, i * T:i * T + n], qiT[r, 2 * (b % 2) + i, qb * P:qb * P + P], kiT[r, 0:n],
                                           start=True, stop=True)
                        mm.then_inc(S("idx_mm"), 1)
                for qb in range(2):
                    n = P * (qb + 1)
                    pe.wait_ge(S("idx_relu"), 8 * l + 4 + 2 * qb + 2)
                    for h in range(4):
                        r = slice(64 * (h % 2), 64 * (h % 2) + 64)
                        mm = pe.matmul(mix[:, 2 * qb + h % 2, h // 2 * T:h // 2 * T + n],
                                       qT[r, h // 2, qb * P:qb * P + P], kT[r, h // 2, 0:n], start=True, stop=True)
                    mm.then_inc(S("logit_mm"), 1)
                gate(l, 2, 3, 4, 5)
                for qb in range(2):
                    pe.wait_ge(S("prob_ready"), 2 * l + qb + 1)
                    for h in range(4):
                        for s in range(qb + 1):
                            i = h * (qb + 1) + s
                            mm = pe.transpose(mix[:, 2 * qb + i // 4, i % 4 * P:i % 4 * P + P],
                                              logit[:, qb, h, s * P:s * P + P], ident)
                    mm.then_inc(S("probT_mm"), 1)
                for qb in range(2):
                    pe.wait_ge(S("probT_ready"), 2 * l + qb + 1)
                    for i in range(4):
                        h = 2 * (i % 2) + i // 2
                        for s in range(qb + 1):
                            mm = pe.matmul(mix[64 * (h % 2):64 * (h % 2) + 64, 1, h // 2 * T + qb * P:h // 2 * T + qb * P + P],
                                           vt[:, s, h * 64:h * 64 + 64], probT[:, qb, i * (qb + 1) + s, :],
                                           start=(s == 0), stop=(s == qb))
                mm.then_inc(S("attn_mm"), 1)

            def hgrn(l):
                k4, q4 = kk, qf
                for i in range(9):
                    bank = 2 * (i % 2)
                    if i == 0:
                        pe.wait_ge(S("hg_key"), l + 1)
                    else:
                        pe.wait_ge(S("hg_x"), 8 * l + i)
                    if i >= 2:
                        pe.wait_ge(S("hg_acc"), 9 * l + i - 1)
                    xt = treeX[(i - 1) % 2].rearrange("p (h t) -> p h t", h=4)
                    if i < 8:
                        for b in range(2):
                            for h in range(4):
                                c = slice(b * P, b * P + P)
                                lhs, rhs = (k4[:, h, c], q4[:, h, c]) if i == 0 else (xt[:, h, c], xt[:, h, c])
                                mm = pe.matmul(mix[:, bank + b, h * P:h * P + P], lhs, rhs, start=True, stop=True)
                    else:
                        for h in range(4):
                            mm = pe.matmul(mix[:, bank, h * P:h * P + P], xt[:, h, 0:P], xt[:, h, P:T], start=True, stop=True)
                    mm.then_inc(S("hg_mm"), 1)
                    if i < 6:
                        gate(l, 6 + i)
                pe.wait_ge(S("hg_acc"), 9 * l + 9)
                for h in range(4):
                    v = slice(h * P, h * P + P)
                    o = lambda t: mix[:, 2 + h // 2, h % 2 * T + t * P:h % 2 * T + t * P + P]
                    pe.matmul(o(0), hi[:, 0, v], pairs[:, h, :], start=True, stop=True)
                    pe.matmul(o(1), hi[:, 0, v], offd[:, h, :], start=True, stop=False)
                    mm = pe.matmul(o(1), hi[:, 1, v], pairs[:, 4 + h, :], start=False, stop=True)
                mm.then_inc(S("hg_o"), 1)
                pe.wait_ge(S("hg_sq"), l + 1)
                for i in range(2):
                    mm = pe.matmul(mix[:, i, :], ones_h[:, :], osq[:, i * 512:i * 512 + 512], start=True, stop=True)
                mm.then_inc(S("hg_ms"), 1)

            def even_tail(l):
                g = G["evengate"]
                w = panel_in(g, 0, 0)
                b = acc_open(g, 0, 0)
                for k in range(KD):
                    mm = pe.matmul(acc[b][0:96, :], w[:, k * PANEL:k * PANEL + 96], H[:, k, :], start=(k == 0), stop=(k == KD - 1))
                mm.then_inc(ready[b], 1)

            def gla():
                pe.wait_ge(S("rank_ready"), 1)
                for d in range(2):
                    r = slice(32 + 32 * d, 48 + 32 * d)
                    for c in range(2):
                        mm = pe.matmul(mix[:, 2 * d + c, :], a2w[r, c * P:c * P + P], rows16[r, :], start=True, stop=True)
                    mm.then_inc(S("decay_mm"), 1)
                def heads(out, lhs, rhs, cs, ct, bank0, at):
                    for h in range(4):
                        r = slice(64 * (h % 2), 64 * (h % 2) + 64)
                        o = (2 * at + h // 2) * P
                        m = pe.matmul(out[:, bank0 + h % 2, o:o + P], lhs[r, h // 2, cs * P:cs * P + P],
                                      rhs[r, h // 2, ct * P:ct * P + P], start=True, stop=True)
                    return m

                pe.wait_ge(S("decay_read"), 2)
                for hf in range(2):
                    for b in range(2):
                        mm = heads(mix, gk, gq, 2 * hf + b, 2 * hf + b, 2 * hf, b)
                    mm.then_inc(S("gla_mm"), 1)
                for n in range(16):
                    lv, d = n // 2, n % 2
                    out, xt = gla_banks[d], gX[d]
                    pe.wait_ge(S("gla_x"), n + 1)
                    if lv < 7:
                        for hf in range(2):
                            before = 2 + 2 * (n - 2) + hf if lv else hf if d == 0 else None
                            if before is not None:
                                pe.wait_ge(S("gla_acc"), before + 1)
                            for b in range(2):
                                mm = heads(out, xt, xt, 2 * hf + b, 2 * hf + b, 2 * hf, b)
                            mm.then_inc(S("gla_mm"), 1)
                    else:
                        pe.wait_ge(S("gla_acc"), 2 + 2 * (n - 2) + 1)
                        for st in range(2):
                            s_, t_ = (0, 1) if d == 0 else (1, 0)
                            mm = heads(out, xt, xt, 2 * st + s_, 2 * st + t_, 0, st)
                        mm.then_inc(S("gla_mm"), 1)
                pe.wait_ge(S("gla_x"), 18)
                pe.wait_ge(S("gla_acc"), 32)
                for h in range(4):
                    r = slice(64 * (h % 2), 64 * (h % 2) + 64)
                    for s in range(2):
                        for d in range(2):
                            mm = pe.matmul(mix[:, h, s * T:s * T + T], gX[d][r, h // 2, s * P:s * P + P],
                                           gX[d][r, h // 2, T:2 * T], start=(d == 0), stop=(d == 1))
                mm.then_inc(S("gla_mm"), 1)
                pe.wait_ge(S("gla_acc"), 33)
                for h in range(4):
                    for t in range(4):
                        o = mix[:, h, t * P:t * P + P]
                        st, tb = t // 2, t % 2
                        terms = [(2 * st + tb, gpairs[:, 8 * st + 4 * (h % 2) + 2 * tb + h // 2, :]),
                                 (2 * st + 1 - tb, goff[:, 8 * (1 - tb) + 4 * (h % 2) + 2 * st + h // 2, :])]
                        if st == 1:
                            terms += [(s, gcross[:, s, h, tb * P:tb * P + P]) for s in range(2)]
                        for i, (s, rhs) in enumerate(terms):
                            mm = pe.matmul(o, gv[:, s, h * P:h * P + P], rhs, start=(i == 0), stop=(i == len(terms) - 1))
                mm.then_inc(S("gla_o"), 1)
                head_norm(0)

            def head_norm(n):
                pe.wait_ge(S("head_sq"), n + 1)
                for h in range(4):
                    mm = pe.matmul(mix[:, h, :], ones_h[:, :], head_squares[n][:, h, :], start=True, stop=True)
                mm.then_inc(S("head_ms"), 1)

            head_squares = [region(E_T, 4, 512), region(E_T, 4, 512)]

            def mlstm():
                pe.wait_ge(S("ml_rows"), 1)
                for t in range(4):
                    mm = pe.transpose(mix[:, 0, t * 16:t * 16 + 16], cum16[:, t * P:t * P + P], ident[0:16, 0:16])
                mm.then_inc(S("ml_cols"), 1)
                for i in range(8):
                    h, d = i % 4, i // 4
                    if i >= 3:
                        pe.wait_ge(S("ml_rall"), i - 2)
                    li, lf = 8 * d + h, 8 * d + 4 + h
                    o = mix[:, 1 + i % 3, :]
                    pe.matmul(o, ident[0:16, li:li + 1].to_broadcast([16, P]), rows16[0:16, :], start=True, stop=False)
                    mm = pe.matmul(o, negid16[:, lf:lf + 1].to_broadcast([16, P]), cum16[:, :], start=False, stop=True)
                    mm.then_inc(S("ml_sel"), 1)
                pe.wait_ge(S("ml_qk"), 1)
                pe.wait_ge(S("ml_rall"), 8)
                for t in range(4):
                    w = T if t < 2 else 2 * T
                    if t >= 1:
                        pe.wait_ge(S("ml_h"), t)
                    for h in range(4):
                        mm = pe.matmul(mix[:, h, 0:w], qkc[:, h, t * P:t * P + P], qkc[:, 4 + h, 0:w], start=True, stop=True)
                    mm.then_inc(S("ml_scores"), 1)
                    pe.wait_ge(S("ml_prob"), t + 1)
                    for h in range(4):
                        for s in range(w // P):
                            mm = pe.transpose(mix[:, h, s * P:s * P + P], psum2[:, h, s * P:s * P + P], ident)
                    mm.then_inc(S("ml_probT"), 1)
                    pe.wait_ge(S("ml_probT_sb"), t + 1)
                    for h in range(4):
                        for s in range(w // P):
                            mm = pe.matmul(mix[:, h, 0:P], mv[:, s, h * P:h * P + P], mprobT[:, h, s * P:s * P + P],
                                           start=(s == 0), stop=(s == w // P - 1))
                    mm.then_inc(S("ml_hmm"), 1)
                head_norm(1)

            def ssd_rates():
                pe.wait_ge(S("dt_rows"), 1)
                for i in range(2):
                    pe.transpose(mix[:, 0, i * 64:i * 64 + 64], dtr[0:64, T + i * P:T + i * P + P], ident[0:64, 0:64])
                    pe.transpose(mix[:, 0, 128 + i * 64:192 + i * 64], dcum[0:64, T + i * P:T + i * P + P], ident[0:64, 0:64])
                    mm = pe.transpose(mix[:, 0, 256 + i * 64:320 + i * 64], dwe[0:64, i * P:i * P + P], ident[0:64, 0:64])
                mm.then_inc(S("dt_cols"), 1)

            def ssd_features(g, q):
                if q >= 6:
                    features(G[f"ssdz{g}"], 0, q - 6, lambda k: H[:, k, lat], T)
                    return
                p, u, j = G[f"ssdx{g}" if q < 4 else f"ssdbc{g}"], q // 2 % 2, q % 2
                w = panel_in(p, 0, u)
                b = acc_open(p, 0, u, j)
                for k in range(KD):
                    mm = pe.matmul(acc[b][:, :], w[:, k * PANEL + j * P:k * PANEL + j * P + P], H[:, k, :], start=(k == 0), stop=(k == KD - 1))
                mm.then_inc(ready[b], 1)

            def ssd_group(g):
                xc, (bc_, cc) = S_XC[g % 2], S_BCC[g % 2]
                pe.wait_ge(S("ssd_conv"), g + 1)
                for s in (1, 2, 3, 0):
                    if g >= 1 and s == 2:
                        pe.wait_ge(S("ssd_yz"), g)
                    if g >= 1 and s == 0:
                        pe.wait_ge(S("ssd_gstd"), g)
                    for c in range(4):
                        mm = pe.transpose(mix[:, s, c * P:c * P + P], xc[:, c, s * P:s * P + P], ident)
                mm.then_inc(S("ssd_xT"), 1)
                if g < 3:
                    ssd_features(g + 1, 0)
                pe.wait_ge(S("ssd_xT_sb"), g + 1)
                for s in range(2):
                    pe.transpose(mix[:, 0, s * P:s * P + P], bc_[:, s * P:s * P + P], ident)
                for s in range(2):
                    mm = pe.matmul(mix[:, 1, s * T:s * T + T], bc_[:, T + s * P:T + s * P + P], cc[:, lat],
                                   start=True, stop=True)
                mm.then_inc(S("ssd_cb"), 1)
                if g < 3:
                    ssd_features(g + 1, 1)
                pe.wait_ge(S("ssd_cb_sb"), g + 1)
                pe.wait_ge(S("ssd_xw"), g + 1)
                for d in range(2):
                    for s in range(2):
                        mm = pe.matmul(mix[:, 2 + d, :], S_BT[:, s, :], S_XW[:, d, s, :], start=(s == 0), stop=(s == 1))
                mm.then_inc(S("ssd_state"), 1)
                pe.wait_ge(S("ssd_state_sb"), g + 1)
                for i in range(16):
                    pr, hh, d = i // 4, i // 2 % 2, i % 2
                    n = 16 * g + i
                    h = 2 * pr + hh
                    row = 32 * d + 8 * g + h
                    if n >= 2:
                        pe.wait_ge(S("ssd_dmin"), n - 1)
                    pe.matmul(mix[:, i % 2, 0:T], ident[0:64, row:row + 1].to_broadcast([64, P]), dcum[0:64, lat],
                              start=True, stop=True).then_inc(S("ssd_row"), 1)
                    if i >= 1:
                        ssd_out(g, i - 1, n - 1)
                    if i % 2 == 1 and i < 12 and g < 3:
                        ssd_features(g + 1, 2 + i // 2)
                ssd_out(g, 15, 16 * g + 15)
                pe.wait_ge(S("ssd_gsq"), g + 1)
                for c in range(4):
                    mm = pe.matmul(mix[:, 0, 0:T], ones_g[:, :], S_SQ[:, c, :], start=(c == 0), stop=(c == 3))
                mm.then_inc(S("ssd_gms"), 1)

            def ssd_out(g, i, n):
                pr, hh, d = i // 4, i // 2 % 2, i % 2
                h = 2 * pr + hh
                r = slice(64 * hh, 64 * hh + 64)
                v = slice(h * 64, h * 64 + 64)
                y = mix[:, 2 + pr % 2, :]
                first, last = i % 2 == 0, i % 2 == 1
                if i % 4 == 0 and i >= 8:
                    pe.wait_ge(S("ssd_y"), 4 * g + pr - 1)
                pe.wait_ge(S("ssd_w"), n + 1)
                w = S_DW[:, n % 2, :]
                pe.matmul(y[r, 0:T], S_ST[:, d, v], S_CW[:, n % 2, :], start=first, stop=False, skip_group_check=True)
                if d == 0:
                    pe.matmul(y[r, 0:T], S_XT[:, 2, v], w[:, 0:T], start=False, stop=False, skip_group_check=True)
                    mm = pe.matmul(y[r, P:T], S_XT[:, 3, v], w[:, T:T + P], start=False, stop=last, skip_group_check=True)
                else:
                    pe.matmul(y[r, 0:T], S_XT[:, 3, v], w[:, P:P + T], start=False, stop=False, skip_group_check=True)
                    mm = pe.matmul(y[r, 0:P], S_XT[:, 2, v], w[:, 0:P], start=False, stop=last, skip_group_check=True)
                mm.then_inc(S("ssd_ymm"), 1)

            pe.wait_ge(S("loaded"), 96)
            pe.matmul(mix[0:4, 0, 0:384], relb[:, :], const("onehot")[0:32, :], start=True, stop=True).then_inc(S("bias_mm"), 1)
            for i in range(HEAD):
                cond_sum("head", 0, i)
            stage_end(pe, count)
            norms = 0
            for l in range(DEPTH):
                for f in range(2):
                    if f == 1:
                        if l == 0:
                            pe.wait_ge(S("hankel"), 16)
                            for i in range(2):
                                mm = pe.matmul(mix[:, i, :], const("flip"), biasC[:, 2 * i:2 * i + 2, :], start=True, stop=True)
                            mm.then_inc(S("bias_flip"), 1)
                        pe.wait_ge(S("h_ready"), 3 * l + 2)
                        g = G[f"mix{l}"]
                        rhs = lambda k: H[:, k, lat]
                        for u in range(15):
                            if u == 5:
                                w = panel_in(g, 0, u)
                                b = acc_open(g, 0, u)
                                for k in range(KD):
                                    pe.matmul(acc[b][:, 0:T], w[:, k * PANEL:k * PANEL + P], rhs(k), start=(k == 0), stop=(k == KD - 1))
                                for tb in range(2):
                                    for k in range(KD):
                                        mm = pe.matmul(acc[b][:, T + 8 * tb:T + 8 * tb + 8], H[:, k, T + tb * P:T + tb * P + P],
                                                       w[:, k * PANEL + P:k * PANEL + P + 8], start=(k == 0), stop=(k == KD - 1))
                                mm.then_inc(ready[b], 1)
                            elif u in (6, 7, 8):
                                tokens(g, u, T, 2)
                            else:
                                features(g, 0, u, rhs, T)
                            cond_sum(f"mix{l}", 0, u)
                        stage_end(pe, count)
                        pool(l)
                        stage_end(pe, count)
                        attention(l)
                        stage_end(pe, count)
                        hgrn(l)
                        stage_end(pe, count)
                        g = G[f"branch{l}"]
                        for u in range(4):
                            w = panel_in(g, 0, u)
                            for r, ks in enumerate((range(0, 2), range(2, 4), range(4, 8))):
                                b = acc_open(g, 0, u, r)
                                for j in range(2):
                                    for k in ks:
                                        mm = pe.matmul(acc[b][:, j * T:j * T + T], w[:, k * PANEL + j * P:k * PANEL + j * P + P],
                                                       ymix[:, k, :], start=(k == ks[0]), stop=(k == ks[-1]))
                                mm.then_inc(ready[b], 1)
                        stage_end(pe, count)
                        g = G[f"mixout{l}"]
                        for u in range(4):
                            features(g, 0, u, lambda k: merged[:, k, :], T)
                        layer_norm(norms, g)
                        norms += 1
                        stage_end(pe, count)
                    pe.wait_ge(S("h_ready"), 3 * l + 1 + 2 * f)

                    def up_panel(it, u, name=f"in{l}{f}"):
                        split_up(G[name], it, u)
                        cond_sum(name, it, u)

                    groups(pe, G[f"in{l}{f}"], up_panel)
                    pe.wait_ge(S("hid_ready"), 2 * l + f + 1)
                    split_down(G[f"out{l}{f}"])
                    layer_norm(norms, G[f"out{l}{f}"])
                    norms += 1
                    stage_end(pe, count)
            rms = 0
            for l in range(DEPTH):
                rms_norm(rms, both)
                rms += 1
                stage_end(pe, count)
                if l == 0:
                    for u in range(14):
                        if u in (2, 3, 10, 11):
                            tokens(G["even"], u, 0, 4)
                        else:
                            features(G["even"], 0, u, lambda k: H[:, k, :], 512)
                        cond_sum("even", 0, u)
                    even_tail(l)
                    stage_end(pe, count)
                    gla()
                    stage_end(pe, count)
                    mlstm()
                    stage_end(pe, count)
                    for u in range(4):
                        features(G["evenout"], 0, u, lambda k: ey[:, k, :], 512)
                else:
                    g = G["dt"]
                    w = panel_in(g, 0, 0)
                    b = acc_open(g, 0, 0)
                    for k in range(KD):
                        mm = pe.matmul(acc[b][0:64, :], w[:, k * PANEL:k * PANEL + 64], H[:, k, :], start=(k == 0), stop=(k == KD - 1))
                    mm.then_inc(ready[b], 1)
                    ssd_rates()
                    stage_end(pe, count)
                    for q in range(8):
                        ssd_features(0, q)
                    for g in range(4):
                        ssd_group(g)
                    stage_end(pe, count)
                    down(G["ssdout"], lambda k: S_Y[:, k, :], T, KD)
                stage_end(pe, count)
                sel = both if l == 0 else lat
                rms_norm(rms, sel)
                rms += 1
                stage_end(pe, count)
                ntok = 512 if l == 0 else T
                groups(pe, G[f"up{l}"], lambda it, u, g=G[f"up{l}"]: features(g, it, u, lambda k: H[:, k, sel], ntok))
                pe.wait_ge(S("ffn_hid"), l + 1)
                down(G[f"down{l}"], lambda k: hid[:, k, 0:ntok], ntok)
                stage_end(pe, count)
            rms_norm(rms, lat)

        @block.gpsimd
        def _(pool):
            def low(g, it, u):
                for j in range(2):
                    pool.wait_ge(S("high_made"), split_count(g, it, u, j))
                    if g.wide and u >= 1:
                        wait_used(pool, g, it, u - 1, j)
                    hi, lo = split_parts(g, u, j)
                    pool.tensor_tensor(lo, half_panel(g, u, j), hi, ALU.subtract)
                    pool.drain().then_inc(S("low_made"), 1)

            for l in range(DEPTH):
                for f in range(2):
                    groups(pool, G[f"in{l}{f}"], lambda it, u, g=G[f"in{l}{f}"]: low(g, it, u))
                    for i in range(8):
                        low(G[f"out{l}{f}"], 0, i)

        @block.scalar
        def _(act):
            act = InOrder(act)
            count = [0]

            def evac(g, it, u, r, dst, src_cols, func, scale=1.0):
                b = wait_ready(act, g, it, u, r)
                src = acc[b][:, src_cols]
                if len(dst.shape) == 3:
                    src = src.rearrange("p (a b) -> p a b", a=dst.shape[1])
                act.activation(dst, src, func, scale=scale).then_inc(free[b], 1)

            def high(g, it, u):
                s = (g.p0 + u) % SLOTS
                act.wait_ge(landed[s], it * 16 + 16 * ((g.p0 + u) // SLOTS + 1))
                for j in range(2):
                    if not isinstance(it, int) or 4 * it + u >= 2:
                        wait_used(act, g, it, u - 2, j)
                    act.eng.activation(split_parts(g, u, j)[0], half_panel(g, u, j), ACT.Copy)
                    act.drain().then_inc(S("high_made"), 1)

            def layer_norm(n, l, j):
                for k in range(KD):
                    act.wait_ge(S("centred"), n * KD + k + 1)
                    act.activation(squares[:, k, 0:T], X[:, k, lat], ACT.Square).then_inc(S("squared"), 1)
                act.wait_ge(S("var_ready"), n + 1)
                act.activation(std[:, 0:T], mix[:, 1, 0:T], ACT.Sqrt, bias=eps_ln).then_inc(S("std_ready"), 1)
                for k in range(KD):
                    act.wait_ge(S("scaled"), n * KD + k + 1)
                    c = (3 * l + j) * KD + k
                    act.activation(X[:, k, lat], X[:, k, lat], ACT.Identity, scale=col("ln_g", c), bias=col("ln_b", c))\
                       .then_inc(S("x_ready"), 1)

            def rms_norm(n, sel):
                w = sel.stop - sel.start
                for k in range(KD):
                    act.activation(squares[:, k, 0:w], X[:, k, sel], ACT.Square).then_inc(S("rms_sq"), 1)
                act.wait_ge(S("rms_ready"), n + 1)
                act.activation(std[:, 0:w], mix[:, 0, 0:w], ACT.Sqrt, bias=eps_rms).then_inc(S("rms_std"), 1)

            def gate(l, *panels):
                for u in panels:
                    evac(G[f"gate{l}"], 0, u, 0, gates[:, 2 * u:2 * u + 2, :], both, ACT.Copy)

            def pool(l):
                gate(l, 0, 1)
                act.wait_ge(S("pool_mm"), l + 1)
                for c in range(2):
                    act.activation(ymix[:, c, :], mix[:, 0, c * T:c * T + T], ACT.Identity, scale=col("pool_scale", 2 * l + c))

            def attention(l):
                for qb in range(2):
                    n = P * (qb + 1)
                    for pr in range(4):
                        act.wait_ge(S("idx_mm"), 8 * l + 4 * qb + pr + 1)
                        if qb == 1 and pr == 0:
                            act.wait_ge(S("idx_sum"), 2 * l + 1)
                        act.activation(relu_s[:, 2 * pr:2 * pr + 2, 0:n],
                                       mix[:, pr, :].rearrange("p (a t) -> p a t", a=2)[:, :, 0:n], ACT.Relu)\
                           .then_inc(S("idx_relu"), 1)
                for qb in range(2):
                    n = P * (qb + 1)
                    gate(l, 2 + 2 * qb, 3 + 2 * qb)
                    act.wait_ge(S("logit_ready"), 2 * l + qb + 1)
                    for h in range(4):
                        e = act.activation(logit[:, qb, h, 0:n], logit[:, qb, h, 0:n], ACT.Exp,
                                           bias=small[:, 8 * qb + h:8 * qb + h + 1],
                                           accum_out=small[:, 8 * qb + 4 + h:8 * qb + 5 + h])
                    act.drain().then_inc(S("exp_ready"), 1)
                for qb in range(2):
                    act.wait_ge(S("probT_mm"), 2 * l + qb + 1)
                    m = 4 * (qb + 1)
                    act.activation(probT[:, qb, 0:m, :].rearrange("p a b -> p (a b)"),
                                   mix[:, 2 * qb:2 * qb + qb + 1, :].rearrange("p a b -> p (a b)"), ACT.Copy)\
                       .then_inc(S("probT_ready"), 1)
                act.wait_ge(S("attn_mm"), l + 1)
                act.activation(ymix[:, 2:4, :].rearrange("p a b -> p (a b)"), mix[:, 1, :], ACT.Copy)

            def halves(v, m):
                return v.rearrange("p (n two m) -> p n two m", two=2, m=m)

            def hgrn(l):
                act.wait_ge(S("hg_key"), l + 1)
                act.activation(pref, pref, ACT.Ln, bias=one_col)
                act.drain()
                for lv in range(8):
                    m = 1 << lv
                    if lv >= 1:
                        act.wait_ge(S("hg_sums"), 7 * l + lv)
                    else:
                        act.wait_ge(S("hg_zero"), l + 1)
                    if lv >= 2:
                        act.wait_ge(S("hg_mm"), 9 * l + lv)
                    x = halves(treeX[lv % 2], m)
                    act.activation(x[:, :, 0, :], halves(suff, m)[:, :, 0, :], ACT.Exp)
                    act.activation(x[:, :, 1, :], halves(pref, m)[:, :, 1, :], ACT.Exp).then_inc(S("hg_exp"), 1)
                    if lv >= 2:
                        gate(l, 4 + lv)
                act.activation(gates[:, :, :], gates[:, :, :], ACT.Sigmoid)
                act.wait_ge(S("hg_o"), l + 1)
                act.activation(osq, mix[:, 2:4, :].rearrange("p a b -> p (a b)"), ACT.Square).then_inc(S("hg_sq"), 1)
                act.wait_ge(S("hg_ms"), l + 1)
                act.activation(ostd, mix[:, 0:2, :].rearrange("p a b -> p (a b)"), ACT.Sqrt, bias=eps_rms)\
                   .then_inc(S("hg_std"), 1)

            def gla():
                for d in range(2):
                    act.wait_ge(S("decay_mm"), d + 1)
                    for c in range(2):
                        act.activation(gX[0][:, c, :], mix[:, 2 * d + c, :], ACT.Identity, bias=col("gla_ab_2", 2 * d + c))
                    act.drain().then_inc(S("decay_read"), 1)
                    act.activation(gX[1][:, :, :], gX[0][:, :, :], ACT.Abs)
                    act.drain()
                    act.activation(gX[1][:, :, :], gX[1][:, :, :], ACT.Exp, scale=-1.0)
                    act.drain()
                    act.activation(gX[1][:, :, :], gX[1][:, :, :], ACT.Ln, bias=one_col).then_inc(S("decay_ln"), 1)
                    act.wait_ge(S("decay_log"), d + 1)
                for n in range(18):
                    lv, d = n // 2, n % 2
                    m = 1 << lv
                    act.wait_ge(S("gla_sums"), n + 1)
                    if lv >= 1:
                        act.wait_ge(S("gla_mm"), 2 + 2 * (n - 2) + 2 if lv < 8 else 31 + d)
                    x = halves(gX[d].rearrange("p c t -> p (c t)"), m)
                    e, o = (0, 1) if (d == 0 or lv == 8) else (1, 0)
                    act.activation(x[:, :, e, :], halves(gsuff[:, d, :], m)[:, :, e, :], ACT.Exp)
                    act.activation(x[:, :, o, :], halves(gpref[:, d, :], m)[:, :, o, :], ACT.Exp).then_inc(S("gla_exp"), 1)
                act.wait_ge(S("gla_o"), 1)
                act.activation(gv[:, :, :], mix[:, :, :], ACT.Copy)
                act.activation(region(E_T, 4, 512), mix[:, :, :], ACT.Square)
                act.drain().then_inc(S("head_sq"), 1)
                act.wait_ge(S("head_ms"), 1)
                act.activation(region(E_T, 4, 512), mix[:, :, :], ACT.Sqrt, bias=eps_rms).then_inc(S("head_std"), 1)

            def mlstm():
                act.activation(tmp16[:, :], rows16[0:16, :], ACT.Abs)
                act.drain()
                act.activation(tmp16[:, :], tmp16[:, :], ACT.Exp, scale=-1.0)
                act.drain()
                act.activation(tmp16[:, :], tmp16[:, :], ACT.Ln, bias=one_col[0:16, :]).then_inc(S("ml_ln"), 1)
                for c in range(8):
                    act.wait_ge(S("ml_conv"), c + 1)
                    i = act.activation(qkc[:, c, :], qkc[:, c, :], ACT.Silu)
                i.then_inc(S("ml_qk"), 1)
                act.wait_ge(S("ml_cols"), 1)
                act.activation(bcol[:, :, :], mix[:, 0, 0:64].rearrange("p (a b) -> p a b", a=4), ACT.Copy).then_inc(S("ml_bcol"), 1)
                for i in range(8):
                    act.wait_ge(S("ml_sel"), i + 1)
                    act.activation(rall[:, i, :], mix[:, 1 + i % 3, :], ACT.Copy).then_inc(S("ml_rall"), 1)
                for t in range(4):
                    w = T if t < 2 else 2 * T
                    act.wait_ge(S("ml_max"), t + 1)
                    for i in range(8):
                        act.activation(dlog[:, i, 0:w], dlog[:, i, 0:w], ACT.Exp, bias=small[:, i:i + 1])
                    act.activation(small[:, 8:16], small[:, 0:8], ACT.Exp)
                    act.drain().then_inc(S("ml_exp"), 1)
                    act.wait_ge(S("ml_probT"), t + 1)
                    act.activation(mprobT[:, :, 0:w], mix[:, :, 0:w], ACT.Copy).then_inc(S("ml_probT_sb"), 1)
                    act.wait_ge(S("ml_hmm"), t + 1)
                    act.activation(mqk[:, 0:4, t * P:t * P + P], mix[:, :, 0:P], ACT.Copy).then_inc(S("ml_h"), 1)
                act.wait_ge(S("ml_gated"), 1)
                act.activation(region(E_T, 4, 512), mqk[:, 0:4, :], ACT.Square).then_inc(S("head_sq"), 1)
                act.wait_ge(S("head_ms"), 2)
                act.activation(region(E_T, 4, 512), mix[:, :, :], ACT.Sqrt, bias=eps_rms).then_inc(S("head_std"), 1)

            def ssd_rates():
                b = wait_ready(act, G["dt"], 0, 0)
                act.activation(dtr[0:64, :], acc[b][0:64, :], ACT.Identity, bias=col("ssd_dt_bias_2", 0, 0, 64)).then_inc(free[b], 1)
                act.activation(negA, col("ssd_a_log_2", 0, 0, 64), ACT.Exp)
                act.drain()
                act.activation(dcum[0:64, :], dtr[0:64, :], ACT.Abs)
                act.drain()
                act.activation(dcum[0:64, :], dcum[0:64, :], ACT.Exp, scale=-1.0).then_inc(S("dt_exp"), 1)
                act.wait_ge(S("dt_onep"), 1)
                act.activation(dtmp[0:64, :], dtmp[0:64, :], ACT.Ln).then_inc(S("dt_ln"), 1)
                act.wait_ge(S("dt_end"), 1)
                act.activation(dwe[0:64, :], dwe[0:64, :], ACT.Exp).then_inc(S("dt_wend"), 1)
                act.wait_ge(S("dt_cols"), 1)
                for dst, o in ((dtT, 0), (dcT, 128), (dwT, 256)):
                    act.activation(dst[:, :, :], mix[:, 0, o:o + 128].rearrange("p (a b) -> p a b", a=2), ACT.Copy)

            def ssd_features(g, q):
                xc, bcc = S_XC[g % 2], S_BCC[g % 2]
                if q >= 6:
                    evac(G[f"ssdz{g}"], 0, q - 6, 0, S_Z[g % 2][:, 2 * q - 12:2 * q - 10, :], both, ACT.Copy)
                    return
                b = wait_ready(act, G[f"ssdx{g}" if q < 4 else f"ssdbc{g}"], 0, q // 2 % 2, q % 2)
                c = ssd_channel(g, q)
                act.eng.activation(S_X[:, q, :] if q < 4 else S_BC[:, q - 4, :], acc[b], ACT.Copy)
                act.eng.activation(xc[:, q, :] if q < 4 else bcc[q - 4], acc[b], ACT.Identity,
                                   scale=col("ssd_conv_w_2", 24 + c), bias=col("ssd_conv_b_2", c)).then_inc(free[b], 1)
                act.drain().then_inc(S("ssd_raw"), 1)

            def ssd_silu(g):
                act.wait_ge(S("ssd_cv"), g + 1)
                act.eng.activation(S_XC[g % 2], S_XC[g % 2], ACT.Silu)
                for v in S_BCC[g % 2]:
                    act.eng.activation(v, v, ACT.Silu)
                act.eng.activation(S_Z[g % 2], S_Z[g % 2], ACT.Silu)
                act.drain().then_inc(S("ssd_conv"), 1)

            def ssd_group(g):
                act.wait_ge(S("ssd_xT"), g + 1)
                act.activation(S_XT[:, :, :], mix[:, :, :], ACT.Copy).then_inc(S("ssd_xT_sb"), 1)
                act.wait_ge(S("ssd_cb"), g + 1)
                act.activation(S_BT[:, :, :], mix[:, 0, 0:T].rearrange("p (a b) -> p a b", a=2), ACT.Copy).then_inc(S("ssd_bt"), 1)
                act.wait_ge(S("ssd_state"), g + 1)
                act.activation(S_ST[:, :, :], mix[:, 2:4, :], ACT.Copy).then_inc(S("ssd_state_sb"), 1)
                if g < 3:
                    ssd_features(g + 1, 0)
                    ssd_features(g + 1, 1)
                for i in range(16):
                    n = 16 * g + i
                    act.wait_ge(S("ssd_row"), n + 1)
                    if n >= 2:
                        act.wait_ge(S("ssd_cw"), n - 1)
                    act.activation(S_ER[:, n % 2, :], mix[:, i % 2, 0:T], ACT.Exp).then_inc(S("ssd_erow"), 1)
                    act.wait_ge(S("ssd_dmin"), n + 1)
                    act.activation(S_DW[:, n % 2, :], S_DW[:, n % 2, :], ACT.Exp).then_inc(S("ssd_edec"), 1)
                    if i % 2 == 0 and 2 <= i < 14 and g < 3:
                        ssd_features(g + 1, 1 + i // 2)
                if g < 3:
                    ssd_silu(g + 1)
                act.wait_ge(S("ssd_yz"), g + 1)
                act.activation(S_SQ[:, :, :], S_Y[:, 4 * g:4 * g + 4, :], ACT.Square).then_inc(S("ssd_gsq"), 1)
                act.wait_ge(S("ssd_gms"), g + 1)
                act.activation(S_STD, mix[:, 0, 0:T], ACT.Sqrt, bias=eps_rms).then_inc(S("ssd_gstd"), 1)

            def ffn_up(l):
                g = G[f"up{l}"]
                w = 512 if l == 0 else T

                def silu(par, count):
                    act.wait_ge(S("up_conv"), count)
                    act.activation(uconv[:, par, 2:4, 0:w], uconv[:, par, 2:4, 0:w], ACT.Silu).then_inc(S("up_silu"), 1)

                def body(it, u):
                    par = u // 2
                    if u % 2 == 0:
                        if isinstance(it, int) and it == 0:
                            if u == 0:
                                act.wait_ge(S("up_zero"), l + 1)
                        else:
                            act.wait_ge(S("up_used"), it * 2 + (11 * l + par - 1))
                    for j in range(2):
                        c = 2 * (u % 2) + j
                        if j == 0 or l == 0:
                            b = wait_ready(act, g, it, u, j if l == 0 else 0)
                        o = j * T if l == 1 else T
                        grid = lambda v: v.rearrange("p (r w) -> p r w", r=GRID_ROWS)
                        lo = T if l == 0 else 0
                        middle, bias = ffn_tap(l, it, 4, u % 2, j, par), ffn_bias(l, it, u % 2, j, par)
                        act.eng.activation(
                            upad_l[:, par, c, :].rearrange("p (r w) -> p r w", r=GRID_ROWS + 2)[:, 1:GRID_ROWS + 1, 1:GRID_W + 1],
                            grid(acc[b][:, o:o + T]), ACT.Copy)
                        if l == 0:
                            act.eng.activation(upad_c[:, par, c, 1:T + 1], acc[b][:, 0:T], ACT.Copy)
                        last = act.eng.activation(uconv[:, par, c, 0:w], acc[b][:, 0:512] if l == 0 else acc[b][:, o:o + T],
                                                  ACT.Identity, scale=middle, bias=bias)
                        if j == 1 or l == 0:
                            last.then_inc(free[b], 1)
                    if u % 2 == 1:
                        act.drain().then_inc(S("up_raw"), 1)
                        if not (isinstance(it, int) and it == 0 and par == 0):
                            silu(1 - par, it * 2 + (11 * l + par))

                groups(act, g, body, peel=True)
                silu(0, 11 * l + 11)

            act.wait_ge(S("loaded"), 96)
            act.activation(cond[:, :], cols[:, COL["c"]:COL["c"] + 8], ACT.Silu)
            act.activation(cond2[:, :, 0], cols[:, COL["c_2"]:COL["c_2"] + 8], ACT.Silu)
            act.activation(cond2[:, :, 1], cols[:, COL["c_ctx_2"]:COL["c_ctx_2"] + 8], ACT.Silu)
            act.drain().then_inc(S("cond_ready"), 1)
            act.wait_ge(S("bias_mm"), 1)
            act.activation(bias_rows[0:4, :], mix[0:4, 0, 0:384], ACT.Copy).then_inc(S("bias_rows"), 1)
            act.wait_ge(S("lb_diff"), 1)
            act.activation(small[:, 0:8], small[:, 0:8], ACT.Exp).then_inc(S("lb_exp"), 1)
            n = 0
            stage_end(act, count)
            for l in range(DEPTH):
                for f in range(2):
                    if f == 1:
                        g = G[f"mix{l}"]
                        for u in range(15):
                            if u == 0:
                                evac(g, 0, u, 0, apad[:, :, PAD:PAD + T], both, ACT.Copy)
                            elif u == 5:
                                b = wait_ready(act, g, 0, u)
                                act.activation(kiT, acc[b][:, 0:T], ACT.Copy)
                                act.activation(wi[:, :, :], acc[b][:, T:T + 16].rearrange("p (a b) -> p a b", a=2), ACT.Copy)\
                                   .then_inc(free[b], 1)
                            else:
                                dst, func, scale = {
                                    1: (qT[:, :, :], ACT.Copy, 1.0), 2: (kT[:, :, :], ACT.Copy, 1.0),
                                    3: (qiT[:, 0:2, :], ACT.Copy, 1.0), 4: (qiT[:, 2:4, :], ACT.Copy, 1.0),
                                    6: (vt[:, :, :], ACT.Copy, 1.0), 7: (hi[:, :, 0:T], ACT.Copy, 1.0),
                                    8: (hi[:, :, T:512], ACT.Copy, 1.0), 9: (qf[:, 0:2, :], ACT.Silu, 1.0),
                                    10: (qf[:, 2:4, :], ACT.Silu, 1.0), 11: (hgs[:, 0:2, :], ACT.Silu, 1.0),
                                    12: (hgs[:, 2:4, :], ACT.Silu, 1.0), 13: (kk[:, 0:2, :], ACT.Sigmoid, -1.0),
                                    14: (kk[:, 2:4, :], ACT.Sigmoid, -1.0)}[u]
                                evac(g, 0, u, 0, dst, both, func, scale)
                        stage_end(act, count)
                        pool(l)
                        stage_end(act, count)
                        attention(l)
                        stage_end(act, count)
                        hgrn(l)
                        stage_end(act, count)
                        stage_end(act, count)
                        layer_norm(n, l, 1)
                        n += 1
                        stage_end(act, count)
                    g = G[f"in{l}{f}"]
                    high(g, 0, 0)

                    def split_and_gate(it, u, g=g):
                        if not (isinstance(it, int) and 4 * it + u + 1 == g.n):
                            high(g, it, u + 1)
                        if u % 2 == 0:
                            evac(g, it, u, 0, hid_raw[:, bass.ds(it * 4 + u, 2), :], both, ACT.Silu)

                    groups(act, g, split_and_gate, peel=True)
                    wait_used(act, g, 5, 1, 1)
                    for i in range(8):
                        high(G[f"out{l}{f}"], 0, i)
                    layer_norm(n, l, 2 * f)
                    n += 1
                    stage_end(act, count)
            rms = 0
            for l in range(DEPTH):
                rms_norm(rms, both)
                rms += 1
                stage_end(act, count)
                if l == 0:
                    g = G["even"]
                    feat = {0: gq, 1: gk, 4: ey[:, 0:2, :], 5: ey[:, 2:4, :], 6: mqk[:, 0:2, :], 7: mqk[:, 2:4, :],
                            8: mqk[:, 4:6, :], 9: mqk[:, 6:8, :], 12: ey[:, 4:6, :], 13: ey[:, 6:8, :]}
                    func = {4: ACT.Silu, 5: ACT.Silu, 12: ACT.Sigmoid, 13: ACT.Sigmoid}
                    for u in range(14):
                        for r in range(2):
                            if u in (2, 3, 10, 11):
                                dst = gv if u < 4 else mv
                                evac(g, 0, u, r, dst[:, 2 * r:2 * r + 2, u % 2 * T:u % 2 * T + T], both, ACT.Copy)
                            else:
                                evac(g, 0, u, r, feat[u][:, r, :], both, func.get(u, ACT.Copy), 0.125 if u == 0 else 1.0)
                    b = wait_ready(act, G["evengate"], 0, 0)
                    act.activation(rows16[0:16, :], acc[b][0:16, :], ACT.Identity, bias=col("ml_gate_b_2", 0, 0, 16))
                    act.activation(rows16[32:64, :], acc[b][32:64, :], ACT.Copy)
                    act.activation(rows16[64:96, :], acc[b][64:96, :], ACT.Copy).then_inc(free[b], 1)
                    act.drain().then_inc(S("rank_ready"), 1)
                    stage_end(act, count)
                    gla()
                    stage_end(act, count)
                    mlstm()
                    stage_end(act, count)
                else:
                    ssd_rates()
                    stage_end(act, count)
                    for q in range(8):
                        ssd_features(0, q)
                    ssd_silu(0)
                    for g in range(4):
                        ssd_group(g)
                    stage_end(act, count)
                stage_end(act, count)
                rms_norm(rms, both if l == 0 else lat)
                rms += 1
                stage_end(act, count)
                ffn_up(l)
                stage_end(act, count)
            rms_norm(rms, lat)

        @block.vector
        def _(dve):
            dve = InOrder(dve)
            count = [0]

            def stt(out, a, s, b, op0, op1, **kw):
                return dve.scalar_tensor_tensor(out=out, in0=a, scalar=s, in1=b, op0=op0, op1=op1, **kw)

            def bc(v, n):
                return v.unsqueeze(1).to_broadcast([v.shape[0], n, v.shape[1]])

            def cond_weigh(phase, i, e):
                n0 = CARRY[phase][0]
                conds = [cond2[:, :, 0], cond2[:, :, 1]] if n0 >= MOD0 else [cond]
                slot = (n0 + e) % 2
                w, parts = cond_slots[phase == "even"][slot], [p[slot] for p in cond_part]
                dve.wait_ge(cond_landed[slot], i * 8 + (8 * (n0 - slot) + 16))
                if not isinstance(i, int) or i + n0 >= 2:
                    dve.wait_ge(S("cond_summed"), i + (n0 - 1))
                for k in range(KD):
                    for c, part in zip(conds, parts):
                        if k == 0:
                            dve.eng.tensor_tensor(part, w[:, 0, :], c[:, 0:1].to_broadcast([P, PANEL]), ALU.mult)
                        else:
                            dve.eng.scalar_tensor_tensor(out=part, in0=w[:, k, :], scalar=c[:, k:k + 1], in1=part, op0=ALU.mult, op1=ALU.add)
                    if k < KD - 1:
                        dve.drain()
                dve.drain().then_inc(S("cond_part"), 1)

            def cond_take(phase):
                n0, cnt = CARRY[phase]
                dve.wait_ge(S("cond_summed"), n0 + cnt)
                src = mix[:, cond_bank(phase), :]
                for first, size, table in [(l * ADA, ADA, mods1[:, l, :]) for l in range(DEPTH)] + \
                                          [(MOD0 + l * MOD, MOD, mods2[:, l, :, :]) for l in range(DEPTH)]:
                    a, b = max(n0, first), min(n0 + cnt, first + size)
                    if a >= b:
                        continue
                    t0, t1, s0, s1 = 2 * (a - first), 2 * (b - first), 2 * (a - n0), 2 * (b - n0)
                    if n0 >= MOD0:
                        bias = cols[:, COL["mod_b_2"] + 2 * (a - MOD0):COL["mod_b_2"] + 2 * (b - MOD0)]
                        for v in range(2):
                            dve.tensor_tensor(table[:, t0:t1, v], src[:, T * v + s0:T * v + s1], bias, ALU.add)
                    else:
                        bias = cols[:, COL["b_ada"] + 2 * a:COL["b_ada"] + 2 * b]
                        dve.tensor_tensor(table[:, t0:t1], src[:, s0:s1], bias, ALU.add)
                        for j in (0, 2):
                            if t0 <= 24 * j + 16 and 24 * j + 24 <= t1:
                                gt = table[:, 24 * j + 16:24 * j + 24]
                                dve.tensor_scalar(gt, gt, 0.5, None, ALU.mult)

            def modulated(l, j):
                mod1 = mods1[:, l, :]
                for k in range(KD):
                    dve.eng.tensor_scalar(H[:, k, lat] if j == 1 else h_raw[:, k, :], X[:, k, lat], mod1[:, 24 * j + 8 + k:24 * j + 9 + k],
                                          mod1[:, 24 * j + k:24 * j + k + 1], ALU.mult, ALU.add)
                if j != 1:
                    dve.drain()
                    dve.tensor_copy(h_hi, h_raw)
                    dve.tensor_tensor(h_lo, h_raw, h_hi, ALU.subtract)
                dve.drain().then_inc(S("h_ready"), 1)
                dve.tensor_scalar(X[:, :, lat], X[:, :, lat], float(ALPHA), None, ALU.mult)
                dve.drain()

            def residual(g, l, gate0):
                mod1 = mods1[:, l, :]
                for n in range(4):
                    b = wait_ready(dve, g, 0, n)
                    for j in range(2):
                        k = 2 * n + j
                        i = stt(X[:, k, lat], acc[b][:, j * T:j * T + T], mod1[:, gate0 + k:gate0 + k + 1], X[:, k, lat], ALU.mult, ALU.add)
                    i.then_inc(free[b], 1)

            def layer_norm(n):
                dve.wait_ge(S("mean_ready"), n + 1)
                for k in range(KD):
                    dve.tensor_tensor(X[:, k, lat], X[:, k, lat], mix[:, 0, 0:T], ALU.subtract).then_inc(S("centred"), 1)
                dve.wait_ge(S("std_ready"), n + 1)
                dve.reciprocal(std[:, 0:T], std[:, 0:T])
                dve.drain()
                for k in range(KD):
                    dve.tensor_tensor(X[:, k, lat], X[:, k, lat], std[:, 0:T], ALU.mult).then_inc(S("scaled"), 1)
                dve.wait_ge(S("x_ready"), KD * (n + 1))

            def rms_norm(n, sel, gain, shift, streams):
                w = sel.stop - sel.start
                dve.wait_ge(S("rms_std"), n + 1)
                dve.reciprocal(std[:, 0:w], std[:, 0:w])
                dve.drain()
                dve.tensor_tensor(H[:, :, sel], X[:, :, sel], bc(std[:, 0:w], KD), ALU.mult)
                dve.drain()
                for k in range(KD):
                    for v in streams:
                        t = lat if v == 0 else slice(0, T)
                        if shift is None:
                            i = dve.tensor_scalar(H[:, k, t], H[:, k, t], gain(k, v), None, ALU.mult)
                        else:
                            i = dve.tensor_scalar(H[:, k, t], H[:, k, t], gain(k, v), shift[:, k, v:v + 1], ALU.mult, ALU.add)
                return i

            def pool(l):
                src = apad
                for i, w in enumerate((1, 2, 4, 8)):
                    dve.tensor_copy(win[i][:, :, 0:w], src[:, :, 0:w])
                    dve.tensor_tensor(win[i][:, :, w:PAD + T], src[:, :, w:PAD + T], src[:, :, 0:PAD + T - w], ALU.add)
                    dve.drain()
                    src = win[i]
                cnt = const("invcnt").rearrange("p (a t) -> p a t", a=2)
                for i in range(4):
                    r = slice(64 * (i % 2), 64 * (i % 2) + 64)
                    dve.tensor_tensor(pdiff[r, i // 2, :], win[i][r, i // 2, PAD:PAD + T], cnt[r, i // 2, :], ALU.mult)
                dve.drain()
                dve.tensor_tensor(pdiff[:, :, :], pdiff[:, :, :], apad[:, :, PAD:PAD + T], ALU.subtract).then_inc(S("pool_diff"), 1)

            def attention(l):
                for qb in range(2):
                    n = P * (qb + 1)
                    off = 0 if qb == 1 else P
                    for h in range(8):
                        if h % 2 == 0:
                            dve.wait_ge(S("idx_relu"), 8 * l + 4 * qb + h // 2 + 1)
                        head = 2 * (2 * (h // 2 % 2) + h % 2) + h // 4
                        w = wi[:, qb, head:head + 1]
                        if h == 0:
                            i = dve.tensor_scalar(score[:, 0:n], relu_s[:, h, 0:n], w, None, ALU.mult)
                        else:
                            i = stt(score[:, 0:n], relu_s[:, h, 0:n], w, score[:, 0:n], ALU.mult, ALU.add)
                        if h == 7:
                            i.then_inc(S("idx_sum"), 1)
                        dve.drain()
                    stt(score[:, 0:n], score[:, 0:n], IDX_SCALE, const("causal")[:, off:off + n], ALU.mult, ALU.add)
                    dve.drain()
                    src = score
                    for r in range(TOPK // 8):
                        dve.max(small[:, 16:24], src[:, 0:n])
                        dve.drain()
                        dve.match_replace(work[:, 0:n], small[:, 16:24], src[:, 0:n], GONE)
                        dve.drain()
                        src = work
                    dve.tensor_tensor(addm[:, 0:n], work[:, 0:n], score[:, 0:n], ALU.is_equal)
                    dve.drain()
                    dve.tensor_scalar(addm[:, 0:n], addm[:, 0:n], MASKED, None, ALU.mult)
                    dve.drain()
                    dve.wait_ge(S("logit_mm"), 2 * l + qb + 1)
                    lg = logit[:, qb, :, 0:n]
                    src = mix[:, 2 * qb:2 * qb + 2, :].rearrange("p a (b t) -> p (a b) t", b=2)[:, :, 0:n]
                    stt(lg, src, 64 ** -0.5, biasC[:, :, off:off + n], ALU.mult, ALU.add)
                    dve.drain()
                    dve.tensor_tensor(lg, lg, bc(addm[:, 0:n], 4), ALU.add)
                    dve.drain()
                    dve.tensor_reduce(small[:, 8 * qb:8 * qb + 4], lg, AXX, ALU.max, negate=True).then_inc(S("logit_ready"), 1)
                for qb in range(2):
                    n = P * (qb + 1)
                    dve.wait_ge(S("exp_ready"), 2 * l + qb + 1)
                    r = small[:, 8 * qb + 4:8 * qb + 8]
                    dve.reciprocal(r, r)
                    dve.drain()
                    dve.tensor_tensor(logit[:, qb, :, 0:n], logit[:, qb, :, 0:n],
                                      r.unsqueeze(2).to_broadcast([P, 4, n]), ALU.mult).then_inc(S("prob_ready"), 1)

            def halves(v, m):
                return v.rearrange("p (n two m) -> p n two m", two=2, m=m)

            def last_bc(v, e, edge, m):
                return halves(v, m)[:, :, e, edge:edge + 1].to_broadcast([P, v.shape[1] // (2 * m), m])

            def hgrn(l):
                for h in range(4):
                    dve.tensor_scalar(kk[:, h, :], kk[:, h, :], one_lb[:, l, h:h + 1], None, ALU.mult)
                dve.drain()
                dve.tensor_scalar(pref, kk[:, :, :].rearrange("p a b -> p (a b)"), KEY_MAX, -1.0, ALU.min, ALU.mult)
                dve.drain().then_inc(S("hg_key"), 1)
                dve.memset(suff, 0.0).then_inc(S("hg_zero"), 1)
                mask = const("tree_f")
                kf, qq = kk[:, :, :].rearrange("p a b -> p (a b)"), qf[:, :, :].rearrange("p a b -> p (a b)")

                def take(i):
                    bank = 2 * (i % 2)
                    dve.wait_ge(S("hg_mm"), 9 * l + i + 1)
                    src = mix[:, bank:bank + 2, :].rearrange("p a (h t) -> p (a h) t", h=4)
                    if i == 0:
                        dve.tensor_tensor(pairs[:, :, :], src, bc(ident, 8), ALU.mult).then_inc(S("hg_acc"), 1)
                    elif i < 8:
                        level = mask[:, (i - 1) * P:i * P].bitcast(mybir.dt.uint32)
                        dve.eng.copy_predicated(pairs[:, :, :], bc(level, 8), src).then_inc(S("hg_acc"), 1)
                        dve.drain()
                    else:
                        dve.tensor_copy(offd[:, :, :], src[:, 0:4, :])
                        dve.drain().then_inc(S("hg_acc"), 1)

                for lv in range(8):
                    m = 1 << lv
                    x = halves(treeX[lv % 2], m)
                    dve.wait_ge(S("hg_exp"), 8 * l + lv + 1)
                    if lv < 7:
                        dve.tensor_tensor(halves(suff, m)[:, :, 0, :], halves(suff, m)[:, :, 0, :], last_bc(pref, 1, m - 1, m), ALU.add)
                        dve.drain()
                        dve.tensor_tensor(halves(pref, m)[:, :, 1, :], halves(pref, m)[:, :, 1, :], last_bc(pref, 0, m - 1, m), ALU.add)
                        dve.drain().then_inc(S("hg_sums"), 1)
                    dve.tensor_tensor(x[:, :, 0, :], x[:, :, 0, :], halves(kf, m)[:, :, 0, :], ALU.mult)
                    dve.tensor_tensor(x[:, :, 1, :], x[:, :, 1, :], halves(qq, m)[:, :, 1, :], ALU.mult)
                    dve.drain().then_inc(S("hg_x"), 1)
                    take(lv)
                take(8)
                dve.wait_ge(S("hg_std"), l + 1)
                dve.reciprocal(ostd, ostd)
                dve.drain()
                dve.tensor_tensor(onorm[:, :, :].rearrange("p a b -> p (a b)"), mix[:, 2:4, :].rearrange("p a b -> p (a b)"), ostd, ALU.mult)
                dve.drain()
                for h in range(4):
                    stt(ymix[:, 4 + h, :], onorm[:, h, :], col("hgrn_norm_g", 4 * l + h), hgs[:, h, :], ALU.mult, ALU.mult)

            def branch(l):
                g = G[f"branch{l}"]
                for u in range(4):
                    for r in range(3):
                        b = wait_ready(dve, g, 0, u, r)
                        src = acc[b][:, :].rearrange("p (a t) -> p a t", a=2)
                        dst = merged[:, 2 * u:2 * u + 2, :]
                        gt = gates[:, 8 * r + 2 * u:8 * r + 2 * u + 2, :]
                        if r == 0:
                            dve.tensor_tensor(dst, src, gt, ALU.mult).then_inc(free[b], 1)
                        else:
                            dve.tensor_tensor(mtmp[:, :, :], src, gt, ALU.mult).then_inc(free[b], 1)
                            dve.drain()
                            dve.tensor_tensor(dst, dst, mtmp[:, :, :], ALU.add)
                        dve.drain()

            def gla():
                for d in range(2):
                    dve.wait_ge(S("decay_ln"), d + 1)
                    v = gX[0][:, :, :].rearrange("p a b -> p (a b)")
                    stt(logd[:, d, :], v, 0.0, gX[1][:, :, :].rearrange("p a b -> p (a b)"), ALU.min, ALU.subtract)
                    dve.drain()
                    dve.tensor_scalar(logd[:, d, :], logd[:, d, :], 1.0 / 16.0, None, ALU.mult)
                    dve.drain().then_inc(S("decay_log"), 1)
                dve.memset(gsuff[:, :, :], 0.0)
                dve.drain().then_inc(S("gla_sums"), 2)

                def take(n):
                    lv, d = n // 2, n % 2
                    if lv == 7:
                        dve.wait_ge(S("gla_mm"), 31 + d)
                        dve.tensor_copy(goff[:, 8 * d:8 * d + 8, :].rearrange("p a t -> p (a t)"),
                                        gla_banks[d][:, 0:2, :].rearrange("p a t -> p (a t)")).then_inc(S("gla_acc"), 1)
                        return
                    for hf in range(2):
                        dve.wait_ge(S("gla_mm"), 2 + 2 * n + hf + 1)
                        src = gla_banks[d][:, 2 * hf:2 * hf + 2, :].rearrange("p a (h t) -> p (a h) t", h=4)
                        mask = const("tree_f" if d == 0 else "tree_b", lv * P, P)
                        dve.eng.copy_predicated(gpairs[:, 8 * hf:8 * hf + 8, :], bc(mask.bitcast(mybir.dt.uint32), 8), src).then_inc(S("gla_acc"), 1)
                        dve.drain()

                for hf in range(2):
                    dve.wait_ge(S("gla_mm"), hf + 1)
                    src = mix[:, 2 * hf:2 * hf + 2, :].rearrange("p a (h t) -> p (a h) t", h=4)
                    stt(gpairs[:, 8 * hf:8 * hf + 8, :], src, 2.0, bc(ident, 8), ALU.mult, ALU.mult).then_inc(S("gla_acc"), 1)
                kf, qq = gk[:, :, :].rearrange("p a b -> p (a b)"), gq[:, :, :].rearrange("p a b -> p (a b)")
                for n in range(18):
                    lv, d = n // 2, n % 2
                    m = 1 << lv
                    x = halves(gX[d].rearrange("p c t -> p (c t)"), m)
                    pref, suff = gpref[:, d, :], gsuff[:, d, :]
                    e, o = (0, 1) if (d == 0 or lv == 8) else (1, 0)
                    edge = m - 1 if d == 0 else 0
                    dve.wait_ge(S("gla_exp"), n + 1)
                    dve.eng.tensor_tensor(x[:, :, e, :], x[:, :, e, :], halves(kf, m)[:, :, e, :], ALU.mult)
                    dve.tensor_tensor(x[:, :, o, :], x[:, :, o, :], halves(qq, m)[:, :, o, :], ALU.mult)
                    dve.drain().then_inc(S("gla_x"), 1)
                    if lv < 8:
                        dve.tensor_tensor(halves(suff, m)[:, :, e, :], halves(suff, m)[:, :, e, :], last_bc(pref, o, edge, m), ALU.add)
                        dve.tensor_tensor(halves(pref, m)[:, :, o, :], halves(pref, m)[:, :, o, :], last_bc(pref, e, edge, m), ALU.add)
                        dve.drain().then_inc(S("gla_sums"), 1)
                    if 1 <= n < 17:
                        take(n - 1)
                dve.wait_ge(S("gla_mm"), 33)
                dve.tensor_copy(gcross[:, :, :, :], mix[:, :, :].rearrange("p h (s t) -> p s h t", s=2))
                dve.drain().then_inc(S("gla_acc"), 1)
                dve.wait_ge(S("head_std"), 1)
                rs = region(E_T, 4, 512)
                dve.reciprocal(rs, rs)
                dve.drain()
                dve.tensor_tensor(rs, rs, gv[:, :, :], ALU.mult)
                dve.drain()
                for h in range(4):
                    stt(ey[:, h, :], rs[:, h, :], col("gla_norm_g_2", h), ey[:, h, :], ALU.mult, ALU.mult)

            def conv3(dst, src, w, b, c, nch, nst):
                dve.tensor_scalar(dst, src, col(w, nch + c), col(b, c), ALU.mult, ALU.add)
                return outer_taps(dst, src, w, c, nch, nst)

            def outer_taps(dst, src, w, c, nch, nst):
                s2 = src.rearrange("p (s t) -> p s t", s=nst)
                d2 = dst.rearrange("p (s t) -> p s t", s=nst)
                stt(d2[:, :, 1:T], s2[:, :, 0:T - 1], col(w, c), d2[:, :, 1:T], ALU.mult, ALU.add)
                dve.drain()
                return stt(d2[:, :, 0:T - 1], s2[:, :, 1:T], col(w, 2 * nch + c), d2[:, :, 0:T - 1], ALU.mult, ALU.add)

            def mlstm():
                for c in range(8):
                    conv3(qkc[:, c, :], mqk[:, c, :], "ml_conv_w_2", "ml_conv_b_2", c, 8, 2).then_inc(S("ml_conv"), 1)
                dve.wait_ge(S("ml_ln"), 1)
                stt(lsg[:, :], rows16[0:16, :], 0.0, tmp16[:, :], ALU.min, ALU.subtract)
                dve.memset(tmp16[:, :], 1.0)
                dve.drain()
                dve.tensor_tensor_scan(cum16[:, :], tmp16[:, :], lsg[:, :], 0.0, ALU.mult, ALU.add)
                dve.drain()
                dve.tensor_tensor(tmp16[:, :], lsg[:, :], cum16[:, :], ALU.subtract)
                dve.drain()
                dve.tensor_scalar(tmp16[:, 0:T], tmp16[:, 0:T], cum16[:, T - 1:T], None, ALU.add)
                dve.tensor_scalar(tmp16[:, T:512], tmp16[:, T:512], cum16[:, 511:512], cum16[:, T - 1:T], ALU.add, ALU.add)
                dve.drain()
                dve.tensor_tensor(tmp16[:, :], tmp16[:, :], cum16[:, :], ALU.subtract)
                dve.drain()
                stt(cum16[:, :], tmp16[:, :], bwd_rows, cum16[:, :], ALU.mult, ALU.add)
                dve.drain().then_inc(S("ml_rows"), 1)
                dve.wait_ge(S("masks_loaded"), 16)
                dve.wait_ge(S("ml_bcol"), 1)
                dve.wait_ge(S("ml_rall"), 8)
                scale = 128 ** -0.5
                for t in range(4):
                    w = T if t < 2 else 2 * T
                    o = 0 if t < 2 else T
                    for i in range(8):
                        h, d = i % 4, i // 4
                        b = bcol[:, t, 8 * d + 4 + h:8 * d + 5 + h]
                        mask = const("mneg", (2 * d + t % 2) * T, T)
                        stt(dlog[:, i, o:o + T], rall[:, i, o:o + T], b, mask, ALU.add, ALU.add)
                        if t >= 2:
                            dve.tensor_scalar(dlog[:, i, 0:T], rall[:, i, 0:T], b, None, ALU.add)
                    dve.drain()
                    dve.tensor_reduce(small[:, 0:8], dlog[:, :, 0:w], AXX, ALU.max)
                    dve.drain()
                    dve.tensor_scalar(small[:, 0:8], small[:, 0:8], 0.0, -1.0, ALU.max, ALU.mult)
                    dve.drain().then_inc(S("ml_max"), 1)
                    dve.wait_ge(S("ml_exp"), t + 1)
                    dve.wait_ge(S("ml_scores"), t + 1)
                    for i in range(8):
                        stt(dlog[:, i, 0:w], dlog[:, i, 0:w], scale, mix[:, i % 4, 0:w], ALU.mult, ALU.mult,
                            accum_out=small[:, 16 + i:17 + i])
                    dve.drain()
                    stt(small[:, 16:24], small[:, 16:24], -1.0, small[:, 16:24], ALU.mult, ALU.max)
                    dve.drain()
                    dve.tensor_tensor(small[:, 16:24], small[:, 16:24], small[:, 8:16], ALU.max)
                    dve.drain()
                    dve.reciprocal(small[:, 16:24], small[:, 16:24])
                    dve.drain()
                    for h in range(4):
                        dve.tensor_scalar(psum2[:, h, 0:w], dlog[:, h, 0:w], small[:, 16 + h:17 + h], None, ALU.mult)
                    dve.drain()
                    for h in range(4):
                        stt(psum2[:, h, 0:w], dlog[:, 4 + h, 0:w], small[:, 20 + h:21 + h], psum2[:, h, 0:w], ALU.mult, ALU.add)
                    dve.drain().then_inc(S("ml_prob"), 1)
                dve.wait_ge(S("ml_h"), 4)
                dve.tensor_tensor(mqk[:, 0:4, :], mqk[:, 0:4, :], ey[:, 4:8, :], ALU.mult).then_inc(S("ml_gated"), 1)
                dve.wait_ge(S("head_std"), 2)
                rs = region(E_T, 4, 512)
                dve.reciprocal(rs, rs)
                dve.drain()
                for h in range(4):
                    stt(ey[:, 4 + h, :], mqk[:, h, :], col("ml_norm_g_2", h), rs[:, h, :], ALU.mult, ALU.mult)

            def ssd_rates():
                dve.wait_ge(S("dt_exp"), 1)
                e, u, d64 = dcum[0:64, :], dtmp[0:64, :], dtr[0:64, :]
                dve.tensor_scalar(u, e, 1.0, None, ALU.add)
                dve.drain().then_inc(S("dt_onep"), 1)
                sp_q, sp_m = S_X[0:64, 0, :], S_X[0:64, 1, :]
                dve.tensor_scalar(sp_q, e, 1.0, -1.0, ALU.add, ALU.add)
                dve.drain()
                dve.tensor_scalar(sp_m, sp_q, 0.0, None, ALU.is_equal)
                dve.drain()
                dve.tensor_tensor(sp_q, sp_q, sp_m, ALU.add)
                dve.drain()
                dve.reciprocal(sp_q, sp_q)
                dve.drain()
                dve.wait_ge(S("dt_ln"), 1)
                dve.tensor_tensor(u, u, sp_q, ALU.mult)
                dve.drain()
                dve.tensor_tensor(u, u, sp_m, ALU.add)
                dve.drain()
                dve.tensor_tensor(u, u, e, ALU.mult)
                dve.drain()
                stt(d64, d64, 0.0, u, ALU.max, ALU.add)
                dve.tensor_scalar(negA, negA, -1.0, None, ALU.mult)
                dve.drain()
                dta = u
                dve.tensor_scalar(dta, d64, negA, None, ALU.mult)
                dve.memset(sp_q, 1.0)
                dve.drain()
                f = dcum[0:64, :]
                for s in range(2):
                    dve.tensor_tensor_scan(f[:, s * T:s * T + T], sp_q[:, 0:T], dta[:, s * T:s * T + T], 0.0, ALU.mult, ALU.add)
                dve.drain()
                we = dwe[0:64, :]
                dve.tensor_scalar(we[0:32, :], f[0:32, 0:T], -1.0, f[0:32, T - 1:T], ALU.mult, ALU.add)
                dve.tensor_tensor(we[32:64, :], f[32:64, 0:T], dta[32:64, 0:T], ALU.subtract)
                dve.tensor_tensor(sp_m[32:64, 0:T], dta[32:64, lat], f[32:64, lat], ALU.subtract)
                dve.tensor_copy(sp_m[32:64, T:T + 1], f[32:64, 511:512])
                dve.drain().then_inc(S("dt_end"), 1)
                dve.tensor_scalar(f[32:64, lat], sp_m[32:64, 0:T], sp_m[32:64, T:T + 1], None, ALU.add)
                dve.drain()
                dve.wait_ge(S("dt_wend"), 1)
                dve.tensor_tensor(we, we, d64[:, 0:T], ALU.mult)
                dve.drain().then_inc(S("dt_rows"), 1)

            def ssd_conv(g, q):
                dve.wait_ge(S("ssd_raw"), 6 * g + q + 1)
                src = S_X[:, q, :] if q < 4 else S_BC[:, q - 4, :]
                dst = S_XC[g % 2][:, q, :] if q < 4 else S_BCC[g % 2][q - 4]
                outer_taps(dst, src, "ssd_conv_w_2", ssd_channel(g, q), 24, 2)
                if q == 5:
                    dve.drain().then_inc(S("ssd_cv"), 1)

            def ssd_group(g):
                cc, xc = S_BCC[g % 2][1], S_XC[g % 2]
                dve.wait_ge(S("ssd_xT_sb"), g + 1)
                for d in range(2):
                    for s in range(2):
                        w = dwT[:, s, 32 * d + 8 * g:32 * d + 8 * g + 8].unsqueeze(2).to_broadcast([P, 8, 64])
                        dve.tensor_tensor(S_XW[:, d, s, :].rearrange("p (h q) -> p h q", h=8),
                                          S_XT[:, s, :].rearrange("p (h q) -> p h q", h=8), w, ALU.mult)
                dve.drain().then_inc(S("ssd_xw"), 1)
                dve.wait_ge(S("ssd_cb"), g + 1)
                dve.wait_ge(S("ssd_bt"), g + 1)
                up, dn = const("tri", 0, P), const("tri", P, P)
                dve.tensor_tensor(S_CB[:, 0, 0:P], mix[:, 1, 0:P], up, ALU.mult)
                dve.tensor_copy(S_CB[:, 0, P:T], mix[:, 1, P:T])
                dve.tensor_tensor(S_CB[:, 0, T:T + P], mix[:, 1, T + P:512], up, ALU.mult)
                dve.tensor_tensor(S_CB[:, 1, 0:P], mix[:, 1, 0:P], dn, ALU.mult)
                dve.tensor_copy(S_CB[:, 1, P:T], mix[:, 1, T:T + P])
                dve.tensor_tensor(S_CB[:, 1, T:T + P], mix[:, 1, T + P:512], dn, ALU.mult)
                dve.drain().then_inc(S("ssd_cb_sb"), 1)
                for i in range(16):
                    pr, hh, d = i // 4, i // 2 % 2, i % 2
                    n = 16 * g + i
                    row = 32 * d + 8 * g + 2 * pr + hh
                    R = mix[:, i % 2, :]
                    W = S_DW[:, n % 2, :]
                    if n >= 2:
                        dve.wait_ge(S("ssd_ymm"), n - 1)
                    dve.wait_ge(S("ssd_erow"), n + 1)
                    cs = [dcT[:, s, row:row + 1] for s in range(2)]
                    spans = ((0, T, 0, T), (T, T + P, P, T)) if d == 0 else ((0, P, 0, P), (P, P + T, 0, T))
                    for s, (a, b, t0, t1) in enumerate(spans):
                        dve.tensor_scalar(W[:, a:b], R[:, t0:t1], cs[s], 0.0, ALU.subtract, ALU.min)
                    dve.drain().then_inc(S("ssd_dmin"), 1)
                    dve.tensor_tensor(S_CW[:, n % 2, :], S_ER[:, n % 2, :], cc[:, lat], ALU.mult)
                    dve.drain().then_inc(S("ssd_cw"), 1)
                    dve.wait_ge(S("ssd_edec"), n + 1)
                    for s, (a, b, t0, t1) in enumerate(spans):
                        stt(W[:, a:b], W[:, a:b], dtT[:, s, row:row + 1], S_CB[:, d, a:b], ALU.mult, ALU.mult)
                    dve.drain().then_inc(S("ssd_w"), 1)
                    if g < 3 and i in (1, 2, 3, 5, 7, 9):
                        ssd_conv(g + 1, (1, 2, 3, 5, 7, 9).index(i))
                    if i % 4 == 1 and i >= 4:
                        ssd_take(g, i // 4 - 1)
                ssd_take(g, 3)
                dve.drain()
                dve.tensor_tensor(S_Y[:, 4 * g:4 * g + 4, :], S_Y[:, 4 * g:4 * g + 4, :], S_Z[g % 2], ALU.mult)\
                   .then_inc(S("ssd_yz"), 1)
                dve.wait_ge(S("ssd_gstd"), g + 1)
                dve.reciprocal(S_STD, S_STD)
                dve.drain()
                for c in range(4):
                    k = 4 * g + c
                    stt(S_Y[:, k, :], S_Y[:, k, :], col("ssd_norm_g_2", k), S_STD, ALU.mult, ALU.mult)

            def ssd_take(g, pr):
                dve.wait_ge(S("ssd_ymm"), 16 * g + 4 * pr + 4)
                k = 4 * g + pr
                stt(S_Y[:, k, :], S_XC[g % 2][:, pr, lat], col("ssd_d_2", k), mix[:, 2 + pr % 2, 0:T], ALU.mult, ALU.add)\
                    .then_inc(S("ssd_y"), 1)

            def ffn_up(l):
                g = G[f"up{l}"]
                w = 512 if l == 0 else T
                lo = T if l == 0 else 0
                dve.memset(upad_l[:, :, :, :].rearrange("p a b c -> p (a b c)"), 0.0)
                dve.memset(upad_c[:, :, :, :].rearrange("p a b c -> p (a b c)"), 0.0)
                dve.drain().then_inc(S("up_zero"), 1)

                def gated(par, k, count):
                    dve.wait_ge(S("up_silu"), count)
                    dve.tensor_tensor(hid[:, k, 0:w], uconv[:, par, 0:2, 0:w], uconv[:, par, 2:4, 0:w], ALU.mult)
                    dve.drain().then_inc(S("up_used"), 1)

                def body(it, u):
                    if u % 2 == 0:
                        return
                    par = u // 2
                    dve.wait_ge(S("up_raw"), it * 2 + (11 * l + par + 1))
                    for tap in (0, 1, 2, 3, 5, 6, 7, 8):
                        dr, dc = tap // 3, tap % 3
                        for half in range(2):
                            for j in range(2):
                                c = 2 * half + j
                                tapw = ffn_tap(l, it, tap, half, j, par)
                                pad = upad_l[:, par, c, :].rearrange("p (r w) -> p r w", r=GRID_ROWS + 2)
                                out = uconv[:, par, c, lo:lo + T].rearrange("p (r w) -> p r w", r=GRID_ROWS)
                                dve.eng.scalar_tensor_tensor(out=out, in0=pad[:, dr:dr + 4, dc:dc + 64], scalar=tapw, in1=out, op0=ALU.mult, op1=ALU.add)
                                if l == 0 and dr == 1:
                                    oc = uconv[:, par, c, 0:T]
                                    dve.eng.scalar_tensor_tensor(out=oc, in0=upad_c[:, par, c, dc:dc + T], scalar=tapw, in1=oc, op0=ALU.mult, op1=ALU.add)
                        dve.drain()
                        if tap == 3 and not (isinstance(it, int) and it == 0 and par == 0):
                            k = slice(2 * par - 2, 2 * par) if isinstance(it, int) and it == 0 else bass.ds(it * 4 + (2 * par - 2), 2)
                            gated(1 - par, k, it * 2 + (11 * l + par))
                    dve.drain().then_inc(S("up_conv"), 1)

                groups(dve, g, body, peel=True)
                gated(0, slice(20, 22), 11 * l + 11)
                dve.drain().then_inc(S("ffn_hid"), 1)

            def add_branch(g, gate, streams):
                for u in range(g.n // g.ppa):
                    for j in range(2):
                        k = 2 * u + j
                        if len(streams) == 2 or j == 0:
                            b = wait_ready(dve, g, 0, u, j if len(streams) == 2 else 0)
                        for v in streams:
                            t = lat if v == 0 else slice(0, T)
                            src = acc[b][:, t] if len(streams) == 2 else acc[b][:, j * T:j * T + T]
                            i = stt(X[:, k, t], src, gate[:, k, v:v + 1], X[:, k, t], ALU.mult, ALU.add)
                        if len(streams) == 2 or j == 1:
                            i.then_inc(free[b], 1)
                dve.drain()

            dve.memset(ones_d[:, :], 1.0 / D)
            dve.memset(ones_h[:, :], 1.0 / P)
            dve.wait_ge(S("loaded"), 96)
            lb = [cols[:, COL["hgrn_lb"] + 4 * i:COL["hgrn_lb"] + 4 * i + 4] for i in range(DEPTH)]
            dve.tensor_tensor(small[:, 8:12], lb[0], lb[1], ALU.max)
            dve.drain()
            for i in range(DEPTH):
                dve.tensor_tensor(small[:, 4 * i:4 * i + 4], lb[i], small[:, 8:12], ALU.subtract)
            dve.drain().then_inc(S("lb_diff"), 1)
            dve.tensor_scalar(negid16[:, :], ident[0:16, 0:16], -1.0, None, ALU.mult)
            dve.wait_ge(S("lb_exp"), 1)
            dve.tensor_tensor(small[:, 8:12], small[:, 0:4], small[:, 4:8], ALU.add)
            dve.drain()
            dve.reciprocal(small[:, 8:12], small[:, 8:12])
            dve.drain()
            for i in range(DEPTH):
                dve.tensor_tensor(small[:, 4 * i:4 * i + 4], small[:, 4 * i:4 * i + 4], small[:, 8:12], ALU.mult)
            dve.memset(one_lb[:, 0, :], 0.0)
            dve.drain()
            dve.tensor_tensor(one_lb[:, 1, :], small[:, 0:4], small[:, 4:8], ALU.add)
            dve.drain()
            dve.tensor_tensor(one_lb[:, 1, :], one_lb[:, 1, :], small[:, 0:4], ALU.subtract)
            dve.drain()
            dve.tensor_scalar(one_lb[:, :, :], one_lb[:, :, :], -1.0, 1.0, ALU.mult, ALU.add)
            for l in range(DEPTH):
                b3 = cols[:, COL["b_ada"] + 72 * l:COL["b_ada"] + 72 * l + 72].rearrange("p (j w) -> p j w", j=3)
                dve.tensor_scalar(b3[:, :, 8:24], b3[:, :, 8:24], 1.0, None, ALU.add)
            dve.drain()
            dve.wait_ge(S("cond_ready"), 1)
            for i in range(HEAD):
                cond_weigh("head", i, i % 2)
            cond_take("head")
            stage_end(dve, count)
            n = 0
            for l in range(DEPTH):
                modulated(l, 0)
                for f in range(2):
                    if f == 1:
                        modulated(l, 1)
                        if l == 0:
                            dve.wait_ge(S("bias_flip"), 1)
                            dve.tensor_tensor(biasC[:, :, :], mix[:, 0:2, :].rearrange("p a (b t) -> p (a b) t", b=2), bc(const("causal"), 4), ALU.add)
                        for i in range(CARRY[f"mix{l}"][1]):
                            cond_weigh(f"mix{l}", i, i % 2)
                        cond_take(f"mix{l}")
                        dve.memset(apad[:, :, 0:PAD], 0.0)
                        stage_end(dve, count)
                        pool(l)
                        stage_end(dve, count)
                        attention(l)
                        stage_end(dve, count)
                        hgrn(l)
                        stage_end(dve, count)
                        branch(l)
                        stage_end(dve, count)
                        residual(G[f"mixout{l}"], l, 24 + 16)
                        layer_norm(n)
                        n += 1
                        stage_end(dve, count)
                        modulated(l, 2)

                    def gate_up(it, u, g=G[f"in{l}{f}"]):
                        for i, e in carried(g.name, it, u):
                            cond_weigh(g.name, i, e)
                        if u % 2 == 0:
                            return
                        b = wait_ready(dve, g, it, u)
                        a = g.a0 + u - 1
                        dve.wait_ge(free[a % BANKS], it + (a // BANKS + 1))
                        k = bass.ds(it * 4 + u - 1, 2)
                        h = hid_raw[:, k, :]
                        dve.tensor_tensor(h, h, acc[b][:, :].rearrange("p (a t) -> p a t", a=2), ALU.mult).then_inc(free[b], 1)
                        dve.tensor_copy(hid_hi[:, k, :], h)
                        dve.tensor_tensor(hid_lo[:, k, :], h, hid_hi[:, k, :], ALU.subtract)

                    groups(dve, G[f"in{l}{f}"], gate_up)
                    dve.drain().then_inc(S("hid_ready"), 1)
                    cond_take(f"in{l}{f}")
                    for i in range(CARRY.get(f"out{l}{f}", (0, 0))[1]):
                        cond_weigh(f"out{l}{f}", i, i % 2)
                    residual(G[f"out{l}{f}"], l, 48 * f + 16)
                    if f"out{l}{f}" in CARRY:
                        cond_take(f"out{l}{f}")
                    layer_norm(n)
                    n += 1
                    stage_end(dve, count)
            rms = 0
            for l in range(DEPTH):
                mod2 = mods2[:, l, :, :]

                def gains(name, s0):
                    for v in range(2):
                        stt(gain2[:, :, v], mod2[:, s0:s0 + 8, v], 1.0, cols[:, COL[name] + 8 * l:COL[name] + 8 * l + 8], ALU.add, ALU.mult)
                    dve.drain()

                gains("norm_mix_g_2", 8)
                if l == 0:
                    dve.memset(ones_g, 1.0 / 512)
                by = lambda k, v: gain2[:, k, v:v + 1]
                rms_norm(rms, both, by, mod2[:, 0:8, :], (0, 1))
                rms += 1
                stage_end(dve, count)
                if l == 0:
                    for i in range(MOD):
                        cond_weigh("even", i, i % 2)
                    cond_take("even")
                    stage_end(dve, count)
                    gla()
                    stage_end(dve, count)
                    mlstm()
                    stage_end(dve, count)
                    add_branch(G["evenout"], mod2[:, 16:24, :], (0, 1))
                else:
                    ssd_rates()
                    stage_end(dve, count)
                    for q in range(6):
                        ssd_conv(0, q)
                    for g in range(4):
                        ssd_group(g)
                    stage_end(dve, count)
                    add_branch(G["ssdout"], mod2[:, 16:24, :], (0,))
                gains("norm_ffn_g_2", 32)
                stage_end(dve, count)
                streams = (0, 1) if l == 0 else (0,)
                rms_norm(rms, both if l == 0 else lat, by, mod2[:, 24:32, :], streams)
                rms += 1
                stage_end(dve, count)
                ffn_up(l)
                add_branch(G[f"down{l}"], mod2[:, 40:48, :], streams)
                stage_end(dve, count)
            rms_norm(rms, lat, lambda k, v: col("final_norm_g_2", k), None, (0,))
            dve.drain().then_inc(S("final"), 1)


def bucket_of(dist):
    if dist < 16:
        return dist
    large = 16 + int(np.float32(np.log(np.float32(dist) / np.float32(16)) / np.log(128 / 16)) * np.float32(16))
    return min(large, 31)


def constants():
    c = np.zeros((P, NCST), np.float32)

    def put(name, v, off=0):
        c[:v.shape[0], CST[name] + off:CST[name] + off + v.shape[1]] = v

    i = np.arange(P)
    s, t = i[:, None], i[None, :]
    put("ident", (s == t).astype(np.float32))
    put("flip", (s + t == P - 1).astype(np.float32))
    for lv in range(NLEV):
        m = 1 << lv
        f = ((s // (2 * m) == t // (2 * m)) & (s // m % 2 == 0) & (t // m % 2 == 1)).astype(np.float32)
        put("tree_f", f, lv * P)
        put("tree_b", f.T, lv * P)
    j = np.arange(T)[None, :]
    put("causal", np.where(P + s - j < 0, NEG, 0).astype(np.float32))
    for d in range(2):
        for par in range(2):
            ok = j <= P * par + s if d == 0 else j >= P * par + s
            put("mneg", np.where(ok, 0, MASKED).astype(np.float32), (2 * d + par) * T)
    put("tri", (t >= s).astype(np.float32))
    put("tri", (t <= s).astype(np.float32), P)
    for c_ in range(2):
        w = np.array([POOL_WINDOWS[2 * c_ + h] for h in range(2)]).repeat(64)[:, None]
        put("invcnt", (1.0 / np.minimum(j + 1, w)).astype(np.float32), c_ * T)
    dist = np.maximum(T - 1 - np.arange(384), 0)
    put("onehot", (np.arange(32)[:, None] == np.array([bucket_of(int(x)) for x in dist])[None, :]).astype(np.float32))
    put("eps", np.array([[LN_EPS, RMS_EPS, 1.0]], np.float32).repeat(P, 0))
    put("eps", ((i >= 8) & (i < 16)).astype(np.float32)[:, None], 3)
    return c


def panels(w, starts):
    k = w.shape[0]
    out = np.zeros((len(starts), P, k // P, PANEL), w.dtype)
    for n, a in enumerate(starts):
        b = w[:, a:a + PANEL]
        out[n, :, :, :b.shape[1]] = b.reshape(k // P, P, -1).transpose(1, 0, 2)
    return out.reshape(len(starts), P, -1)


def down_panels(w, rows):
    out = [panels(w[r:r + rows], [a]) for a in range(0, w.shape[1], PANEL) for r in range(0, w.shape[0], rows)]
    return np.concatenate(out)


def custom_panel(pieces):
    out = np.zeros((1, P, KD, PANEL), np.float32)
    for w, at in pieces:
        out[0, :, :, at:at + w.shape[1]] = w.reshape(KD, P, -1).transpose(1, 0, 2)
    return out.reshape(1, P, -1)


def weight_stream(x):
    w8, w11, wc = [], [], []
    step = lambda a, n: [a + PANEL * i for i in range(n)]
    for l in range(DEPTH):
        wc.append(panels(x["w_ada"][l], step(0, ADA)))
        pairs = [c for i in range(11) for c in (PANEL * i, D_FF + PANEL * i)]
        m = x["mix_w_in"][l]
        for f in range(2):
            if f == 1:
                w8.append(panels(m, [0, 256, 512, 1024, 1280]))
                w8.append(custom_panel([(m[:, 1536:1600], 0), (m[:, 1536:1600], 64), (m[:, 1600:1608], 128)]))
                w8.append(panels(m, [768, 2632, 2888, 1608, 1864, 3144, 3400, 2120, 2376] + step(3656, 12)))
                w8.append(panels(x["w_branch"][l], step(0, 4)))
                w8.append(panels(x["w_out"][l], step(0, 4)))
            w8.append(panels(x["ffn_w_in"][l, f], pairs))
            w11.append(down_panels(x["ffn_w_out"][l, f], KSPLIT * P))
    for l in range(DEPTH):
        wc.append(panels(x["mod_w_2"][l], step(0, MOD)))
        if l == 0:
            e = x["even_w_in_2"][0]
            w8.append(panels(e, step(0, 14)))
            w8.append(custom_panel([(e[:, 3584:3600], 0), (x["gla_a1_2"][0, 0], 32), (x["gla_a1_2"][0, 1], 64)]))
            w8.append(panels(x["even_w_out_2"][0], step(0, 4)))
        else:
            o = x["ssd_w_in_2"][0]
            w8.append(custom_panel([(o[:, 5120:5184], 0)]))
            for g in range(4):
                w8.append(panels(o, step(2048 + 512 * g, 2)))
                w8.append(custom_panel([(o[:, 4096 + P * g:4096 + P * g + P], 0), (o[:, 4608 + P * g:4608 + P * g + P], P)]))
                w8.append(panels(o, step(512 * g, 2)))
            w8.append(down_panels(x["ssd_w_out_2"][0], KD * P))
        w8.append(panels(x["ffn_w_up_2"][l], pairs))
        w11.append(down_panels(x["ffn_w_down_2"][l], KSPLIT * P))
    return np.concatenate(w8), np.concatenate(w11), np.concatenate(wc)


def vectors(x):
    c = np.zeros((P, NCOL), np.float32)
    for name, n in COL_SPEC:
        v = x[name].reshape(-1)
        if name == "ssd_d_2":
            v = v.repeat(64)
        if n == 1:
            c[:v.size, COL[name]] = v
        else:
            c[:, COL[name]:COL[name] + n] = v.reshape(n, P).T
    return c


def kernel(**inputs):
    import concourse.bacc as bacc
    from concourse.bass_utils import run_bass_kernel_spmd

    x = {k: np.asarray(v) for k, v in inputs.items()}
    arrays = {}
    arrays["w8"], arrays["w11"], arrays["wc"] = weight_stream(x)
    arrays["consts"] = constants()
    arrays["cols"] = vectors(x)
    arrays["xs"] = np.ascontiguousarray(np.concatenate([x["ctx_2"][0].T, x["x"][0].T], axis=1))
    pw = np.zeros((P, DEPTH, 2, P), np.float32)
    for g in range(4):
        r = slice(64 * (g % 2), 64 * (g % 2) + 64)
        pw[r, :, g // 2, r] = x["pool_w"][:, g].transpose(1, 0, 2)
    arrays["poolw"] = pw
    a2 = np.zeros((64, T), np.float32)
    a2[0:16], a2[32:48] = x["gla_a2_2"][0, 0], x["gla_a2_2"][0, 1]
    arrays["a2w"] = a2
    arrays["rel_bias"] = np.ascontiguousarray(x["rel_bias"][:, [0, 2, 1, 3]])
    nc = bacc.Bacc("TRN2", target_bir_lowering=False, num_devices=1)
    io = {}
    for name, a in arrays.items():
        io[name] = nc.dram_tensor(name, a.shape, mybir.dt.from_np(a.dtype), kind="ExternalInput").ap()
    io["out"] = nc.dram_tensor("out", (D, T), F32, kind="ExternalOutput").ap()
    program(nc, io)
    r = run_bass_kernel_spmd(nc, [arrays], core_ids=[0])
    return np.ascontiguousarray(r.results[0]["out"].T)[None]
```

```python
from contextlib import ExitStack

import concourse.bass as bass
from concourse import mybir
import numpy as np

F32 = mybir.dt.float32
F32R = mybir.dt.float32r
ALU = mybir.AluOpType
ACT = mybir.ActivationFunctionType
AXX = mybir.AxisListType.X

P = 128
T = 256
D = 1024
KD = D // P
DEPTH = 2
D_FF = 2816
KF = D_FF // P
PANEL = 256
KSPLIT = KF // 2
SLOTS = BANKS = 4
SLOT_W = KSPLIT * PANEL
ALPHA = (2 * DEPTH) ** 0.25
LN_EPS, RMS_EPS = 1e-5, 1e-6
KEY_MAX = 1.0 - 1e-6
TOPK = 64
IDX_SCALE = (64 ** -0.5) * (8 ** -0.5)
NEG = -3.0e38
GONE = -3.3e38
MASKED = -1.0e30
POOL_WINDOWS = (2, 4, 8, 16)
PAD = 16
NLEV = 7
GRID_ROWS, GRID_W = 4, 64
LATPAD = (GRID_ROWS + 2) * (GRID_W + 2)
CTXPAD = T + 2

COL_SPEC = [("c", 8), ("b_ada", 2 * 72), ("ln_g", 48), ("ln_b", 48), ("pool_scale", 4), ("hgrn_lb", 8),
            ("hgrn_norm_g", 8), ("c_2", 8), ("c_ctx_2", 8), ("mod_b_2", 96), ("norm_mix_g_2", 16),
            ("norm_ffn_g_2", 16), ("final_norm_g_2", 8), ("ffn_conv_w_2", 2 * 9 * 44), ("ffn_conv_b_2", 88),
            ("gla_ab_2", 4), ("ml_conv_w_2", 24), ("ml_conv_b_2", 8), ("ml_gate_b_2", 1), ("gla_norm_g_2", 4),
            ("ml_norm_g_2", 4), ("ssd_conv_w_2", 72), ("ssd_conv_b_2", 24), ("ssd_dt_bias_2", 1),
            ("ssd_a_log_2", 1), ("ssd_d_2", 16), ("ssd_norm_g_2", 16)]
COL = {}
NCOL = 0
for _name, _n in COL_SPEC:
    COL[_name] = NCOL
    NCOL += _n

CONST_SPEC = [("ident", 128), ("flip", 128), ("tree_f", NLEV * 128), ("tree_b", NLEV * 128), ("causal", 256),
              ("mneg", 4 * 256), ("tri", 256), ("invcnt", 512), ("onehot", 384), ("eps", 4)]
CST = {}
NCST = 0
for _name, _n in CONST_SPEC:
    CST[_name] = NCST
    NCST += _n


class InOrder:

    def __init__(self, eng):
        self.eng = eng
        self.wait_ge, self.drain, self.Fori = eng.wait_ge, eng.drain, eng.Fori

    def activation(self, *a, **k):
        i = self.eng.activation(*a, **k)
        self.eng.drain()
        return i

    def tensor_scalar(self, *a, **k):
        i = self.eng.tensor_scalar(*a, **k)
        self.eng.drain()
        return i

    def tensor_tensor(self, *a, **k):
        i = self.eng.tensor_tensor(*a, **k)
        self.eng.drain()
        return i

    def scalar_tensor_tensor(self, *a, **k):
        i = self.eng.scalar_tensor_tensor(*a, **k)
        self.eng.drain()
        return i

    def tensor_copy(self, *a, **k):
        i = self.eng.tensor_copy(*a, **k)
        self.eng.drain()
        return i

    def tensor_reduce(self, *a, **k):
        i = self.eng.tensor_reduce(*a, **k)
        self.eng.drain()
        return i

    def tensor_tensor_scan(self, *a, **k):
        i = self.eng.tensor_tensor_scan(*a, **k)
        self.eng.drain()
        return i

    def reciprocal(self, *a, **k):
        i = self.eng.reciprocal(*a, **k)
        self.eng.drain()
        return i

    def memset(self, *a, **k):
        i = self.eng.memset(*a, **k)
        self.eng.drain()
        return i

    def max(self, *a, **k):
        i = self.eng.max(*a, **k)
        self.eng.drain()
        return i

    def match_replace(self, *a, **k):
        i = self.eng.match_replace(*a, **k)
        self.eng.drain()
        return i


class Gemm:

    def __init__(self, name, panels, accs_per_panel=1, wide=False, panels_per_acc=1, split=False, kept=False, ahead=1):
        self.name, self.n, self.apa, self.wide, self.ppa = name, panels, accs_per_panel, wide, panels_per_acc
        self.split = split
        self.parts = [(n + m, part) for n in range(0, panels // 2, ahead) for part in range(2) for m in range(ahead)]
        self.kept = kept


def plan():
    order = []
    for l in range(DEPTH):
        order += [Gemm(f"in{l}0", 22, split=True), Gemm(f"out{l}0", 8, wide=True, panels_per_acc=2, split=True),
                  Gemm(f"mix{l}", 15), Gemm(f"gate{l}", 12), Gemm(f"branch{l}", 4, 3), Gemm(f"mixout{l}", 4),
                  Gemm(f"in{l}1", 22, split=True), Gemm(f"out{l}1", 8, wide=True, panels_per_acc=2, split=True)]
    for l in range(DEPTH):
        both = 2 if l == 0 else 1
        if l == 0:
            order += [Gemm("evengate", 1, split=True, kept=True), Gemm("even", 14, 2, split=True, kept=True), Gemm("evenout", 4, 2)]
        else:
            order += [Gemm("dt", 1)]
            for g in range(4):
                order += [Gemm(f"ssdx{g}", 2, 2), Gemm(f"ssdbc{g}", 1, 2), Gemm(f"ssdz{g}", 2)]
            order += [Gemm("ssdout", 8, panels_per_acc=2)]
        order += [Gemm(f"up{l}", 22, both, split=(l == 0), kept=(l == 0)), Gemm(f"down{l}", 8, both, wide=True, panels_per_acc=2, ahead=BANKS // both)]
    p = a = splits = 0
    row = {False: 0, True: 0}
    finished = []
    halves = 0
    for g in order:
        g.p0, g.a0, g.row0, g.s0, g.h0 = p, a, row[g.wide], splits, halves
        row[g.wide] += g.n
        for i in range(g.n):
            n, part = g.parts[i] if g.ppa == 2 else (i, 1)
            if part == 0:
                halves += 1
            last = a + g.apa * (n + 1) - 1
            if g.split:
                splits += 1
            if g.split and not g.kept:
                finished.append(("low_made", 0, 2 * splits))
            elif part == 0:
                finished.append(("half_read", 0, halves))
            else:
                finished.append(("ready", last % BANKS, last // BANKS + 1))
        p += g.n
        a += g.n // g.ppa * g.apa
    return {g.name: g for g in order}, order, finished, row


ADA, MOD = 36, 24
MOD0 = DEPTH * ADA
HEAD = 8
CARRY = {"head": (0, HEAD), "in00": (8, 11), "out00": (19, 6), "mix0": (25, 15), "in01": (40, 11), "out01": (51, 6),
         "in10": (57, 11), "out10": (68, 4), "mix1": (72, 13), "in11": (85, 11), "out11": (96, 7),
         "evenout": (103, 3), "down0": (106, 14)}


LATER = {"evenout": 1, "down0": 2}


def carried(phase, it, u):
    if phase not in CARRY:
        return []
    if phase[:2] == "in":
        units = [(it * 2 + u // 2, u // 2)] if u % 2 == 1 else []
    elif phase in ("evenout", "down0"):
        i = u - LATER[phase]
        units = [(i, i % 2)] if i >= 0 else []
    else:
        units = [(it * 4 + u, u % 2)]
    return [(i, e) for i, e in units if not isinstance(it, int) or i < CARRY[phase][1]]


def program(nc, io):
    G, order, finished, _ = plan()
    w8, w11, wc = io["w8"], io["w11"], io["wc"]
    with ExitStack() as ctx:
        def sb(name, shape):
            return ctx.enter_context(nc.sbuf_tensor(name, shape, F32))

        def sem(name):
            return ctx.enter_context(nc.semaphore(name))

        def sb_r(name, shape):
            with nc.sbuf_tensor(name, shape, F32R) as t:
                return t

        slots, slots_r = [], []
        for i in range(SLOTS):
            slots_r.append(sb_r(f"panel{i}_r", [P, SLOT_W]))
            slots.append(sb(f"panel{i}", [P, SLOT_W]))
        X = sb("residual", [P, KD, 2 * T])
        H_r = sb_r("normed_r", [P, KD, 2 * T])
        H = sb("normed", [P, KD, 2 * T])
        cst_r = sb_r("constants_r", [P, NCST])
        cst = sb("constants", [P, NCST])
        cols = sb("vectors", [P, NCOL])
        mods1 = sb("mods1", [P, DEPTH, 72])
        mods2 = sb("mods2", [P, DEPTH, 48, 2])
        cond_slot1_r = sb_r("cond_panel1_r", [P, KD, PANEL])
        cond_slot1 = sb("cond_panel1", [P, KD, PANEL])
        gain2 = sb("gain2", [P, KD, 2])
        cond = sb("cond", [P, KD])
        cond2 = sb("cond2", [P, KD, 2])
        ones_d = sb("ones_d", [P, P])
        ones_h = sb("ones_h", [P, P])
        biasC_r = sb_r("bias_causal_r", [P, 4, T])
        biasC = sb("bias_causal", [P, 4, T])
        poolw = sb("pool_blocks", [P, DEPTH, 2, P])
        relb = sb("rel_table", [32, 4])
        one_lb = sb("one_minus_lb", [P, DEPTH, 4])
        std = sb("std", [P, 2 * T])
        small = sb("small", [P, 64])
        AW = 22656
        arena_r = sb_r("arena_r", [P, AW])
        arena = sb("arena", [P, AW])
        accs = ctx.enter_context(nc.psum_tensor("accs", [P, BANKS, 512], F32))
        acc = [accs[:, i, :] for i in range(BANKS)]
        mix = ctx.enter_context(nc.psum_tensor("mix", [P, 4, 512], F32))
        zrow_d = nc.dram_tensor("bias_rows", [4, 384], F32, kind="Internal")

        def region(off, *dims, of=arena):
            n = int(np.prod(dims))
            assert off + n <= AW, (off, n)
            v = of[:, off:off + n]
            if len(dims) == 2:
                v = v.rearrange("p (a b) -> p a b", a=dims[0])
            if len(dims) == 3:
                v = v.rearrange("p (a b c) -> p a b c", a=dims[0], b=dims[1])
            if len(dims) == 4:
                v = v.rearrange("p (a b c d) -> p a b c d", a=dims[0], b=dims[1], c=dims[2])
            return v

        def const(name, off=0, n=None):
            return cst[:, CST[name] + off:CST[name] + off + (n or dict(CONST_SPEC)[name])]

        def col(name, i, p0=0, p1=P):
            return cols[p0:p1, COL[name] + i:COL[name] + i + 1]

        ident = const("ident")
        a2w = const("onehot")[:, 0:T]
        eps_ln, eps_rms, one_col = (const("eps", i, 1) for i in range(3))
        lat = slice(T, 2 * T)
        both = slice(0, 2 * T)
        cond_slot0 = {"evenout": region(4096, KD, PANEL), "down0": region(11264, KD, PANEL)}

        def cond_slot(phase, slot):
            return cond_slot1[:, :, :] if slot == 1 else cond_slot0.get(phase, H[:, :, 0:T])

        cond_part = [[const("mneg", PANEL * (2 * v + i), PANEL) for i in range(2)] for v in range(2)]
        hid = region(0, KF, 2 * T)
        squares = region(0, KD, 2 * T)
        hid_hi, hid_lo = region(0, KF, T, of=arena_r), region(KF * T, KF, T, of=arena_r)
        hid_raw = region(KF * T, KF, T)
        h_hi, h_lo, h_raw = H_r[:, :, T:2 * T], region(2 * KF * T, KD, T, of=arena_r), region(2 * KF * T, KD, T)
        SPLIT = 2 * KF * T + KD * T
        up_hi = [region(SPLIT + i * KD * P, KD, P, of=arena_r) for i in range(4)]
        up_lo = [region(SPLIT + (4 + i) * KD * P, KD, P, of=arena_r) for i in range(4)]
        down_hi = [region(SPLIT + i * KSPLIT * P, KSPLIT, P, of=arena_r) for i in range(4)]
        down_lo = [region(SPLIT + (4 + i) * KSPLIT * P, KSPLIT, P, of=arena_r) for i in range(2)]
        apad = region(0, 2, PAD + T)
        qT, kT, qiT, kiT = region(544, 2, T), region(1056, 2, T), region(1568, 4, T), region(2592, T)
        vt, wi = region(2848, 2, T), region(3360, 2, 8)
        hi, qf, kk, hgs = region(3376, 2, 512), region(4400, 4, T), region(5424, 4, T), region(6448, 4, T)
        gates = region(7472, 24, T)
        ymix = region(13616, KD, T)
        TMP = 15664
        win = [region(TMP + 544 * i, 2, PAD + T) for i in range(4)]
        pdiff = region(TMP + 2176, 2, T)
        relu_s = region(TMP, 8, T)
        bias_rows = region(SPLIT + 6 * KSPLIT * P, 384)
        score, work, addm = region(TMP + 2048, T), region(TMP + 2304, T), region(TMP + 2560, T)
        logit = region(TMP + 2816, 2, 4, T)
        probT = region(TMP + 4864, 2, 8, P)
        pref, suff = region(TMP, 4 * T), region(TMP + 1024, 4 * T)
        treeX = [region(TMP + 2048 + 1024 * i, 4 * T) for i in range(2)]
        pairs, offd, ptmp = region(TMP + 4096, 8, P), region(TMP + 5120, 4, P), region(TMP + 5632, 8, P)
        osq, onorm, ostd = region(TMP + 2048, 4 * T), region(TMP, 4, T), region(TMP + 1024, 4 * T)
        merged, mtmp = region(TMP, KD, T), region(TMP + 2048, 2, T)
        E_Q, E_K, E_V, E_MQ, E_MV, E_Y, E_T = 0, 1024, 2048, 4096, 8192, 10240, 14336
        gq, gk, gv = region(E_Q, 2, 512), region(E_K, 2, 512), region(E_V, 4, 512)
        mqk, mv = region(E_MQ, 8, 512), region(E_MV, 4, 512)
        ey = region(E_Y, 8, 512)
        logd = H[:, 0:4, :].rearrange("p a t -> p (a t)").rearrange("p (d n) -> p d n", d=2)
        gpref = logd
        gsuff = H[:, 4:8, :].rearrange("p a t -> p (a t)").rearrange("p (d n) -> p d n", d=2)
        gX = [region(E_T + 1024 * i, 2, 512) for i in range(2)]
        gpairs = region(E_T + 2048, 16, P)
        goff = region(E_T + 4096, 16, P)
        gla_banks = [mix, accs]
        gcross = region(E_T + 6144, 2, 4, T)
        gtmp = region(E_T + 6144, 8, P)
        head_std = region(E_T + 2048, 512)
        mqk_raw = region(E_T + 2048, 8, 512)
        rows16 = biasC[:, 0:2, :].rearrange("p a b -> p (a b)")
        bcol = biasC[:, 2, 0:64].rearrange("p (a b) -> p a b", a=4)
        dcol = biasC[:, 2, 64:96]
        ones_g = biasC[:, 3, 0:P]
        bwd_rows = const("eps", 3, 1)[0:16, :]
        lsg = region(E_T + 6144, 512)[0:16, :]
        cum16 = std[0:16, :]
        tmp16 = region(E_T + 7168, 512)[0:16, :]
        rall = H
        dlogs = [region(E_T, 8, 512), region(0, 8, 512)]
        ln_next = sb("ln_vectors", [P, 4, KD])
        ml_max = sb("ml_maxima", [P, 32])
        psum2 = region(E_T + 4096, 4, 512)
        mprobT = region(E_T + 6144, 4, 512)
        S_X, S_BC = region(0, 4, 512), region(2048, 2, 512)
        S_XC = [region(3072, 4, 512), cond_slot1[:, :, :].rearrange("p a b -> p (a b)").rearrange("p (a b) -> p a b", a=4)]
        S_BCC = [[region(5120, 512), region(5632, 512)], [region(19200, 512), region(20224, 512)]]
        S_Z = [region(6144, 4, T), region(21376, 4, T)]
        S_XT, S_BT = region(7168, 4, 512), region(9216, 2, P)
        S_XW, S_ST = region(9472, 2, 2, 512), region(11520, 2, 512)
        S_Y = region(12544, 16, T)
        S_CB = region(16640, 2, 384)
        S_ER, S_CW = region(17408, 2, T), region(17920, 2, T)
        S_DW = region(18432, 2, 384)
        dtr = region(19200, 512)
        dcum, dwe, dtmp = region(19712, 512), region(20224, T), region(20480, 512)
        dtT, dcT, dwT = region(20992, 2, 64), region(21120, 2, 64), region(21248, 2, 64)
        S_SQ = region(9472, 4, T)
        S_STD = region(22400, T)
        negA = small[0:64, 60:61]
        upad_l = region(11264, 2, 4, LATPAD)
        upad_c = region(11264 + 8 * LATPAD, 2, 4, CTXPAD)
        UC = 11264 + 8 * LATPAD + 8 * CTXPAD
        uconv = region(UC, 2, 4, 512)
        squares2 = region(UC, KD, 2 * T)
        kept_hi = {"evengate": region(E_T, KD, PANEL, of=arena_r), "up0": region(UC + 4096, KD, PANEL, of=arena_r)}
        kept_hi["even"] = kept_hi["evengate"]

        def input_chunks(slot, consts, bias, mem):
            m = CST["mneg"]
            six = [slot[:, 2 * i:2 * i + 2, :].rearrange("p a b -> p (a b)") for i in range(4)] + \
                  [consts[:, m + 512 * i:m + 512 * i + 512] for i in range(2)]
            return [six + [region(E_T + 6656 + 1024 * i, 512, of=mem) for i in range(2)],
                    six + [bias[:, 2 * i:2 * i + 2, :].rearrange("p a b -> p (a b)") for i in range(2)]]

        in_raw, in_lo = input_chunks(cond_slot1, cst, biasC, arena), input_chunks(cond_slot1_r, cst_r, biasC_r, arena_r)

        landed = [sem(f"panel_landed{i}") for i in range(SLOTS)]
        ready = [sem(f"acc_ready{i}") for i in range(BANKS)]
        free = [sem(f"acc_free{i}") for i in range(BANKS)]
        half_read = sem("half_read")
        first_used = sem("first_half_used")
        cond_landed = [sem(f"cond_landed{i}") for i in range(2)]
        stage = sem("stage_end")
        named = {}

        def S(name):
            if name not in named:
                named[name] = sem(name)
            return named[name]


        def ffn_tap(l, it, tap, half, j, par):
            base = COL["ffn_conv_w_2"] + (l * 9 + tap) * 44 + half * 22
            return cols[:, bass.ds(it * 4 + (base + 2 * par + j), 1)]

        def ffn_bias(l, it, half, j, par):
            return cols[:, bass.ds(it * 4 + (COL["ffn_conv_b_2"] + l * 44 + half * 22 + 2 * par + j), 1)]

        def ssd_channel(g, q):
            return 4 * g + q if q < 4 else 16 + 4 * (q - 4) + g

        def cond_bank(phase):
            return 3 if phase[:2] in ("he", "in") else 2

        block = ctx.enter_context(nc.Block())

        def stage_end(eng, count):
            count[0] += 1
            eng.drain().then_inc(stage, 1)
            eng.wait_ge(stage, 3 * count[0])

        def groups(eng, g, body, peel=False):
            first = 0
            if peel or g.p0 < SLOTS:
                for u in range(4):
                    body(0, u)
                first = 1
            with eng.Fori(first, g.n // 4) as it:
                for u in range(4):
                    body(it, u)
            for u in range(g.n % 4):
                body(g.n // 4, u)

        def half_panel(g, u, j, of=slots):
            k = KSPLIT if g.wide else KD
            return of[(g.p0 + u) % SLOTS][:, 0:k * PANEL].rearrange("p (k c) -> p k c", k=k)[:, :, j * P:j * P + P]

        def split_parts(g, u, j):
            if g.kept:
                return kept_hi[g.name][:, :, j * P:j * P + P], half_panel(g, u, j, slots_r)
            return (down_hi[(2 * u + j) % 4], down_lo[j]) if g.wide else (up_hi[(2 * u + j) % 4], up_lo[(2 * u + j) % 4])

        def split_count(g, it, u, j):
            return it * 8 + (2 * (g.s0 + u) + j + 1)

        def wait_used(eng, g, it, u, j):
            if j == 0:
                eng.wait_ge(first_used, it * 4 + (g.s0 + u + 1))
            elif g.ppa == 1:
                a = g.a0 + u
                eng.wait_ge(ready[a % BANKS], it + (a // BANKS + 1))
            elif u % 2 == 0:
                eng.wait_ge(half_read, g.h0 + u // 2 + 1)
            else:
                a = g.a0 + u // 2
                eng.wait_ge(ready[a % BANKS], a // BANKS + 1)

        def wait_ready(eng, g, it, u, r=0):
            a = g.a0 + g.apa * u + r
            eng.wait_ge(ready[a % BANKS], it * g.apa + (a // BANKS + 1))
            return a % BANKS

        @block.sync
        def _(sp):
            m0, m1 = CST["mneg"], CST["tri"]
            def load(g, i, static_i):
                src = (w11 if g.wide else w8)[bass.ds(i + g.row0, 1), :, :].rearrange("a p n -> p (a n)")
                s = (g.p0 + static_i) % SLOTS
                width = SLOT_W if g.wide else KD * PANEL
                sp.dma_start(slots[s][:, 0:width], src).then_inc(landed[s], 16)

            def load_static(g, i):
                p = g.p0 + i
                if p >= SLOTS:
                    kind, b, v = finished[p - SLOTS]
                    sp.wait_ge({"half_read": half_read, "low_made": S("low_made")}.get(kind, ready[b]), v)
                load(g, 2 * g.parts[i][0] + g.parts[i][1] if g.ppa == 2 else i, i)

            def load_cond(phase, it, u):
                for i, e in carried(phase, it, u):
                    n0 = CARRY[phase][0]
                    slot = (n0 + e) % 2
                    if not isinstance(i, int) or i + n0 >= 2:
                        sp.wait_ge(S("cond_part"), i + (n0 - 1))
                    if phase == "evenout" and i == 0:
                        sp.wait_ge(ready[G[phase].a0 % BANKS], G[phase].a0 // BANKS + 1)
                    if phase == "down0" and i == 0:
                        sp.wait_ge(S("up_used"), KF // 2)
                    src = wc[bass.ds(i + n0, 1), :, :].rearrange("a p (k c) -> p (a k) c", k=KD)
                    sp.dma_start(cond_slot(phase, slot), src).then_inc(cond_landed[slot], 16)

            xs = io["xs"].rearrange("(k p) t -> p k t", p=P)
            sp.dma_start(cols[:, :], io["cols"]).then_inc(S("cols_loaded"), 16)
            load_cond("head", 0, 0)
            sp.dma_start(cst[:, m1:NCST], io["consts"][:, m1:NCST]).then_inc(S("consts_loaded"), 16)
            load_cond("head", 0, 1)
            sp.dma_start(poolw[:, :, :, :], io["poolw"]).then_inc(S("loaded"), 16)
            sp.dma_start(relb[:, :], io["rel_bias"]).then_inc(S("loaded"), 16)
            sp.wait_ge(S("consts_loaded"), 16)
            sp.dma_start(a2w[32:96, :], io["a2w"]).then_inc(S("loaded"), 16)
            for i in range(2, HEAD):
                load_cond("head", 0, i)
                if i == 4:
                    sp.dma_start(cst[:, 0:m0], io["consts"][:, 0:m0]).then_inc(S("loaded"), 16)
                if i == 6:
                    sp.dma_start(X[:, :, lat], xs[:, :, lat]).then_inc(S("loaded"), 16)
            for g in order:
                if g.n >= 12 and g.ppa == 1:
                    for i in range(4):
                        load_static(g, i)
                        load_cond(g.name, 0, i)
                    with sp.Fori(1, g.n // 4) as it:
                        for u in range(4):
                            a = g.a0 + g.apa * (u + 1) - 1
                            if g.split and not g.kept:
                                sp.wait_ge(S("low_made"), split_count(g, it, u - SLOTS, 1))
                            else:
                                sp.wait_ge(ready[a % BANKS], it * g.apa + (a // BANKS + 1 - g.apa))
                            load(g, it * 4 + u, u)
                            load_cond(g.name, it, u)
                    for i in range(g.n - g.n % 4, g.n):
                        load_static(g, i)
                        load_cond(g.name, 0, i)
                else:
                    for i in range(g.n):
                        load_static(g, i)
                        if g.name != "down0":
                            load_cond(g.name, 0, i)
                        elif i >= 2:
                            for u in range(2 * i - 2, 2 * i if i + 1 < g.n else 2 * g.n):
                                load_cond(g.name, 0, u)
                if g.name == "even":
                    sp.wait_ge(ready[(g.a0 + 2 * g.n - 1) % BANKS], (g.a0 + 2 * g.n - 1) // BANKS + 1)
                    sp.dma_start(const("mneg"), io["consts"][:, m0:m1]).then_inc(S("masks_loaded"), 16)
                if g.name == "in00":
                    sp.dma_start(X[:, :, 0:T], xs[:, :, 0:T]).then_inc(S("context_loaded"), 16)
                    sp.wait_ge(S("bias_rows"), 1)
                    sp.dma_start(zrow_d.ap(), bias_rows[0:4, :]).then_inc(S("bias_stored"), 16)
                    sp.wait_ge(S("bias_stored"), 16)
                    sp.dma_start(biasC[:, :, :],
                                 bass.AP(zrow_d, 0, [[1, P], [384, 4], [1, T]])).then_inc(S("hankel"), 16)
            sp.wait_ge(S("final"), 1)
            sp.dma_start(io["out"].rearrange("(k p) t -> p k t", p=P), H[:, :, lat]).then_inc(S("stored"), 16)
            sp.wait_ge(S("stored"), 16)

        @block.tensor
        def _(pe):
            count = [0]

            def panel_in(g, it, u):
                s = (g.p0 + u) % SLOTS
                pe.wait_ge(landed[s], it * 16 + 16 * ((g.p0 + u) // SLOTS + 1))
                return slots[s]

            def acc_open(g, it, u, r=0):
                a = g.a0 + g.apa * u + r
                if a >= BANKS or not isinstance(it, int) or it > 0:
                    pe.wait_ge(free[a % BANKS], it * g.apa + a // BANKS)
                return a % BANKS

            def input_chunk(n, k):
                pe.wait_ge(S("rms_out"), n * KD + k + 1)

            def features(g, it, u, rhs, ntok, norm=None, js=range(2)):
                w = panel_in(g, it, u)
                for j in js:
                    r = j if ntok == 512 else 0
                    if j == js[0] or ntok == 512:
                        b = acc_open(g, it, u, r)
                    o = 0 if ntok == 512 else j * ntok
                    for k in range(KD):
                        if norm is not None and j == 0 and isinstance(it, int) and it == 0 and u == 0:
                            input_chunk(norm, k)
                        mm = pe.matmul(acc[b][:, o:o + ntok], w[:, k * PANEL + j * P:k * PANEL + j * P + P], rhs(k),
                                       start=(k == 0), stop=(k == KD - 1))
                    if j == 1 or ntok == 512:
                        mm.then_inc(ready[b], 1)

            def split_half(g, it, u, j, out, src_hi, src_lo, clear, last, done, h=None, norm=None, m=P):
                pe.wait_ge(S("low_made"), split_count(g, it, u, j))
                hi, lo = split_parts(g, u, j)
                n = hi.shape[1]
                for k in range(n):
                    if h is not None:
                        pe.wait_ge(S("h_ready"), h * KD + k + 1)
                    if norm is not None:
                        input_chunk(norm, k)
                    pe.matmul(out, hi[:, k, 0:m], src_hi(k), start=clear and k == 0, stop=False, skip_group_check=True)
                    pe.matmul(out, hi[:, k, 0:m], src_lo(k), start=False, stop=False, skip_group_check=True)
                    mm = pe.matmul(out, lo[:, k, 0:m], src_hi(k), start=False, stop=last and k == n - 1, skip_group_check=True)
                mm.then_inc(done, 1)

            def split_up(g, it, u, h):
                first = isinstance(it, int) and it == 0 and u == 0
                b = acc_open(g, it, u)
                for j in range(2):
                    split_half(g, it, u, j, acc[b][:, j * T:j * T + T], lambda k: h_hi[:, k, :], lambda k: h_lo[:, k, :],
                               j == 0, True, (first_used, ready[b])[j], h if first and j == 0 else None)

            def kept_features(g, it, u, norm):
                first = norm == 1 and isinstance(it, int) and it == 0 and u == 0
                for j in range(2):
                    b = acc_open(g, it, u, j)
                    split_half(g, it, u, j, acc[b], lambda k: H_r[:, k, :], lambda k: in_lo[norm][k], True, True, ready[b],
                               norm=norm if first and j == 0 else None)

            def kept_tokens(g, u):
                hi, lo = kept_hi[g.name], slots_r[(g.p0 + u) % SLOTS]
                pe.wait_ge(S("high_made"), split_count(g, 0, u, 1))
                banks = [acc_open(g, 0, u, r) for r in range(2)]
                out = [acc[banks[tb // 2]][:, tb % 2 * T:tb % 2 * T + T] for tb in range(4)]
                for tb in range(4):
                    t = slice(tb * P, tb * P + P)
                    for k in range(KD):
                        pe.matmul(out[tb], H_r[:, k, t], hi[:, k, :], start=(tb % 2 == 0 and k == 0), stop=False, skip_group_check=True)
                        mm = pe.matmul(out[tb], in_lo[0][k][:, t], hi[:, k, :], start=False, stop=False, skip_group_check=True)
                mm.then_inc(first_used, 1)
                pe.wait_ge(S("low_made"), split_count(g, 0, u, 1))
                for tb in range(4):
                    for k in range(KD):
                        mm = pe.matmul(out[tb], H_r[:, k, tb * P:tb * P + P], lo[:, k * PANEL:k * PANEL + PANEL],
                                       start=False, stop=(k == KD - 1), skip_group_check=True)
                    if tb % 2 == 1:
                        mm.then_inc(ready[banks[tb // 2]], 1)

            def split_down(g):
                for i in range(g.n):
                    a, part = g.a0 + i // 2, i % 2
                    b = a % BANKS
                    if part == 0:
                        pe.wait_ge(free[b], a // BANKS)
                    for j in range(2):
                        split_half(g, 0, i, j, acc[b][:, j * T:j * T + T],
                                   lambda k: hid_hi[:, part * KSPLIT + k, :], lambda k: hid_lo[:, part * KSPLIT + k, :],
                                   part == 0 and j == 0, part == 1, (first_used, ready[b] if part else half_read)[j])
                    cond_sum(g.name, 0, i)

            def tokens(g, u, lo, nblk, ncol=PANEL, off=0):
                w = panel_in(g, 0, u)
                for tb in range(nblk):
                    if tb % 2 == 0:
                        b = acc_open(g, 0, u, tb // 2)
                    for k in range(KD):
                        mm = pe.matmul(acc[b][:, tb % 2 * T:tb % 2 * T + ncol], H[:, k, lo + tb * P:lo + tb * P + P],
                                       w[:, k * PANEL + off:k * PANEL + off + ncol], start=(k == 0), stop=(k == KD - 1))
                    if tb % 2 == 1:
                        mm.then_inc(ready[b], 1)

            def cond_sum(phase, it, u):
                for i, e in carried(phase, it, u):
                    n0 = CARRY[phase][0]
                    pe.wait_ge(S("cond_part"), i + (n0 + 1))
                    for v in range(2 if n0 >= MOD0 else 1):
                        for j in range(2):
                            c = i * 2 + (T * v + j)
                            mm = pe.matmul(mix[:, cond_bank(phase), bass.ds(c, 1) if not isinstance(c, int) else slice(c, c + 1)],
                                           cond_part[v][(n0 + e) % 2][:, j * P:j * P + P], one_col, start=True, stop=True)
                    mm.then_inc(S("cond_summed"), 1)

            def down(g, src, ntok, kper=KSPLIT, pairs=None):
                for i, (n, part) in enumerate(g.parts):
                    w = panel_in(g, 0, i)
                    if pairs is not None and (i == 0 or part == 1):
                        pe.wait_ge(S("up_used"), pairs + (KF // 2 if part else (KSPLIT + 1) // 2))
                    for j in range(2):
                        a = g.a0 + g.apa * n + (j if ntok == 512 else 0)
                        if part == 0 and (j == 0 or ntok == 512) and a >= BANKS:
                            pe.wait_ge(free[a % BANKS], a // BANKS)
                        o = 0 if ntok == 512 else j * ntok
                        for k in range(kper):
                            first = part == 0 and k == 0 and (j == 0 or ntok == 512)
                            mm = pe.matmul(acc[a % BANKS][:, o:o + ntok],
                                           w[:, k * PANEL + j * P:k * PANEL + j * P + P],
                                           src(part * kper + k), start=first, stop=(part == 1 and k == kper - 1),
                                           skip_group_check=True)
                        if part == 1 and (j == 1 or ntok == 512):
                            mm.then_inc(ready[a % BANKS], 1)
                        if part == 0 and j == 1:
                            mm.then_inc(half_read, 1)
                        cond_sum(g.name, 0, 2 * i + j)

            def layer_norm(n, g):
                for i in range(4):
                    a = g.a0 + i
                    pe.wait_ge(free[a % BANKS], a // BANKS + 1)
                    for j in range(2):
                        k = 2 * i + j
                        mm = pe.matmul(mix[:, 0, 0:T], ones_d[:, :], X[:, k, lat], start=(k == 0), stop=(k == KD - 1))
                mm.then_inc(S("mean_ready"), 1)
                for k in range(KD):
                    pe.wait_ge(S("squared"), n * KD + k + 1)
                    mm = pe.matmul(mix[:, 1, 0:T], ones_d[:, :], squares[:, k, 0:T], start=(k == 0), stop=(k == KD - 1))
                mm.then_inc(S("var_ready"), 1)

            def rms_norm(n, sel):
                sq = squares2 if n in (2, 4) else squares
                for k in range(KD):
                    pe.wait_ge(S("rms_sq"), n * KD + k + 1)
                    mm = pe.matmul(mix[:, 0, 0:sel.stop - sel.start], ones_d[:, :], sq[:, k, 0:sel.stop - sel.start],
                                   start=(k == 0), stop=(k == KD - 1))
                mm.then_inc(S("rms_ready"), 1)

            def gate(l, *panels):
                for u in panels:
                    features(G[f"gate{l}"], 0, u, lambda k: H[:, k, lat], T)

            def pool(l):
                gate(l, 0, 1)
                pe.wait_ge(S("pool_diff"), l + 1)
                for c in range(2):
                    mm = pe.matmul(mix[:, 0, c * T:c * T + T], poolw[:, l, c, :], pdiff[:, c, :], start=True, stop=True)
                mm.then_inc(S("pool_mm"), 1)

            def attention(l):
                for qb in range(2):
                    n = P * (qb + 1)
                    for b in range(4):
                        if qb == 1:
                            pe.wait_ge(S("idx_relu"), 8 * l + b + 1)
                        for i in range(2):
                            r = slice(64 * (b // 2), 64 * (b // 2) + 64)
                            mm = pe.matmul(mix[:, b, i * T:i * T + n], qiT[r, 2 * (b % 2) + i, qb * P:qb * P + P], kiT[r, 0:n],
                                           start=True, stop=True)
                        mm.then_inc(S("idx_mm"), 1)
                for qb in range(2):
                    n = P * (qb + 1)
                    pe.wait_ge(S("idx_relu"), 8 * l + 4 + 2 * qb + 2)
                    for h in range(4):
                        r = slice(64 * (h % 2), 64 * (h % 2) + 64)
                        mm = pe.matmul(mix[:, 2 * qb + h % 2, h // 2 * T:h // 2 * T + n],
                                       qT[r, h // 2, qb * P:qb * P + P], kT[r, h // 2, 0:n], start=True, stop=True)
                    mm.then_inc(S("logit_mm"), 1)
                gate(l, 2, 3, 4, 5)
                for qb in range(2):
                    pe.wait_ge(S("prob_ready"), 2 * l + qb + 1)
                    for h in range(4):
                        for s in range(qb + 1):
                            i = h * (qb + 1) + s
                            mm = pe.transpose(mix[:, 2 * qb + i // 4, i % 4 * P:i % 4 * P + P],
                                              logit[:, qb, h, s * P:s * P + P], ident)
                    mm.then_inc(S("probT_mm"), 1)
                for qb in range(2):
                    pe.wait_ge(S("probT_ready"), 2 * l + qb + 1)
                    for i in range(4):
                        h = 2 * (i % 2) + i // 2
                        for s in range(qb + 1):
                            mm = pe.matmul(mix[64 * (h % 2):64 * (h % 2) + 64, 1, h // 2 * T + qb * P:h // 2 * T + qb * P + P],
                                           vt[:, s, h * 64:h * 64 + 64], probT[:, qb, i * (qb + 1) + s, :],
                                           start=(s == 0), stop=(s == qb))
                mm.then_inc(S("attn_mm"), 1)

            def hgrn(l):
                k4, q4 = kk, qf
                for i in range(9):
                    bank = 2 * (i % 2)
                    if i == 0:
                        pe.wait_ge(S("hg_key"), l + 1)
                    else:
                        pe.wait_ge(S("hg_x"), 8 * l + i)
                    if i >= 2:
                        pe.wait_ge(S("hg_acc"), 9 * l + i - 1)
                    xt = treeX[(i - 1) % 2].rearrange("p (h t) -> p h t", h=4)
                    if i < 8:
                        for b in range(2):
                            for h in range(4):
                                c = slice(b * P, b * P + P)
                                lhs, rhs = (k4[:, h, c], q4[:, h, c]) if i == 0 else (xt[:, h, c], xt[:, h, c])
                                mm = pe.matmul(mix[:, bank + b, h * P:h * P + P], lhs, rhs, start=True, stop=True)
                    else:
                        for h in range(4):
                            mm = pe.matmul(mix[:, bank, h * P:h * P + P], xt[:, h, 0:P], xt[:, h, P:T], start=True, stop=True)
                    mm.then_inc(S("hg_mm"), 1)
                    if i < 6:
                        gate(l, 6 + i)
                pe.wait_ge(S("hg_acc"), 9 * l + 9)
                for h in range(4):
                    v = slice(h * P, h * P + P)
                    o = lambda t: mix[:, 2 + h // 2, h % 2 * T + t * P:h % 2 * T + t * P + P]
                    pe.matmul(o(0), hi[:, 0, v], pairs[:, h, :], start=True, stop=True)
                    pe.matmul(o(1), hi[:, 0, v], offd[:, h, :], start=True, stop=False)
                    mm = pe.matmul(o(1), hi[:, 1, v], pairs[:, 4 + h, :], start=False, stop=True)
                mm.then_inc(S("hg_o"), 1)
                pe.wait_ge(S("hg_sq"), l + 1)
                for i in range(2):
                    mm = pe.matmul(mix[:, i, :], ones_h[:, :], osq[:, i * 512:i * 512 + 512], start=True, stop=True)
                mm.then_inc(S("hg_ms"), 1)

            def even_gates():
                g = G["evengate"]
                b = acc_open(g, 0, 0)
                pe.wait_ge(S("low_made"), split_count(g, 0, 0, 1))
                split_half(g, 0, 0, 0, acc[b][0:96, :], lambda k: H_r[:, k, :], lambda k: in_lo[0][k], True, True, ready[b],
                           norm=0, m=96)

            def gla():
                pe.wait_ge(S("rank_ready"), 1)
                for d in range(2):
                    r = slice(32 + 32 * d, 48 + 32 * d)
                    for c in range(2):
                        mm = pe.matmul(mix[:, 2 * d + c, :], a2w[r, c * P:c * P + P], rows16[r, :], start=True, stop=True)
                    mm.then_inc(S("decay_mm"), 1)
                def heads(out, lhs, rhs, cs, ct, bank0, at):
                    for h in range(4):
                        r = slice(64 * (h % 2), 64 * (h % 2) + 64)
                        o = (2 * at + h // 2) * P
                        m = pe.matmul(out[:, bank0 + h % 2, o:o + P], lhs[r, h // 2, cs * P:cs * P + P],
                                      rhs[r, h // 2, ct * P:ct * P + P], start=True, stop=True)
                    return m

                pe.wait_ge(S("decay_read"), 2)
                for hf in range(2):
                    for b in range(2):
                        mm = heads(mix, gk, gq, 2 * hf + b, 2 * hf + b, 2 * hf, b)
                    mm.then_inc(S("gla_mm"), 1)
                for n in range(16):
                    lv, d = n // 2, n % 2
                    out, xt = gla_banks[d], gX[d]
                    pe.wait_ge(S("gla_x"), n + 1)
                    if lv < 7:
                        for hf in range(2):
                            before = 2 + 2 * (n - 2) + hf if lv else hf if d == 0 else None
                            if before is not None:
                                pe.wait_ge(S("gla_acc"), before + 1)
                            for b in range(2):
                                mm = heads(out, xt, xt, 2 * hf + b, 2 * hf + b, 2 * hf, b)
                            mm.then_inc(S("gla_mm"), 1)
                    else:
                        pe.wait_ge(S("gla_acc"), 2 + 2 * (n - 2) + 1)
                        for st in range(2):
                            s_, t_ = (0, 1) if d == 0 else (1, 0)
                            mm = heads(out, xt, xt, 2 * st + s_, 2 * st + t_, 0, st)
                        mm.then_inc(S("gla_mm"), 1)
                pe.wait_ge(S("gla_x"), 18)
                pe.wait_ge(S("gla_acc"), 32)
                for h in range(4):
                    r = slice(64 * (h % 2), 64 * (h % 2) + 64)
                    for s in range(2):
                        for d in range(2):
                            mm = pe.matmul(mix[:, h, s * T:s * T + T], gX[d][r, h // 2, s * P:s * P + P],
                                           gX[d][r, h // 2, T:2 * T], start=(d == 0), stop=(d == 1))
                mm.then_inc(S("gla_mm"), 1)
                pe.wait_ge(S("gla_acc"), 33)
                for h in range(4):
                    for t in range(4):
                        o = mix[:, h, t * P:t * P + P]
                        st, tb = t // 2, t % 2
                        terms = [(2 * st + tb, gpairs[:, 8 * st + 4 * (h % 2) + 2 * tb + h // 2, :]),
                                 (2 * st + 1 - tb, goff[:, 8 * (1 - tb) + 4 * (h % 2) + 2 * st + h // 2, :])]
                        if st == 1:
                            terms += [(s, gcross[:, s, h, tb * P:tb * P + P]) for s in range(2)]
                        for i, (s, rhs) in enumerate(terms):
                            mm = pe.matmul(o, gv[:, s, h * P:h * P + P], rhs, start=(i == 0), stop=(i == len(terms) - 1))
                mm.then_inc(S("gla_o"), 1)
                head_mean_square(0)

            def head_mean_square(n):
                pe.wait_ge(S("head_sq"), n + 1)
                for h in range(4):
                    mm = pe.matmul(mix[32 * h:32 * h + 32, 0, :], ones_h[:, 0:32], region(E_T, 4, 512)[:, h, :], start=True, stop=True)
                mm.then_inc(S("head_ms"), 1)

            def head_spread(n):
                pe.wait_ge(S("head_rec"), n + 1)
                for h in range(4):
                    mm = pe.matmul(mix[:, h, :], ident[:, 32 * h:32 * h + 1].to_broadcast([P, P]), head_std, start=True, stop=True)
                mm.then_inc(S("head_bc"), 1)

            def mlstm():
                for i in range(8):
                    if i == 4:
                        head_spread(0)
                    if i >= 4:
                        pe.wait_ge(S("ml_rall"), i - 3)
                    for t in range(4):
                        mm = pe.matmul(accs[:, i % 4, t * P:t * P + P], dcol[:, 8 * t + i:8 * t + i + 1].to_broadcast([P, P]), ident, start=True, stop=True)
                    mm.then_inc(S("ml_sel"), 1)
                pe.wait_ge(S("ml_rall"), 8)
                pe.wait_ge(S("head_normed"), 1)
                for t in range(4):
                    w = T if t < 2 else 2 * T
                    if t >= 1:
                        pe.wait_ge(S("ml_h"), t)
                    for h in range(4):
                        mm = pe.matmul(mix[:, h, 0:w], mqk[:, h, t * P:t * P + P], mqk[:, 4 + h, 0:w], start=True, stop=True)
                    mm.then_inc(S("ml_scores"), 1)
                    pe.wait_ge(S("ml_prob"), t + 1)
                    for h in range(4):
                        for s in range(w // P):
                            mm = pe.transpose(mix[:, h, s * P:s * P + P], psum2[:, h, s * P:s * P + P], ident)
                    mm.then_inc(S("ml_probT"), 1)
                    pe.wait_ge(S("ml_probT_sb"), t + 1)
                    for h in range(4):
                        for s in range(w // P):
                            mm = pe.matmul(mix[:, h, 0:P], mv[:, s, h * P:h * P + P], mprobT[:, h, s * P:s * P + P],
                                           start=(s == 0), stop=(s == w // P - 1))
                    mm.then_inc(S("ml_hmm"), 1)
                head_mean_square(1)
                head_spread(1)

            def ssd_rates():
                pe.wait_ge(S("dt_rows"), 1)
                for i in range(2):
                    pe.transpose(mix[:, 0, i * 64:i * 64 + 64], dtr[0:64, T + i * P:T + i * P + P], ident[0:64, 0:64])
                    pe.transpose(mix[:, 0, 128 + i * 64:192 + i * 64], dcum[0:64, T + i * P:T + i * P + P], ident[0:64, 0:64])
                    mm = pe.transpose(mix[:, 0, 256 + i * 64:320 + i * 64], dwe[0:64, i * P:i * P + P], ident[0:64, 0:64])
                mm.then_inc(S("dt_cols"), 1)

            def ssd_features(g, q, half=None):
                if q >= 6:
                    features(G[f"ssdz{g}"], 0, q - 6, lambda k: H[:, k, lat], T, js=range(2) if half is None else (half,))
                    return
                p, u, j = G[f"ssdx{g}" if q < 4 else f"ssdbc{g}"], q // 2 % 2, q % 2
                w = panel_in(p, 0, u)
                b = acc_open(p, 0, u, j)
                for k in range(KD) if half is None else range(half * KD // 2, (half + 1) * KD // 2):
                    mm = pe.matmul(acc[b][:, :], w[:, k * PANEL + j * P:k * PANEL + j * P + P], H[:, k, :], start=(k == 0), stop=(k == KD - 1))
                if half != 0:
                    mm.then_inc(ready[b], 1)

            def ssd_group(g):
                xc, (bc_, cc) = S_XC[g % 2], S_BCC[g % 2]
                pe.wait_ge(S("ssd_conv"), g + 1)
                for s in (1, 2, 3, 0):
                    if g >= 1 and s == 2:
                        pe.wait_ge(S("ssd_yz"), g)
                    if g >= 1 and s == 0:
                        pe.wait_ge(S("ssd_gstd"), g)
                    for c in range(4):
                        mm = pe.transpose(mix[:, s, c * P:c * P + P], xc[:, c, s * P:s * P + P], ident)
                mm.then_inc(S("ssd_xT"), 1)
                if g < 3:
                    ssd_features(g + 1, 0)
                pe.wait_ge(S("ssd_xT_sb"), g + 1)
                for s in range(2):
                    pe.transpose(mix[:, 0, s * P:s * P + P], bc_[:, s * P:s * P + P], ident)
                for s in range(2):
                    mm = pe.matmul(mix[:, 1, s * T:s * T + T], bc_[:, T + s * P:T + s * P + P], cc[:, lat],
                                   start=True, stop=True)
                mm.then_inc(S("ssd_cb"), 1)
                if g < 3:
                    ssd_features(g + 1, 1)
                pe.wait_ge(S("ssd_cb_sb"), g + 1)
                pe.wait_ge(S("ssd_xw"), g + 1)
                for d in range(2):
                    for s in range(2):
                        mm = pe.matmul(mix[:, 2 + d, :], S_BT[:, s, :], S_XW[:, d, s, :], start=(s == 0), stop=(s == 1))
                mm.then_inc(S("ssd_state"), 1)
                pe.wait_ge(S("ssd_state_sb"), g + 1)
                for i in range(16):
                    pr, hh, d = i // 4, i // 2 % 2, i % 2
                    n = 16 * g + i
                    h = 2 * pr + hh
                    row = 32 * d + 8 * g + h
                    if n >= 2:
                        pe.wait_ge(S("ssd_dmin"), n - 1)
                    pe.matmul(mix[:, i % 2, 0:T], ident[0:64, row:row + 1].to_broadcast([64, P]), dcum[0:64, lat],
                              start=True, stop=True).then_inc(S("ssd_row"), 1)
                    if i >= 1:
                        ssd_out(g, i - 1, n - 1)
                    if i < 12 and g < 3:
                        ssd_features(g + 1, 2 + i // 2, i % 2)
                ssd_out(g, 15, 16 * g + 15)
                pe.wait_ge(S("ssd_gsq"), g + 1)
                for c in range(4):
                    mm = pe.matmul(mix[:, 0, 0:T], ones_g[:, :], S_SQ[:, c, :], start=(c == 0), stop=(c == 3))
                mm.then_inc(S("ssd_gms"), 1)

            def ssd_out(g, i, n):
                pr, hh, d = i // 4, i // 2 % 2, i % 2
                h = 2 * pr + hh
                r = slice(64 * hh, 64 * hh + 64)
                v = slice(h * 64, h * 64 + 64)
                y = mix[:, 2 + pr % 2, :]
                first, last = i % 2 == 0, i % 2 == 1
                if i % 4 == 0 and i >= 8:
                    pe.wait_ge(S("ssd_y"), 4 * g + pr - 1)
                pe.wait_ge(S("ssd_w"), n + 1)
                w = S_DW[:, n % 2, :]
                pe.matmul(y[r, 0:T], S_ST[:, d, v], S_CW[:, n % 2, :], start=first, stop=False, skip_group_check=True)
                if d == 0:
                    pe.matmul(y[r, 0:T], S_XT[:, 2, v], w[:, 0:T], start=False, stop=False, skip_group_check=True)
                    mm = pe.matmul(y[r, P:T], S_XT[:, 3, v], w[:, T:T + P], start=False, stop=last, skip_group_check=True)
                else:
                    pe.matmul(y[r, 0:T], S_XT[:, 3, v], w[:, P:P + T], start=False, stop=False, skip_group_check=True)
                    mm = pe.matmul(y[r, 0:P], S_XT[:, 2, v], w[:, 0:P], start=False, stop=last, skip_group_check=True)
                mm.then_inc(S("ssd_ymm"), 1)

            pe.wait_ge(S("consts_loaded"), 16)
            for i in range(HEAD):
                cond_sum("head", 0, i)
            pe.wait_ge(S("loaded"), 80)
            pe.matmul(mix[0:4, 0, 0:384], relb[:, :], const("onehot")[0:32, :], start=True, stop=True).then_inc(S("bias_mm"), 1)
            stage_end(pe, count)
            norms = 0
            for l in range(DEPTH):
                for f in range(2):
                    if f == 1:
                        pe.wait_ge(S("h_ready"), (3 * l + 2) * KD)
                        if l == 0:
                            pe.wait_ge(S("hankel"), 16)
                            for i in range(2):
                                mm = pe.matmul(mix[:, i, :], const("flip"), biasC[:, 2 * i:2 * i + 2, :], start=True, stop=True)
                            mm.then_inc(S("bias_flip"), 1)
                        g = G[f"mix{l}"]
                        rhs = lambda k: H[:, k, lat]
                        for u in range(15):
                            if u == 5:
                                w = panel_in(g, 0, u)
                                b = acc_open(g, 0, u)
                                for k in range(KD):
                                    pe.matmul(acc[b][:, 0:T], w[:, k * PANEL:k * PANEL + P], rhs(k), start=(k == 0), stop=(k == KD - 1))
                                for tb in range(2):
                                    for k in range(KD):
                                        mm = pe.matmul(acc[b][:, T + 8 * tb:T + 8 * tb + 8], H[:, k, T + tb * P:T + tb * P + P],
                                                       w[:, k * PANEL + P:k * PANEL + P + 8], start=(k == 0), stop=(k == KD - 1))
                                mm.then_inc(ready[b], 1)
                            elif u in (6, 7, 8):
                                tokens(g, u, T, 2)
                            else:
                                features(g, 0, u, rhs, T)
                            cond_sum(f"mix{l}", 0, u)
                        stage_end(pe, count)
                        pool(l)
                        stage_end(pe, count)
                        attention(l)
                        stage_end(pe, count)
                        hgrn(l)
                        stage_end(pe, count)
                        g = G[f"branch{l}"]
                        for u in range(4):
                            w = panel_in(g, 0, u)
                            for r, ks in enumerate((range(0, 2), range(2, 4), range(4, 8))):
                                b = acc_open(g, 0, u, r)
                                for j in range(2):
                                    for k in ks:
                                        mm = pe.matmul(acc[b][:, j * T:j * T + T], w[:, k * PANEL + j * P:k * PANEL + j * P + P],
                                                       ymix[:, k, :], start=(k == ks[0]), stop=(k == ks[-1]))
                                mm.then_inc(ready[b], 1)
                        stage_end(pe, count)
                        g = G[f"mixout{l}"]
                        for u in range(4):
                            features(g, 0, u, lambda k: merged[:, k, :], T)
                        layer_norm(norms, g)
                        norms += 1

                    def up_panel(it, u, name=f"in{l}{f}"):
                        split_up(G[name], it, u, 3 * l + 2 * f)
                        cond_sum(name, it, u)

                    groups(pe, G[f"in{l}{f}"], up_panel, peel=True)
                    pe.wait_ge(S("hid_ready"), 2 * l + f + 1)
                    split_down(G[f"out{l}{f}"])
                    layer_norm(norms, G[f"out{l}{f}"])
                    norms += 1
                    if l == DEPTH - 1 and f == 1:
                        stage_end(pe, count)
            rms = 0
            for l in range(DEPTH):
                rms_norm(rms, both)
                rms += 1
                if l == 0:
                    even_gates()
                    for u in range(14):
                        if u in (2, 3, 10, 11):
                            kept_tokens(G["even"], u)
                        else:
                            kept_features(G["even"], 0, u, 0)
                    pe.wait_ge(S("ml_rows"), 1)
                    for t in range(4):
                        pe.transpose(mix[:, 0, t * 16:t * 16 + 16], cum16[:, t * P:t * P + P], ident[0:16, 0:16])
                        mm = pe.transpose(mix[:, 0, 64 + t * 16:80 + t * 16], rows16[0:16, t * P:t * P + P], ident[0:16, 0:16])
                    mm.then_inc(S("ml_cols"), 1)
                    stage_end(pe, count)
                    gla()
                    mlstm()
                    stage_end(pe, count)
                    for u in range(4):
                        features(G["evenout"], 0, u, lambda k: ey[:, k, :], 512)
                        cond_sum("evenout", 0, u)
                else:
                    g = G["dt"]
                    w = panel_in(g, 0, 0)
                    b = acc_open(g, 0, 0)
                    for k in range(KD):
                        input_chunk(2, k)
                        mm = pe.matmul(acc[b][0:64, :], w[:, k * PANEL:k * PANEL + 64], H[:, k, :], start=(k == 0), stop=(k == KD - 1))
                    mm.then_inc(ready[b], 1)
                    for q in range(2):
                        ssd_features(0, q)
                    ssd_rates()
                    ssd_features(0, 2)
                    stage_end(pe, count)
                    for q in range(3, 8):
                        ssd_features(0, q)
                    for g in range(4):
                        ssd_group(g)
                    stage_end(pe, count)
                    down(G["ssdout"], lambda k: S_Y[:, k, :], T, KD)
                sel = both if l == 0 else lat
                rms_norm(rms, sel)
                ntok = 512 if l == 0 else T
                if l == 0:
                    groups(pe, G["up0"], lambda it, u: kept_features(G["up0"], it, u, 1), peel=True)
                else:
                    groups(pe, G["up1"], lambda it, u, n=rms: features(G["up1"], it, u, lambda k: H[:, k, sel], ntok, n), peel=True)
                rms += 1
                down(G[f"down{l}"], lambda k: hid[:, k, 0:ntok], ntok, pairs=11 * l)
            rms_norm(rms, lat)

        @block.gpsimd
        def _(pool):
            def low(g, it, u):
                for j in range(2):
                    pool.wait_ge(S("high_made"), split_count(g, it, u, j))
                    if g.wide and u >= 1:
                        wait_used(pool, g, it, u - 1, j)
                    hi, lo = split_parts(g, u, j)
                    pool.tensor_tensor(lo, half_panel(g, u, j), hi, ALU.subtract)
                    pool.drain().then_inc(S("low_made"), 1)

            for l in range(DEPTH):
                for f in range(2):
                    groups(pool, G[f"in{l}{f}"], lambda it, u, g=G[f"in{l}{f}"]: low(g, it, u))
                    for i in range(8):
                        low(G[f"out{l}{f}"], 0, i)
            low(G["evengate"], 0, 0)
            for name in ("even", "up0"):
                groups(pool, G[name], lambda it, u, g=G[name]: low(g, it, u))
            g = G["up1"]

            def gated(it, u):
                if u % 2 == 1:
                    par = u // 2
                    pool.wait_ge(S("up_silu"), it * 2 + (11 + par + 1))
                    pool.tensor_tensor(hid[:, bass.ds(it * 4 + u - 1, 2), 0:T], uconv[:, par, 0:2, 0:T], uconv[:, par, 2:4, 0:T], ALU.mult)
                    pool.drain().then_inc(S("up_used"), 1)

            groups(pool, g, gated)

        @block.scalar
        def _(act):
            act = InOrder(act)
            count = [0]

            def evac(g, it, u, r, dst, src_cols, func, scale=1.0):
                b = wait_ready(act, g, it, u, r)
                src = acc[b][:, src_cols]
                if len(dst.shape) == 3:
                    src = src.rearrange("p (a b) -> p a b", a=dst.shape[1])
                act.activation(dst, src, func, scale=scale).then_inc(free[b], 1)

            def high(g, it, u):
                s = (g.p0 + u) % SLOTS
                act.wait_ge(landed[s], it * 16 + 16 * ((g.p0 + u) // SLOTS + 1))
                for j in range(2):
                    if not isinstance(it, int) or 4 * it + u >= 2:
                        wait_used(act, g, it, u - 2, j)
                    act.eng.activation(split_parts(g, u, j)[0], half_panel(g, u, j), ACT.Copy)
                    act.drain().then_inc(S("high_made"), 1)

            def high_kept(g, it, u, j):
                s = (g.p0 + u) % SLOTS
                act.wait_ge(landed[s], it * 16 + 16 * ((g.p0 + u) // SLOTS + 1))
                act.eng.activation(split_parts(g, u, j)[0], half_panel(g, u, j), ACT.Copy)
                act.drain().then_inc(S("high_made"), 1)

            def layer_norm(n, l, j):
                for k in range(KD):
                    act.wait_ge(S("centred"), n * KD + k + 1)
                    act.activation(squares[:, k, 0:T], X[:, k, lat], ACT.Square).then_inc(S("squared"), 1)
                act.wait_ge(S("var_ready"), n + 1)
                act.activation(std[:, 0:T], mix[:, 1, 0:T], ACT.Sqrt, bias=eps_ln).then_inc(S("std_ready"), 1)
                if j < 2 or l + 1 < DEPTH:
                    if j != 0:
                        high(G[f"in{l}1" if j == 1 else f"in{l + 1}0"], 0, 0)
                    for k in range(KD):
                        act.wait_ge(S("scaled"), n * KD + k + 1)
                        g, b = ln_next[:, 0, k:k + 1], ln_next[:, 1, k:k + 1]
                        if j == 0:
                            act.eng.activation(H[:, k, lat], X[:, k, lat], ACT.Identity, scale=g, bias=b)
                            act.drain().then_inc(S("h_ready"), 1)
                        else:
                            act.eng.activation(h_raw[:, k, :], X[:, k, lat], ACT.Identity, scale=g, bias=b)
                            act.eng.activation(h_hi[:, k, :], X[:, k, lat], ACT.Identity, scale=g, bias=b)
                            act.drain().then_inc(S("h_parts"), 1)
                    for k in range(KD):
                        act.eng.activation(X[:, k, lat], X[:, k, lat], ACT.Identity, scale=ln_next[:, 2, k:k + 1], bias=ln_next[:, 3, k:k + 1])
                else:
                    for k in range(KD):
                        act.wait_ge(S("scaled"), n * KD + k + 1)
                        c = (3 * l + j) * KD + k
                        act.eng.activation(X[:, k, lat], X[:, k, lat], ACT.Identity, scale=col("ln_g", c), bias=col("ln_b", c))
                act.drain().then_inc(S("x_ready"), 1)

            def rms_norm(n, sel, gain, shift=None):
                w = sel.stop - sel.start
                sq = squares2 if n in (2, 4) else squares
                if n == 0:
                    act.wait_ge(S("context_loaded"), 16)
                for k in range(KD):
                    if n > 0:
                        act.wait_ge(S("rms_in"), (n - 1) * KD + k + 1)
                    act.activation(sq[:, k, 0:w], X[:, k, sel], ACT.Square).then_inc(S("rms_sq"), 1)
                act.wait_ge(S("rms_ready"), n + 1)
                act.activation(std[:, 0:w], mix[:, 0, 0:w], ACT.Sqrt, bias=eps_rms).then_inc(S("rms_std"), 1)
                split = n < 2
                if split:
                    for j in range(2):
                        high_kept(G[("evengate", "up0")[n]], 0, 0, j)
                for k in range(KD + 1):
                    if k < KD:
                        act.wait_ge(S("rms_scaled"), n * KD + k + 1)
                        for v in (1, 0) if sel == both else (0,):
                            t = lat if v == 0 else slice(0, T)
                            dst = in_raw[n][k][:, t] if split else H[:, k, t]
                            if shift is None:
                                act.eng.activation(dst, H[:, k, t], ACT.Identity, scale=gain(k, v))
                            else:
                                act.eng.activation(dst, H[:, k, t], ACT.Identity, scale=gain(k, v), bias=shift[:, k, v:v + 1])
                    if split and k > 0:
                        act.eng.activation(H_r[:, k - 1, :], in_raw[n][k - 1], ACT.Copy)
                    if split and k > 0:
                        act.drain().then_inc(S("rms_parts"), 1)
                    elif split:
                        act.drain()
                    elif k < KD:
                        act.drain().then_inc(S("rms_out"), 1)

            def gate(l, *panels):
                for u in panels:
                    evac(G[f"gate{l}"], 0, u, 0, gates[:, 2 * u:2 * u + 2, :], both, ACT.Copy)

            def pool(l):
                gate(l, 0, 1)
                act.wait_ge(S("pool_mm"), l + 1)
                for c in range(2):
                    act.activation(ymix[:, c, :], mix[:, 0, c * T:c * T + T], ACT.Identity, scale=col("pool_scale", 2 * l + c))

            def attention(l):
                for qb in range(2):
                    n = P * (qb + 1)
                    for pr in range(4):
                        act.wait_ge(S("idx_mm"), 8 * l + 4 * qb + pr + 1)
                        if qb == 1 and pr == 0:
                            act.wait_ge(S("idx_sum"), 2 * l + 1)
                        act.activation(relu_s[:, 2 * pr:2 * pr + 2, 0:n],
                                       mix[:, pr, :].rearrange("p (a t) -> p a t", a=2)[:, :, 0:n], ACT.Relu)\
                           .then_inc(S("idx_relu"), 1)
                for qb in range(2):
                    n = P * (qb + 1)
                    gate(l, 2 + 2 * qb, 3 + 2 * qb)
                    act.wait_ge(S("logit_ready"), 2 * l + qb + 1)
                    for h in range(4):
                        e = act.activation(logit[:, qb, h, 0:n], logit[:, qb, h, 0:n], ACT.Exp,
                                           bias=small[:, 8 * qb + h:8 * qb + h + 1],
                                           accum_out=small[:, 8 * qb + 4 + h:8 * qb + 5 + h])
                    act.drain().then_inc(S("exp_ready"), 1)
                for qb in range(2):
                    act.wait_ge(S("probT_mm"), 2 * l + qb + 1)
                    m = 4 * (qb + 1)
                    act.activation(probT[:, qb, 0:m, :].rearrange("p a b -> p (a b)"),
                                   mix[:, 2 * qb:2 * qb + qb + 1, :].rearrange("p a b -> p (a b)"), ACT.Copy)\
                       .then_inc(S("probT_ready"), 1)
                act.wait_ge(S("attn_mm"), l + 1)
                act.activation(ymix[:, 2:4, :].rearrange("p a b -> p (a b)"), mix[:, 1, :], ACT.Copy)

            def halves(v, m):
                return v.rearrange("p (n two m) -> p n two m", two=2, m=m)

            def hgrn(l):
                act.wait_ge(S("hg_key"), l + 1)
                act.activation(pref, pref, ACT.Ln, bias=one_col)
                act.drain()
                for lv in range(8):
                    m = 1 << lv
                    if lv >= 1:
                        act.wait_ge(S("hg_sums"), 7 * l + lv)
                    else:
                        act.wait_ge(S("hg_zero"), l + 1)
                    if lv >= 2:
                        act.wait_ge(S("hg_mm"), 9 * l + lv)
                    x = halves(treeX[lv % 2], m)
                    act.activation(x[:, :, 0, :], halves(suff, m)[:, :, 0, :], ACT.Exp)
                    act.activation(x[:, :, 1, :], halves(pref, m)[:, :, 1, :], ACT.Exp).then_inc(S("hg_exp"), 1)
                    if lv >= 2:
                        gate(l, 4 + lv)
                act.activation(gates[:, :, :], gates[:, :, :], ACT.Sigmoid)
                act.wait_ge(S("hg_o"), l + 1)
                act.activation(osq, mix[:, 2:4, :].rearrange("p a b -> p (a b)"), ACT.Square).then_inc(S("hg_sq"), 1)
                act.wait_ge(S("hg_ms"), l + 1)
                act.activation(ostd, mix[:, 0:2, :].rearrange("p a b -> p (a b)"), ACT.Sqrt, bias=eps_rms)\
                   .then_inc(S("hg_std"), 1)

            def gla():
                for d in range(2):
                    act.wait_ge(S("decay_mm"), d + 1)
                    for c in range(2):
                        act.activation(gX[0][:, c, :], mix[:, 2 * d + c, :], ACT.Identity, bias=col("gla_ab_2", 2 * d + c))
                    act.drain().then_inc(S("decay_read"), 1)
                    act.activation(gX[1][:, :, :], gX[0][:, :, :], ACT.Abs)
                    act.drain()
                    act.activation(gX[1][:, :, :], gX[1][:, :, :], ACT.Exp, scale=-1.0)
                    act.drain()
                    act.activation(gX[1][:, :, :], gX[1][:, :, :], ACT.Ln, bias=one_col).then_inc(S("decay_ln"), 1)
                    act.wait_ge(S("decay_log"), d + 1)
                for n in range(18):
                    lv, d = n // 2, n % 2
                    m = 1 << lv
                    act.wait_ge(S("gla_sums"), n + 1)
                    if lv >= 1:
                        act.wait_ge(S("gla_mm"), 2 + 2 * (n - 2) + 2 if lv < 8 else 31 + d)
                    x = halves(gX[d].rearrange("p c t -> p (c t)"), m)
                    e, o = (0, 1) if (d == 0 or lv == 8) else (1, 0)
                    act.activation(x[:, :, e, :], halves(gsuff[:, d, :], m)[:, :, e, :], ACT.Exp)
                    act.activation(x[:, :, o, :], halves(gpref[:, d, :], m)[:, :, o, :], ACT.Exp).then_inc(S("gla_exp"), 1)
                act.wait_ge(S("gla_o"), 1)
                act.activation(gv[:, :, :], mix[:, :, :], ACT.Copy)
                act.activation(region(E_T, 4, 512), mix[:, :, :], ACT.Square)
                act.drain().then_inc(S("head_sq"), 1)
                act.wait_ge(S("head_ms"), 1)
                act.activation(head_std, mix[:, 0, :], ACT.Sqrt, bias=eps_rms).then_inc(S("head_std"), 1)

            def ml_rows():
                act.activation(tmp16[:, :], rows16[0:16, :], ACT.Abs)
                act.drain()
                act.activation(tmp16[:, :], tmp16[:, :], ACT.Exp, scale=-1.0)
                act.drain()
                act.activation(tmp16[:, :], tmp16[:, :], ACT.Ln, bias=one_col[0:16, :]).then_inc(S("ml_ln"), 1)

            def mlstm():
                def decays(t):
                    dlog, sm = dlogs[t % 2], 24 * (t % 2)
                    o = 0 if t < 2 else T
                    act.wait_ge(S("ml_max"), t + 1)
                    for i in range(8):
                        act.eng.activation(dlog[:, i, o:o + T], dlog[:, i, o:o + T], ACT.Exp, bias=small[:, sm + i:sm + i + 1])
                        if t >= 2:
                            b = 16 + 8 * (t % 2) + i
                            act.eng.activation(dlog[:, i, 0:T], rall[:, i, 0:T], ACT.Exp, bias=ml_max[:, b:b + 1])
                    act.eng.activation(small[:, sm + 8:sm + 16], small[:, sm:sm + 8], ACT.Exp)
                    act.drain().then_inc(S("ml_exp"), 1)

                for i in range(8):
                    act.wait_ge(S("ml_sel"), i + 1)
                    act.activation(rall[:, i, :], accs[:, i % 4, :], ACT.Copy).then_inc(S("ml_rall"), 1)
                decays(0)
                for t in range(4):
                    w = T if t < 2 else 2 * T
                    if t < 3:
                        decays(t + 1)
                    act.wait_ge(S("ml_probT"), t + 1)
                    act.activation(mprobT[:, :, 0:w], mix[:, :, 0:w], ACT.Copy).then_inc(S("ml_probT_sb"), 1)
                    act.wait_ge(S("ml_hmm"), t + 1)
                    act.activation(mqk[:, 0:4, t * P:t * P + P], mix[:, :, 0:P], ACT.Copy).then_inc(S("ml_h"), 1)
                act.wait_ge(S("ml_gated"), 1)
                act.activation(region(E_T, 4, 512), mqk[:, 0:4, :], ACT.Square).then_inc(S("head_sq"), 1)
                act.wait_ge(S("head_ms"), 2)
                act.activation(head_std, mix[:, 0, :], ACT.Sqrt, bias=eps_rms).then_inc(S("head_std"), 1)

            def ssd_rates():
                b = wait_ready(act, G["dt"], 0, 0)
                act.activation(dtr[0:64, :], acc[b][0:64, :], ACT.Identity, bias=col("ssd_dt_bias_2", 0, 0, 64)).then_inc(free[b], 1)
                act.activation(negA, col("ssd_a_log_2", 0, 0, 64), ACT.Exp)
                act.drain()
                act.activation(dcum[0:64, :], dtr[0:64, :], ACT.Abs)
                act.drain()
                act.activation(dcum[0:64, :], dcum[0:64, :], ACT.Exp, scale=-1.0).then_inc(S("dt_exp"), 1)
                act.wait_ge(S("dt_onep"), 1)
                act.activation(dtmp[0:64, :], dtmp[0:64, :], ACT.Ln).then_inc(S("dt_ln"), 1)
                act.wait_ge(S("dt_end"), 1)
                act.activation(dwe[0:64, :], dwe[0:64, :], ACT.Exp).then_inc(S("dt_wend"), 1)
                act.wait_ge(S("dt_cols"), 1)
                for dst, o in ((dtT, 0), (dcT, 128), (dwT, 256)):
                    act.activation(dst[:, :, :], mix[:, 0, o:o + 128].rearrange("p (a b) -> p a b", a=2), ACT.Copy)

            def ssd_features(g, q):
                xc, bcc = S_XC[g % 2], S_BCC[g % 2]
                if q >= 6:
                    evac(G[f"ssdz{g}"], 0, q - 6, 0, S_Z[g % 2][:, 2 * q - 12:2 * q - 10, :], both, ACT.Copy)
                    return
                b = wait_ready(act, G[f"ssdx{g}" if q < 4 else f"ssdbc{g}"], 0, q // 2 % 2, q % 2)
                c = ssd_channel(g, q)
                act.eng.activation(S_X[:, q, :] if q < 4 else S_BC[:, q - 4, :], acc[b], ACT.Copy)
                act.eng.activation(xc[:, q, :] if q < 4 else bcc[q - 4], acc[b], ACT.Identity,
                                   scale=col("ssd_conv_w_2", 24 + c), bias=col("ssd_conv_b_2", c)).then_inc(free[b], 1)
                act.drain().then_inc(S("ssd_raw"), 1)

            def ssd_silu(g):
                act.wait_ge(S("ssd_cv"), g + 1)
                act.eng.activation(S_XC[g % 2], S_XC[g % 2], ACT.Silu)
                for v in S_BCC[g % 2]:
                    act.eng.activation(v, v, ACT.Silu)
                act.eng.activation(S_Z[g % 2], S_Z[g % 2], ACT.Silu)
                act.drain().then_inc(S("ssd_conv"), 1)

            def ssd_group(g):
                act.wait_ge(S("ssd_xT"), g + 1)
                act.activation(S_XT[:, :, :], mix[:, :, :], ACT.Copy).then_inc(S("ssd_xT_sb"), 1)
                act.wait_ge(S("ssd_cb"), g + 1)
                act.activation(S_BT[:, :, :], mix[:, 0, 0:T].rearrange("p (a b) -> p a b", a=2), ACT.Copy).then_inc(S("ssd_bt"), 1)
                act.wait_ge(S("ssd_state"), g + 1)
                act.activation(S_ST[:, :, :], mix[:, 2:4, :], ACT.Copy).then_inc(S("ssd_state_sb"), 1)
                if g < 3:
                    ssd_features(g + 1, 0)
                    ssd_features(g + 1, 1)
                for i in range(16):
                    n = 16 * g + i
                    act.wait_ge(S("ssd_row"), n + 1)
                    if n >= 2:
                        act.wait_ge(S("ssd_cw"), n - 1)
                    act.activation(S_ER[:, n % 2, :], mix[:, i % 2, 0:T], ACT.Exp).then_inc(S("ssd_erow"), 1)
                    act.wait_ge(S("ssd_dmin"), n + 1)
                    act.activation(S_DW[:, n % 2, :], S_DW[:, n % 2, :], ACT.Exp).then_inc(S("ssd_edec"), 1)
                    if i % 2 == 0 and 2 <= i < 14 and g < 3:
                        ssd_features(g + 1, 1 + i // 2)
                if g < 3:
                    ssd_silu(g + 1)
                act.wait_ge(S("ssd_yz"), g + 1)
                act.activation(S_SQ[:, :, :], S_Y[:, 4 * g:4 * g + 4, :], ACT.Square).then_inc(S("ssd_gsq"), 1)
                act.wait_ge(S("ssd_gms"), g + 1)
                act.activation(S_STD, mix[:, 0, 0:T], ACT.Sqrt, bias=eps_rms).then_inc(S("ssd_gstd"), 1)

            def ffn_up(l):
                g = G[f"up{l}"]
                w = 512 if l == 0 else T

                def silu(par, count):
                    act.wait_ge(S("up_conv"), count)
                    act.activation(uconv[:, par, 2:4, 0:w], uconv[:, par, 2:4, 0:w], ACT.Silu).then_inc(S("up_silu"), 1)

                def body(it, u):
                    par = u // 2
                    for j in range(2):
                        c = 2 * (u % 2) + j
                        if j == 0 or l == 0:
                            b = wait_ready(act, g, it, u, j if l == 0 else 0)
                        if l == 0 and not (isinstance(it, int) and 4 * it + u + 1 == g.n):
                            high_kept(g, it, u + 1, j)
                        if u % 2 == 0 and j == 0:
                            if isinstance(it, int) and it == 0:
                                if u == 0:
                                    act.wait_ge(S("up_zero"), l + 1)
                            else:
                                act.wait_ge(S("up_used"), it * 2 + (11 * l + par - 1))
                        o = j * T if l == 1 else T
                        grid = lambda v: v.rearrange("p (r w) -> p r w", r=GRID_ROWS)
                        lo = T if l == 0 else 0
                        middle, bias = ffn_tap(l, it, 4, u % 2, j, par), ffn_bias(l, it, u % 2, j, par)
                        act.eng.activation(
                            upad_l[:, par, c, :].rearrange("p (r w) -> p r w", r=GRID_ROWS + 2)[:, 1:GRID_ROWS + 1, 1:GRID_W + 1],
                            grid(acc[b][:, o:o + T]), ACT.Copy)
                        if l == 0:
                            act.eng.activation(upad_c[:, par, c, 1:T + 1], acc[b][:, 0:T], ACT.Copy)
                        last = act.eng.activation(uconv[:, par, c, 0:w], acc[b][:, 0:512] if l == 0 else acc[b][:, o:o + T],
                                                  ACT.Identity, scale=middle, bias=bias)
                        if j == 1 or l == 0:
                            last.then_inc(free[b], 1)
                    if u % 2 == 1:
                        act.drain().then_inc(S("up_raw"), 1)
                        if not (isinstance(it, int) and it == 0 and par == 0):
                            silu(1 - par, it * 2 + (11 * l + par))

                groups(act, g, body, peel=True)
                silu(0, 11 * l + 11)

            act.wait_ge(S("cols_loaded"), 16)
            act.activation(cond[:, :], cols[:, COL["c"]:COL["c"] + 8], ACT.Silu)
            act.activation(cond2[:, :, 0], cols[:, COL["c_2"]:COL["c_2"] + 8], ACT.Silu)
            act.activation(cond2[:, :, 1], cols[:, COL["c_ctx_2"]:COL["c_ctx_2"] + 8], ACT.Silu)
            act.drain().then_inc(S("cond_ready"), 1)
            act.wait_ge(S("lb_diff"), 1)
            act.activation(small[:, 0:8], small[:, 0:8], ACT.Exp).then_inc(S("lb_exp"), 1)
            act.wait_ge(S("bias_mm"), 1)
            act.activation(bias_rows[0:4, :], mix[0:4, 0, 0:384], ACT.Copy).then_inc(S("bias_rows"), 1)
            n = 0
            stage_end(act, count)
            for l in range(DEPTH):
                for f in range(2):
                    if f == 1:
                        g = G[f"mix{l}"]
                        for u in range(15):
                            if u == 0:
                                evac(g, 0, u, 0, apad[:, :, PAD:PAD + T], both, ACT.Copy)
                            elif u == 5:
                                b = wait_ready(act, g, 0, u)
                                act.activation(kiT, acc[b][:, 0:T], ACT.Copy)
                                act.activation(wi[:, :, :], acc[b][:, T:T + 16].rearrange("p (a b) -> p a b", a=2), ACT.Copy)\
                                   .then_inc(free[b], 1)
                            else:
                                dst, func, scale = {
                                    1: (qT[:, :, :], ACT.Copy, 1.0), 2: (kT[:, :, :], ACT.Copy, 1.0),
                                    3: (qiT[:, 0:2, :], ACT.Copy, 1.0), 4: (qiT[:, 2:4, :], ACT.Copy, 1.0),
                                    6: (vt[:, :, :], ACT.Copy, 1.0), 7: (hi[:, :, 0:T], ACT.Copy, 1.0),
                                    8: (hi[:, :, T:512], ACT.Copy, 1.0), 9: (qf[:, 0:2, :], ACT.Silu, 1.0),
                                    10: (qf[:, 2:4, :], ACT.Silu, 1.0), 11: (hgs[:, 0:2, :], ACT.Silu, 1.0),
                                    12: (hgs[:, 2:4, :], ACT.Silu, 1.0), 13: (kk[:, 0:2, :], ACT.Sigmoid, -1.0),
                                    14: (kk[:, 2:4, :], ACT.Sigmoid, -1.0)}[u]
                                evac(g, 0, u, 0, dst, both, func, scale)
                        stage_end(act, count)
                        pool(l)
                        stage_end(act, count)
                        attention(l)
                        stage_end(act, count)
                        hgrn(l)
                        stage_end(act, count)
                        stage_end(act, count)
                        layer_norm(n, l, 1)
                        n += 1
                    g = G[f"in{l}{f}"]
                    if (l, f) == (0, 0):
                        high(g, 0, 0)

                    def split_and_gate(it, u, g=g):
                        if not (isinstance(it, int) and 4 * it + u + 1 == g.n):
                            high(g, it, u + 1)
                        if u % 2 == 0:
                            evac(g, it, u, 0, hid_raw[:, bass.ds(it * 4 + u, 2), :], both, ACT.Silu)

                    groups(act, g, split_and_gate, peel=True)
                    wait_used(act, g, 5, 1, 1)
                    for i in range(8):
                        high(G[f"out{l}{f}"], 0, i)
                    layer_norm(n, l, 2 * f)
                    n += 1
                    if l == DEPTH - 1 and f == 1:
                        stage_end(act, count)
            rms = 0
            for l in range(DEPTH):
                gain, mod2 = (lambda k, v: gain2[:, k, v:v + 1]), mods2[:, l, :, :]
                rms_norm(rms, both, gain, mod2[:, 0:8, :])
                rms += 1
                if l == 0:
                    g = G["even"]
                    feat = {0: gq, 1: gk, 4: ey[:, 0:2, :], 5: ey[:, 2:4, :], 12: ey[:, 4:6, :], 13: ey[:, 6:8, :]}
                    func = {4: ACT.Silu, 5: ACT.Silu, 12: ACT.Sigmoid, 13: ACT.Sigmoid}
                    b = wait_ready(act, G["evengate"], 0, 0)
                    for j in range(2):
                        high_kept(g, 0, 0, j)
                    act.activation(rows16[0:16, :], acc[b][0:16, :], ACT.Identity, bias=col("ml_gate_b_2", 0, 0, 16))
                    act.activation(rows16[32:64, :], acc[b][32:64, :], ACT.Copy)
                    act.activation(rows16[64:96, :], acc[b][64:96, :], ACT.Copy).then_inc(free[b], 1)
                    act.drain().then_inc(S("rank_ready"), 1)
                    ml_rows()
                    for u in range(14):
                        if u in (2, 3, 10, 11):
                            act.wait_ge(S("low_made"), split_count(g, 0, u, 1))
                            act.wait_ge(first_used, G["evengate"].s0 + (2, 3, 10, 11).index(u) + 1)
                            for j in range(2):
                                high_kept(g, 0, u + 1, j)
                        for r in range(2):
                            if u not in (2, 3, 10, 11, 13):
                                wait_ready(act, g, 0, u, r)
                                high_kept(g, 0, u + 1, r)
                            if u in (2, 3, 10, 11):
                                dst = gv if u < 4 else mv
                                evac(g, 0, u, r, dst[:, 2 * r:2 * r + 2, u % 2 * T:u % 2 * T + T], both, ACT.Copy)
                            elif 6 <= u < 10:
                                c = 2 * (u - 6) + r
                                b = wait_ready(act, g, 0, u, r)
                                act.eng.activation(mqk_raw[:, c, :], acc[b], ACT.Copy)
                                act.eng.activation(mqk[:, c, :], acc[b], ACT.Identity, scale=col("ml_conv_w_2", 8 + c),
                                                   bias=col("ml_conv_b_2", c)).then_inc(free[b], 1)
                                act.drain().then_inc(S("ml_raw"), 1)
                            else:
                                evac(g, 0, u, r, feat[u][:, r, :], both, func.get(u, ACT.Copy), 0.125 if u == 0 else 1.0)
                        if u >= 12:
                            c = 4 * (u - 12)
                            act.wait_ge(S("ml_conv"), c + 4)
                            act.activation(mqk[:, c:c + 4, :], mqk[:, c:c + 4, :], ACT.Silu)
                    act.wait_ge(S("ml_cols"), 1)
                    act.activation(bcol[:, :, :], mix[:, 0, 0:64].rearrange("p (a b) -> p a b", a=4), ACT.Copy).then_inc(S("ml_bcol"), 1)
                    stage_end(act, count)
                    gla()
                    mlstm()
                    stage_end(act, count)
                else:
                    ssd_rates()
                    stage_end(act, count)
                    for q in range(8):
                        ssd_features(0, q)
                    ssd_silu(0)
                    for g in range(4):
                        ssd_group(g)
                    stage_end(act, count)
                rms_norm(rms, both if l == 0 else lat, gain, mod2[:, 24:32, :])
                rms += 1
                ffn_up(l)
            rms_norm(rms, lat, lambda k, v: col("final_norm_g_2", k))
            act.drain().then_inc(S("final"), 1)

        @block.vector
        def _(dve):
            dve = InOrder(dve)
            count = [0]

            def stt(out, a, s, b, op0, op1, **kw):
                return dve.scalar_tensor_tensor(out=out, in0=a, scalar=s, in1=b, op0=op0, op1=op1, **kw)

            def bc(v, n):
                return v.unsqueeze(1).to_broadcast([v.shape[0], n, v.shape[1]])

            def cond_weigh(phase, i, e):
                n0 = CARRY[phase][0]
                conds = [cond2[:, :, 0], cond2[:, :, 1]] if n0 >= MOD0 else [cond]
                slot = (n0 + e) % 2
                w, parts = cond_slot(phase, slot), [p[slot] for p in cond_part]
                dve.wait_ge(cond_landed[slot], i * 8 + (8 * (n0 - slot) + 16))
                if not isinstance(i, int) or i + n0 >= 2:
                    dve.wait_ge(S("cond_summed"), i + (n0 - 1))
                for k in range(KD):
                    for c, part in zip(conds, parts):
                        if k == 0:
                            dve.eng.tensor_tensor(part, w[:, 0, :], c[:, 0:1].to_broadcast([P, PANEL]), ALU.mult)
                        else:
                            dve.eng.scalar_tensor_tensor(out=part, in0=w[:, k, :], scalar=c[:, k:k + 1], in1=part, op0=ALU.mult, op1=ALU.add)
                    if k < KD - 1:
                        dve.drain()
                dve.drain().then_inc(S("cond_part"), 1)

            def cond_take(phase):
                n0, cnt = CARRY[phase]
                dve.wait_ge(S("cond_summed"), n0 + cnt)
                src = mix[:, cond_bank(phase), :]
                for first, size, table in [(l * ADA, ADA, mods1[:, l, :]) for l in range(DEPTH)] + \
                                          [(MOD0 + l * MOD, MOD, mods2[:, l, :, :]) for l in range(DEPTH)]:
                    a, b = max(n0, first), min(n0 + cnt, first + size)
                    if a >= b:
                        continue
                    t0, t1, s0, s1 = 2 * (a - first), 2 * (b - first), 2 * (a - n0), 2 * (b - n0)
                    if n0 >= MOD0:
                        bias = cols[:, COL["mod_b_2"] + 2 * (a - MOD0):COL["mod_b_2"] + 2 * (b - MOD0)]
                        for v in range(2):
                            dve.tensor_tensor(table[:, t0:t1, v], src[:, T * v + s0:T * v + s1], bias, ALU.add)
                    else:
                        bias = cols[:, COL["b_ada"] + 2 * a:COL["b_ada"] + 2 * b]
                        dve.tensor_tensor(table[:, t0:t1], src[:, s0:s1], bias, ALU.add)
                        for j in (0, 2):
                            if t0 <= 24 * j + 16 and 24 * j + 24 <= t1:
                                gt = table[:, 24 * j + 16:24 * j + 24]
                                dve.tensor_scalar(gt, gt, 0.5, None, ALU.mult)

            def first_input():
                for k in range(KD):
                    dve.eng.tensor_scalar(h_raw[:, k, :], X[:, k, lat], mods1[:, 0, 8 + k:9 + k], mods1[:, 0, k:k + 1], ALU.mult, ALU.add)
                dve.drain()
                dve.tensor_copy(h_hi, h_raw)
                dve.tensor_tensor(h_lo, h_raw, h_hi, ALU.subtract)
                dve.drain().then_inc(S("h_ready"), KD)
                dve.tensor_scalar(X[:, :, lat], X[:, :, lat], float(ALPHA), None, ALU.mult)
                dve.drain()

            def residual(g, l, gate0, norms_done):
                mod1 = mods1[:, l, :]
                if norms_done:
                    dve.wait_ge(S("x_ready"), norms_done)
                for n in range(4):
                    b = wait_ready(dve, g, 0, n)
                    for j in range(2):
                        k = 2 * n + j
                        i = stt(X[:, k, lat], acc[b][:, j * T:j * T + T], mod1[:, gate0 + k:gate0 + k + 1], X[:, k, lat], ALU.mult, ALU.add)
                    i.then_inc(free[b], 1)

            def norm_vectors(l, j):
                if j == 2 and l + 1 == DEPTH:
                    return
                c = (3 * l + j) * KD
                g, b = cols[:, COL["ln_g"] + c:COL["ln_g"] + c + KD], cols[:, COL["ln_b"] + c:COL["ln_b"] + c + KD]
                m = mods1[:, l + (j + 1) // 3, 24 * ((j + 1) % 3):]
                dve.eng.tensor_tensor(ln_next[:, 0, :], g, m[:, 8:16], ALU.mult)
                dve.eng.tensor_tensor(ln_next[:, 1, :], b, m[:, 8:16], ALU.mult)
                dve.eng.tensor_scalar(ln_next[:, 2, :], g, float(ALPHA), None, ALU.mult)
                dve.eng.tensor_scalar(ln_next[:, 3, :], b, float(ALPHA), None, ALU.mult)
                dve.drain()
                dve.tensor_tensor(ln_next[:, 1, :], ln_next[:, 1, :], m[:, 0:8], ALU.add)

            def layer_norm(n, l, j):
                norm_vectors(l, j)
                dve.wait_ge(S("mean_ready"), n + 1)
                for k in range(KD):
                    dve.tensor_tensor(X[:, k, lat], X[:, k, lat], mix[:, 0, 0:T], ALU.subtract).then_inc(S("centred"), 1)
                dve.wait_ge(S("std_ready"), n + 1)
                dve.reciprocal(std[:, 0:T], std[:, 0:T])
                dve.drain()
                for k in range(KD):
                    dve.tensor_tensor(X[:, k, lat], X[:, k, lat], std[:, 0:T], ALU.mult).then_inc(S("scaled"), 1)
                if j == 1 or (j == 2 and l + 1 < DEPTH):
                    parts = KD * (n - n // 3 - 1)
                    for k in range(KD):
                        dve.wait_ge(S("h_parts"), parts + k + 1)
                        dve.tensor_tensor(h_lo[:, k, :], h_raw[:, k, :], h_hi[:, k, :], ALU.subtract).then_inc(S("h_ready"), 1)

            def rms_norm(n, sel):
                w = sel.stop - sel.start
                dve.wait_ge(S("rms_std"), n + 1)
                dve.reciprocal(std[:, 0:w], std[:, 0:w])
                dve.drain()
                for k in range(KD):
                    dve.tensor_tensor(H[:, k, sel], X[:, k, sel], std[:, 0:w], ALU.mult).then_inc(S("rms_scaled"), 1)
                if n < 2:
                    for k in range(KD):
                        dve.wait_ge(S("rms_parts"), n * KD + k + 1)
                        dve.tensor_tensor(in_lo[n][k], in_raw[n][k], H_r[:, k, :], ALU.subtract).then_inc(S("rms_out"), 1)

            def pool(l):
                src = apad
                for i, w in enumerate((1, 2, 4, 8)):
                    dve.tensor_copy(win[i][:, :, 0:w], src[:, :, 0:w])
                    dve.tensor_tensor(win[i][:, :, w:PAD + T], src[:, :, w:PAD + T], src[:, :, 0:PAD + T - w], ALU.add)
                    dve.drain()
                    src = win[i]
                cnt = const("invcnt").rearrange("p (a t) -> p a t", a=2)
                for i in range(4):
                    r = slice(64 * (i % 2), 64 * (i % 2) + 64)
                    dve.tensor_tensor(pdiff[r, i // 2, :], win[i][r, i // 2, PAD:PAD + T], cnt[r, i // 2, :], ALU.mult)
                dve.drain()
                dve.tensor_tensor(pdiff[:, :, :], pdiff[:, :, :], apad[:, :, PAD:PAD + T], ALU.subtract).then_inc(S("pool_diff"), 1)

            def attention(l):
                for qb in range(2):
                    n = P * (qb + 1)
                    off = 0 if qb == 1 else P
                    for h in range(8):
                        if h % 2 == 0:
                            dve.wait_ge(S("idx_relu"), 8 * l + 4 * qb + h // 2 + 1)
                        head = 2 * (2 * (h // 2 % 2) + h % 2) + h // 4
                        w = wi[:, qb, head:head + 1]
                        if h == 0:
                            i = dve.tensor_scalar(score[:, 0:n], relu_s[:, h, 0:n], w, None, ALU.mult)
                        else:
                            i = stt(score[:, 0:n], relu_s[:, h, 0:n], w, score[:, 0:n], ALU.mult, ALU.add)
                        if h == 7:
                            i.then_inc(S("idx_sum"), 1)
                        dve.drain()
                    stt(score[:, 0:n], score[:, 0:n], IDX_SCALE, const("causal")[:, off:off + n], ALU.mult, ALU.add)
                    dve.drain()
                    src = score
                    for r in range(TOPK // 8):
                        dve.max(small[:, 16:24], src[:, 0:n])
                        dve.drain()
                        dve.match_replace(work[:, 0:n], small[:, 16:24], src[:, 0:n], GONE)
                        dve.drain()
                        src = work
                    dve.tensor_tensor(addm[:, 0:n], work[:, 0:n], score[:, 0:n], ALU.is_equal)
                    dve.drain()
                    dve.tensor_scalar(addm[:, 0:n], addm[:, 0:n], MASKED, None, ALU.mult)
                    dve.drain()
                    dve.wait_ge(S("logit_mm"), 2 * l + qb + 1)
                    lg = logit[:, qb, :, 0:n]
                    src = mix[:, 2 * qb:2 * qb + 2, :].rearrange("p a (b t) -> p (a b) t", b=2)[:, :, 0:n]
                    stt(lg, src, 64 ** -0.5, biasC[:, :, off:off + n], ALU.mult, ALU.add)
                    dve.drain()
                    dve.tensor_tensor(lg, lg, bc(addm[:, 0:n], 4), ALU.add)
                    dve.drain()
                    dve.tensor_reduce(small[:, 8 * qb:8 * qb + 4], lg, AXX, ALU.max, negate=True).then_inc(S("logit_ready"), 1)
                for qb in range(2):
                    n = P * (qb + 1)
                    dve.wait_ge(S("exp_ready"), 2 * l + qb + 1)
                    r = small[:, 8 * qb + 4:8 * qb + 8]
                    dve.reciprocal(r, r)
                    dve.drain()
                    dve.tensor_tensor(logit[:, qb, :, 0:n], logit[:, qb, :, 0:n],
                                      r.unsqueeze(2).to_broadcast([P, 4, n]), ALU.mult).then_inc(S("prob_ready"), 1)

            def halves(v, m):
                return v.rearrange("p (n two m) -> p n two m", two=2, m=m)

            def last_bc(v, e, edge, m):
                return halves(v, m)[:, :, e, edge:edge + 1].to_broadcast([P, v.shape[1] // (2 * m), m])

            def hgrn(l):
                for h in range(4):
                    dve.tensor_scalar(kk[:, h, :], kk[:, h, :], one_lb[:, l, h:h + 1], None, ALU.mult)
                dve.drain()
                dve.tensor_scalar(pref, kk[:, :, :].rearrange("p a b -> p (a b)"), KEY_MAX, -1.0, ALU.min, ALU.mult)
                dve.drain().then_inc(S("hg_key"), 1)
                dve.memset(suff, 0.0).then_inc(S("hg_zero"), 1)
                mask = const("tree_f")
                kf, qq = kk[:, :, :].rearrange("p a b -> p (a b)"), qf[:, :, :].rearrange("p a b -> p (a b)")

                def take(i):
                    bank = 2 * (i % 2)
                    dve.wait_ge(S("hg_mm"), 9 * l + i + 1)
                    src = mix[:, bank:bank + 2, :].rearrange("p a (h t) -> p (a h) t", h=4)
                    if i == 0:
                        dve.tensor_tensor(pairs[:, :, :], src, bc(ident, 8), ALU.mult).then_inc(S("hg_acc"), 1)
                    elif i < 8:
                        level = mask[:, (i - 1) * P:i * P].bitcast(mybir.dt.uint32)
                        dve.eng.copy_predicated(pairs[:, :, :], bc(level, 8), src).then_inc(S("hg_acc"), 1)
                        dve.drain()
                    else:
                        dve.tensor_copy(offd[:, :, :], src[:, 0:4, :])
                        dve.drain().then_inc(S("hg_acc"), 1)

                for lv in range(8):
                    m = 1 << lv
                    x = halves(treeX[lv % 2], m)
                    dve.wait_ge(S("hg_exp"), 8 * l + lv + 1)
                    if lv < 7:
                        dve.tensor_tensor(halves(suff, m)[:, :, 0, :], halves(suff, m)[:, :, 0, :], last_bc(pref, 1, m - 1, m), ALU.add)
                        dve.drain()
                        dve.tensor_tensor(halves(pref, m)[:, :, 1, :], halves(pref, m)[:, :, 1, :], last_bc(pref, 0, m - 1, m), ALU.add)
                        dve.drain().then_inc(S("hg_sums"), 1)
                    dve.tensor_tensor(x[:, :, 0, :], x[:, :, 0, :], halves(kf, m)[:, :, 0, :], ALU.mult)
                    dve.tensor_tensor(x[:, :, 1, :], x[:, :, 1, :], halves(qq, m)[:, :, 1, :], ALU.mult)
                    dve.drain().then_inc(S("hg_x"), 1)
                    take(lv)
                take(8)
                dve.wait_ge(S("hg_std"), l + 1)
                dve.reciprocal(ostd, ostd)
                dve.drain()
                dve.tensor_tensor(onorm[:, :, :].rearrange("p a b -> p (a b)"), mix[:, 2:4, :].rearrange("p a b -> p (a b)"), ostd, ALU.mult)
                dve.drain()
                for h in range(4):
                    stt(ymix[:, 4 + h, :], onorm[:, h, :], col("hgrn_norm_g", 4 * l + h), hgs[:, h, :], ALU.mult, ALU.mult)

            def branch(l):
                g = G[f"branch{l}"]
                for u in range(4):
                    for r in range(3):
                        b = wait_ready(dve, g, 0, u, r)
                        src = acc[b][:, :].rearrange("p (a t) -> p a t", a=2)
                        dst = merged[:, 2 * u:2 * u + 2, :]
                        gt = gates[:, 8 * r + 2 * u:8 * r + 2 * u + 2, :]
                        if r == 0:
                            dve.tensor_tensor(dst, src, gt, ALU.mult).then_inc(free[b], 1)
                        else:
                            dve.tensor_tensor(mtmp[:, :, :], src, gt, ALU.mult).then_inc(free[b], 1)
                            dve.drain()
                            dve.tensor_tensor(dst, dst, mtmp[:, :, :], ALU.add)
                        dve.drain()

            def gla():
                for d in range(2):
                    dve.wait_ge(S("decay_ln"), d + 1)
                    v = gX[0][:, :, :].rearrange("p a b -> p (a b)")
                    stt(logd[:, d, :], v, 0.0, gX[1][:, :, :].rearrange("p a b -> p (a b)"), ALU.min, ALU.subtract)
                    dve.drain()
                    dve.tensor_scalar(logd[:, d, :], logd[:, d, :], 1.0 / 16.0, None, ALU.mult)
                    dve.drain().then_inc(S("decay_log"), 1)
                dve.memset(gsuff[:, :, :], 0.0)
                dve.drain().then_inc(S("gla_sums"), 2)

                def take(n):
                    lv, d = n // 2, n % 2
                    if lv == 7:
                        dve.wait_ge(S("gla_mm"), 31 + d)
                        dve.tensor_copy(goff[:, 8 * d:8 * d + 8, :].rearrange("p a t -> p (a t)"),
                                        gla_banks[d][:, 0:2, :].rearrange("p a t -> p (a t)")).then_inc(S("gla_acc"), 1)
                        return
                    for hf in range(2):
                        dve.wait_ge(S("gla_mm"), 2 + 2 * n + hf + 1)
                        src = gla_banks[d][:, 2 * hf:2 * hf + 2, :].rearrange("p a (h t) -> p (a h) t", h=4)
                        mask = const("tree_f" if d == 0 else "tree_b", lv * P, P)
                        dve.eng.copy_predicated(gpairs[:, 8 * hf:8 * hf + 8, :], bc(mask.bitcast(mybir.dt.uint32), 8), src).then_inc(S("gla_acc"), 1)
                        dve.drain()

                for hf in range(2):
                    dve.wait_ge(S("gla_mm"), hf + 1)
                    src = mix[:, 2 * hf:2 * hf + 2, :].rearrange("p a (h t) -> p (a h) t", h=4)
                    stt(gpairs[:, 8 * hf:8 * hf + 8, :], src, 2.0, bc(ident, 8), ALU.mult, ALU.mult).then_inc(S("gla_acc"), 1)
                kf, qq = gk[:, :, :].rearrange("p a b -> p (a b)"), gq[:, :, :].rearrange("p a b -> p (a b)")
                for n in range(18):
                    lv, d = n // 2, n % 2
                    m = 1 << lv
                    x = halves(gX[d].rearrange("p c t -> p (c t)"), m)
                    pref, suff = gpref[:, d, :], gsuff[:, d, :]
                    e, o = (0, 1) if (d == 0 or lv == 8) else (1, 0)
                    edge = m - 1 if d == 0 else 0
                    dve.wait_ge(S("gla_exp"), n + 1)
                    dve.eng.tensor_tensor(x[:, :, e, :], x[:, :, e, :], halves(kf, m)[:, :, e, :], ALU.mult)
                    dve.tensor_tensor(x[:, :, o, :], x[:, :, o, :], halves(qq, m)[:, :, o, :], ALU.mult)
                    dve.drain().then_inc(S("gla_x"), 1)
                    if lv < 8:
                        dve.tensor_tensor(halves(suff, m)[:, :, e, :], halves(suff, m)[:, :, e, :], last_bc(pref, o, edge, m), ALU.add)
                        dve.tensor_tensor(halves(pref, m)[:, :, o, :], halves(pref, m)[:, :, o, :], last_bc(pref, e, edge, m), ALU.add)
                        dve.drain().then_inc(S("gla_sums"), 1)
                    if 1 <= n < 17:
                        take(n - 1)
                dve.wait_ge(S("gla_mm"), 33)
                dve.tensor_copy(gcross[:, :, :, :], mix[:, :, :].rearrange("p h (s t) -> p s h t", s=2))
                dve.drain().then_inc(S("gla_acc"), 1)
                head_reciprocal(0)
                for h in range(4):
                    dve.eng.scalar_tensor_tensor(out=gv[:, h, :], in0=gv[:, h, :], scalar=col("gla_norm_g_2", h), in1=mix[:, h, :], op0=ALU.mult, op1=ALU.mult)
                dve.drain().then_inc(S("head_normed"), 1)
                dve.tensor_tensor(ey[:, 0:4, :], gv[:, :, :], ey[:, 0:4, :], ALU.mult)

            def head_reciprocal(n):
                dve.wait_ge(S("head_std"), n + 1)
                dve.reciprocal(head_std, head_std)
                dve.drain().then_inc(S("head_rec"), 1)
                dve.wait_ge(S("head_bc"), n + 1)

            def outer_taps(dst, src, w, c, nch, nst):
                s2 = src.rearrange("p (s t) -> p s t", s=nst)
                d2 = dst.rearrange("p (s t) -> p s t", s=nst)
                stt(d2[:, :, 1:T], s2[:, :, 0:T - 1], col(w, c), d2[:, :, 1:T], ALU.mult, ALU.add)
                dve.drain()
                return stt(d2[:, :, 0:T - 1], s2[:, :, 1:T], col(w, 2 * nch + c), d2[:, :, 0:T - 1], ALU.mult, ALU.add)

            def ml_rows():
                dve.wait_ge(S("ml_ln"), 1)
                stt(lsg[:, :], rows16[0:16, :], 0.0, tmp16[:, :], ALU.min, ALU.subtract)
                dve.memset(tmp16[:, :], 1.0)
                dve.drain()
                dve.tensor_tensor_scan(cum16[:, :], tmp16[:, :], lsg[:, :], 0.0, ALU.mult, ALU.add)
                dve.drain()
                dve.tensor_tensor(tmp16[:, :], lsg[:, :], cum16[:, :], ALU.subtract)
                dve.drain()
                dve.tensor_scalar(tmp16[:, 0:T], tmp16[:, 0:T], cum16[:, T - 1:T], None, ALU.add)
                dve.tensor_scalar(tmp16[:, T:512], tmp16[:, T:512], cum16[:, 511:512], cum16[:, T - 1:T], ALU.add, ALU.add)
                dve.drain()
                dve.tensor_tensor(tmp16[:, :], tmp16[:, :], cum16[:, :], ALU.subtract)
                dve.drain()
                stt(cum16[:, :], tmp16[:, :], bwd_rows, cum16[:, :], ALU.mult, ALU.add)
                dve.drain().then_inc(S("ml_rows"), 1)

            def mlstm():
                dve.wait_ge(S("masks_loaded"), 16)
                dve.wait_ge(S("ml_rall"), 8)
                scale = 128 ** -0.5
                dve.tensor_reduce(ml_max[:, 0:8], rall[:, :, 0:T], AXX, ALU.max)

                def decays(t):
                    dlog, sm = dlogs[t % 2], 24 * (t % 2)
                    o = 0 if t < 2 else T
                    bt = bcol[:, t, :].rearrange("p (d w) -> p d w", d=2)[:, :, 4:8]
                    for i in range(8):
                        h, d = i % 4, i // 4
                        mask = const("mneg", (2 * d + t % 2) * T, T)
                        dve.eng.scalar_tensor_tensor(out=dlog[:, i, o:o + T], in0=rall[:, i, o:o + T], scalar=bt[:, d, h:h + 1], in1=mask, op0=ALU.add, op1=ALU.add)
                    dve.drain()
                    m = small[:, sm:sm + 8]
                    dve.tensor_reduce(m, dlog[:, :, o:o + T], AXX, ALU.max)
                    split = lambda v: v.rearrange("p (d w) -> p d w", d=2)
                    if t >= 2:
                        dve.tensor_tensor(split(ml_max[:, 8:16]), split(ml_max[:, 0:8]), bt, ALU.add)
                        dve.tensor_tensor(m, m, ml_max[:, 8:16], ALU.max)
                    dve.tensor_scalar(m, m, 0.0, -1.0, ALU.max, ALU.mult)
                    if t >= 2:
                        b = 16 + 8 * (t % 2)
                        dve.tensor_tensor(split(ml_max[:, b:b + 8]), split(m), bt, ALU.add)
                    dve.drain().then_inc(S("ml_max"), 1)

                decays(0)
                for t in range(4):
                    w = T if t < 2 else 2 * T
                    if t < 3:
                        decays(t + 1)
                    dlog, sm = dlogs[t % 2], 24 * (t % 2)
                    den = small[:, sm + 16:sm + 24]
                    dve.wait_ge(S("ml_exp"), t + 1)
                    dve.wait_ge(S("ml_scores"), t + 1)
                    for i in range(8):
                        dve.eng.scalar_tensor_tensor(out=dlog[:, i, 0:w], in0=dlog[:, i, 0:w], scalar=scale, in1=mix[:, i % 4, 0:w],
                                                     op0=ALU.mult, op1=ALU.mult, accum_out=den[:, i:i + 1])
                    dve.drain()
                    stt(den, den, -1.0, den, ALU.mult, ALU.max)
                    dve.tensor_tensor(den, den, small[:, sm + 8:sm + 16], ALU.max)
                    dve.reciprocal(den, den)
                    for h in range(4):
                        dve.eng.tensor_scalar(psum2[:, h, 0:w], dlog[:, h, 0:w], den[:, h:h + 1], None, ALU.mult)
                    dve.drain()
                    for h in range(4):
                        dve.eng.scalar_tensor_tensor(out=psum2[:, h, 0:w], in0=dlog[:, 4 + h, 0:w], scalar=den[:, 4 + h:5 + h],
                                                     in1=psum2[:, h, 0:w], op0=ALU.mult, op1=ALU.add)
                    dve.drain().then_inc(S("ml_prob"), 1)
                dve.wait_ge(S("ml_h"), 4)
                dve.tensor_tensor(mqk[:, 0:4, :], mqk[:, 0:4, :], ey[:, 4:8, :], ALU.mult).then_inc(S("ml_gated"), 1)
                head_reciprocal(1)
                for h in range(4):
                    stt(ey[:, 4 + h, :], mqk[:, h, :], col("ml_norm_g_2", h), mix[:, h, :], ALU.mult, ALU.mult)

            def ssd_rates():
                dve.wait_ge(S("dt_exp"), 1)
                e, u, d64 = dcum[0:64, :], dtmp[0:64, :], dtr[0:64, :]
                dve.tensor_scalar(u, e, 1.0, None, ALU.add)
                dve.drain().then_inc(S("dt_onep"), 1)
                sp_q, sp_m = S_X[0:64, 0, :], S_X[0:64, 1, :]
                dve.tensor_scalar(sp_q, e, 1.0, -1.0, ALU.add, ALU.add)
                dve.drain()
                dve.tensor_scalar(sp_m, sp_q, 0.0, None, ALU.is_equal)
                dve.drain()
                dve.tensor_tensor(sp_q, sp_q, sp_m, ALU.add)
                dve.drain()
                dve.reciprocal(sp_q, sp_q)
                dve.drain()
                dve.wait_ge(S("dt_ln"), 1)
                dve.tensor_tensor(u, u, sp_q, ALU.mult)
                dve.drain()
                dve.tensor_tensor(u, u, sp_m, ALU.add)
                dve.drain()
                dve.tensor_tensor(u, u, e, ALU.mult)
                dve.drain()
                stt(d64, d64, 0.0, u, ALU.max, ALU.add)
                dve.tensor_scalar(negA, negA, -1.0, None, ALU.mult)
                dve.drain()
                dta = u
                dve.tensor_scalar(dta, d64, negA, None, ALU.mult)
                dve.memset(sp_q, 1.0)
                dve.drain()
                f = dcum[0:64, :]
                for s in range(2):
                    dve.tensor_tensor_scan(f[:, s * T:s * T + T], sp_q[:, 0:T], dta[:, s * T:s * T + T], 0.0, ALU.mult, ALU.add)
                dve.drain()
                we = dwe[0:64, :]
                dve.tensor_scalar(we[0:32, :], f[0:32, 0:T], -1.0, f[0:32, T - 1:T], ALU.mult, ALU.add)
                dve.tensor_tensor(we[32:64, :], f[32:64, 0:T], dta[32:64, 0:T], ALU.subtract)
                dve.tensor_tensor(sp_m[32:64, 0:T], dta[32:64, lat], f[32:64, lat], ALU.subtract)
                dve.tensor_copy(sp_m[32:64, T:T + 1], f[32:64, 511:512])
                dve.drain().then_inc(S("dt_end"), 1)
                dve.tensor_scalar(f[32:64, lat], sp_m[32:64, 0:T], sp_m[32:64, T:T + 1], None, ALU.add)
                dve.drain()
                dve.wait_ge(S("dt_wend"), 1)
                dve.tensor_tensor(we, we, d64[:, 0:T], ALU.mult)
                dve.drain().then_inc(S("dt_rows"), 1)

            def ssd_conv(g, q):
                dve.wait_ge(S("ssd_raw"), 6 * g + q + 1)
                src = S_X[:, q, :] if q < 4 else S_BC[:, q - 4, :]
                dst = S_XC[g % 2][:, q, :] if q < 4 else S_BCC[g % 2][q - 4]
                outer_taps(dst, src, "ssd_conv_w_2", ssd_channel(g, q), 24, 2)
                if q == 5:
                    dve.drain().then_inc(S("ssd_cv"), 1)

            def ssd_group(g):
                cc, xc = S_BCC[g % 2][1], S_XC[g % 2]
                dve.wait_ge(S("ssd_xT_sb"), g + 1)
                for d in range(2):
                    for s in range(2):
                        w = dwT[:, s, 32 * d + 8 * g:32 * d + 8 * g + 8].unsqueeze(2).to_broadcast([P, 8, 64])
                        dve.tensor_tensor(S_XW[:, d, s, :].rearrange("p (h q) -> p h q", h=8),
                                          S_XT[:, s, :].rearrange("p (h q) -> p h q", h=8), w, ALU.mult)
                dve.drain().then_inc(S("ssd_xw"), 1)
                dve.wait_ge(S("ssd_cb"), g + 1)
                dve.wait_ge(S("ssd_bt"), g + 1)
                up, dn = const("tri", 0, P), const("tri", P, P)
                dve.tensor_tensor(S_CB[:, 0, 0:P], mix[:, 1, 0:P], up, ALU.mult)
                dve.tensor_copy(S_CB[:, 0, P:T], mix[:, 1, P:T])
                dve.tensor_tensor(S_CB[:, 0, T:T + P], mix[:, 1, T + P:512], up, ALU.mult)
                dve.tensor_tensor(S_CB[:, 1, 0:P], mix[:, 1, 0:P], dn, ALU.mult)
                dve.tensor_copy(S_CB[:, 1, P:T], mix[:, 1, T:T + P])
                dve.tensor_tensor(S_CB[:, 1, T:T + P], mix[:, 1, T + P:512], dn, ALU.mult)
                dve.drain().then_inc(S("ssd_cb_sb"), 1)
                for i in range(16):
                    pr, hh, d = i // 4, i // 2 % 2, i % 2
                    n = 16 * g + i
                    row = 32 * d + 8 * g + 2 * pr + hh
                    R = mix[:, i % 2, :]
                    W = S_DW[:, n % 2, :]
                    if n >= 2:
                        dve.wait_ge(S("ssd_ymm"), n - 1)
                    dve.wait_ge(S("ssd_erow"), n + 1)
                    cs = [dcT[:, s, row:row + 1] for s in range(2)]
                    spans = ((0, T, 0, T), (T, T + P, P, T)) if d == 0 else ((0, P, 0, P), (P, P + T, 0, T))
                    for s, (a, b, t0, t1) in enumerate(spans):
                        dve.tensor_scalar(W[:, a:b], R[:, t0:t1], cs[s], 0.0, ALU.subtract, ALU.min)
                    dve.drain().then_inc(S("ssd_dmin"), 1)
                    dve.tensor_tensor(S_CW[:, n % 2, :], S_ER[:, n % 2, :], cc[:, lat], ALU.mult)
                    dve.drain().then_inc(S("ssd_cw"), 1)
                    dve.wait_ge(S("ssd_edec"), n + 1)
                    for s, (a, b, t0, t1) in enumerate(spans):
                        stt(W[:, a:b], W[:, a:b], dtT[:, s, row:row + 1], S_CB[:, d, a:b], ALU.mult, ALU.mult)
                    dve.drain().then_inc(S("ssd_w"), 1)
                    if g < 3 and i in (1, 2, 3, 5, 7, 9):
                        ssd_conv(g + 1, (1, 2, 3, 5, 7, 9).index(i))
                    if i % 4 == 1 and i >= 4:
                        ssd_take(g, i // 4 - 1)
                ssd_take(g, 3)
                dve.drain()
                dve.tensor_tensor(S_Y[:, 4 * g:4 * g + 4, :], S_Y[:, 4 * g:4 * g + 4, :], S_Z[g % 2], ALU.mult)\
                   .then_inc(S("ssd_yz"), 1)
                dve.wait_ge(S("ssd_gstd"), g + 1)
                dve.reciprocal(S_STD, S_STD)
                dve.drain()
                for c in range(4):
                    k = 4 * g + c
                    stt(S_Y[:, k, :], S_Y[:, k, :], col("ssd_norm_g_2", k), S_STD, ALU.mult, ALU.mult)

            def ssd_take(g, pr):
                dve.wait_ge(S("ssd_ymm"), 16 * g + 4 * pr + 4)
                k = 4 * g + pr
                stt(S_Y[:, k, :], S_XC[g % 2][:, pr, lat], col("ssd_d_2", k), mix[:, 2 + pr % 2, 0:T], ALU.mult, ALU.add)\
                    .then_inc(S("ssd_y"), 1)

            def ffn_up(l):
                g = G[f"up{l}"]
                w = 512 if l == 0 else T
                lo = T if l == 0 else 0
                dve.memset(upad_l[:, :, :, :].rearrange("p a b c -> p (a b c)"), 0.0)
                dve.memset(upad_c[:, :, :, :].rearrange("p a b c -> p (a b c)"), 0.0)
                dve.drain().then_inc(S("up_zero"), 1)

                def gated(par, k, count):
                    dve.wait_ge(S("up_silu"), count)
                    dve.tensor_tensor(hid[:, k, 0:w], uconv[:, par, 0:2, 0:w], uconv[:, par, 2:4, 0:w], ALU.mult)
                    dve.drain().then_inc(S("up_used"), 1)

                def body(it, u):
                    if u % 2 == 0:
                        return
                    par = u // 2
                    dve.wait_ge(S("up_raw"), it * 2 + (11 * l + par + 1))
                    for tap in (0, 1, 2, 3, 5, 6, 7, 8):
                        dr, dc = tap // 3, tap % 3
                        for half in range(2):
                            for j in range(2):
                                c = 2 * half + j
                                tapw = ffn_tap(l, it, tap, half, j, par)
                                pad = upad_l[:, par, c, :].rearrange("p (r w) -> p r w", r=GRID_ROWS + 2)
                                out = uconv[:, par, c, lo:lo + T].rearrange("p (r w) -> p r w", r=GRID_ROWS)
                                dve.eng.scalar_tensor_tensor(out=out, in0=pad[:, dr:dr + 4, dc:dc + 64], scalar=tapw, in1=out, op0=ALU.mult, op1=ALU.add)
                                if l == 0 and dr == 1:
                                    oc = uconv[:, par, c, 0:T]
                                    dve.eng.scalar_tensor_tensor(out=oc, in0=upad_c[:, par, c, dc:dc + T], scalar=tapw, in1=oc, op0=ALU.mult, op1=ALU.add)
                        dve.drain()
                        if l == 0 and tap == 1 and not (isinstance(it, int) and it == 0 and par == 0):
                            k = slice(2 * par - 2, 2 * par) if isinstance(it, int) and it == 0 else bass.ds(it * 4 + (2 * par - 2), 2)
                            gated(1 - par, k, it * 2 + (11 * l + par))
                    dve.drain().then_inc(S("up_conv"), 1)

                groups(dve, g, body, peel=True)
                if l == 0:
                    gated(0, slice(20, 22), 11 * l + 11)

            def add_branch(g, gate, streams):
                for u in range(g.n // g.ppa):
                    if g.name in CARRY:
                        n = CARRY[g.name][1]
                        first, end = {"evenout": (u - 1, u), "down0": ((0, n // 2 - 1, n // 2 - 1, n)[u], (n // 2 - 1, n // 2 - 1, n, n)[u])}[g.name]
                        for i in range(max(first, 0), end):
                            cond_weigh(g.name, i, i % 2)
                    for j in range(2):
                        k = 2 * u + j
                        if len(streams) == 2 or j == 0:
                            b = wait_ready(dve, g, 0, u, j if len(streams) == 2 else 0)
                        for v in streams:
                            t = lat if v == 0 else slice(0, T)
                            src = acc[b][:, t] if len(streams) == 2 else acc[b][:, j * T:j * T + T]
                            i = stt(X[:, k, t], src, gate[:, k, v:v + 1], X[:, k, t], ALU.mult, ALU.add)
                        if len(streams) == 2 or j == 1:
                            i.then_inc(free[b], 1)
                        dve.drain().then_inc(S("rms_in"), 1)
                if g.name in CARRY:
                    cond_take(g.name)

            dve.memset(ones_d[:, :], 1.0 / D)
            dve.memset(ones_h[:, :], 1.0 / P)
            dve.wait_ge(S("cols_loaded"), 16)
            lb = [cols[:, COL["hgrn_lb"] + 4 * i:COL["hgrn_lb"] + 4 * i + 4] for i in range(DEPTH)]
            dve.tensor_tensor(small[:, 8:12], lb[0], lb[1], ALU.max)
            dve.drain()
            for i in range(DEPTH):
                dve.tensor_tensor(small[:, 4 * i:4 * i + 4], lb[i], small[:, 8:12], ALU.subtract)
            dve.drain().then_inc(S("lb_diff"), 1)
            dve.wait_ge(S("lb_exp"), 1)
            dve.tensor_tensor(small[:, 8:12], small[:, 0:4], small[:, 4:8], ALU.add)
            dve.drain()
            dve.reciprocal(small[:, 8:12], small[:, 8:12])
            dve.drain()
            for i in range(DEPTH):
                dve.tensor_tensor(small[:, 4 * i:4 * i + 4], small[:, 4 * i:4 * i + 4], small[:, 8:12], ALU.mult)
            dve.memset(one_lb[:, 0, :], 0.0)
            dve.drain()
            dve.tensor_tensor(one_lb[:, 1, :], small[:, 0:4], small[:, 4:8], ALU.add)
            dve.drain()
            dve.tensor_tensor(one_lb[:, 1, :], one_lb[:, 1, :], small[:, 0:4], ALU.subtract)
            dve.drain()
            dve.tensor_scalar(one_lb[:, :, :], one_lb[:, :, :], -1.0, 1.0, ALU.mult, ALU.add)
            for l in range(DEPTH):
                b3 = cols[:, COL["b_ada"] + 72 * l:COL["b_ada"] + 72 * l + 72].rearrange("p (j w) -> p j w", j=3)
                dve.tensor_scalar(b3[:, :, 8:24], b3[:, :, 8:24], 1.0, None, ALU.add)
            dve.drain()
            dve.wait_ge(S("cond_ready"), 1)
            for i in range(HEAD):
                cond_weigh("head", i, i % 2)
            cond_take("head")
            stage_end(dve, count)
            n = 0
            for l in range(DEPTH):
                if l == 0:
                    first_input()
                for f in range(2):
                    if f == 1:
                        if l == 0:
                            dve.wait_ge(S("bias_flip"), 1)
                            dve.tensor_tensor(biasC[:, :, :], mix[:, 0:2, :].rearrange("p a (b t) -> p (a b) t", b=2), bc(const("causal"), 4), ALU.add)
                        for i in range(CARRY[f"mix{l}"][1]):
                            cond_weigh(f"mix{l}", i, i % 2)
                        cond_take(f"mix{l}")
                        dve.memset(apad[:, :, 0:PAD], 0.0)
                        stage_end(dve, count)
                        pool(l)
                        stage_end(dve, count)
                        attention(l)
                        stage_end(dve, count)
                        hgrn(l)
                        stage_end(dve, count)
                        branch(l)
                        stage_end(dve, count)
                        residual(G[f"mixout{l}"], l, 24 + 16, n)
                        layer_norm(n, l, 1)
                        n += 1

                    def gate_up(it, u, g=G[f"in{l}{f}"]):
                        for i, e in carried(g.name, it, u):
                            cond_weigh(g.name, i, e)
                        if u % 2 == 0:
                            return
                        b = wait_ready(dve, g, it, u)
                        a = g.a0 + u - 1
                        dve.wait_ge(free[a % BANKS], it + (a // BANKS + 1))
                        k = bass.ds(it * 4 + u - 1, 2)
                        h = hid_raw[:, k, :]
                        dve.tensor_tensor(h, h, acc[b][:, :].rearrange("p (a t) -> p a t", a=2), ALU.mult).then_inc(free[b], 1)
                        dve.tensor_copy(hid_hi[:, k, :], h)
                        dve.tensor_tensor(hid_lo[:, k, :], h, hid_hi[:, k, :], ALU.subtract)

                    groups(dve, G[f"in{l}{f}"], gate_up)
                    dve.drain().then_inc(S("hid_ready"), 1)
                    cond_take(f"in{l}{f}")
                    for i in range(CARRY.get(f"out{l}{f}", (0, 0))[1]):
                        cond_weigh(f"out{l}{f}", i, i % 2)
                    residual(G[f"out{l}{f}"], l, 48 * f + 16, n)
                    if f"out{l}{f}" in CARRY:
                        cond_take(f"out{l}{f}")
                    layer_norm(n, l, 2 * f)
                    n += 1
                    if l == DEPTH - 1 and f == 1:
                        dve.wait_ge(S("x_ready"), n)
                        stage_end(dve, count)
            rms = 0
            for l in range(DEPTH):
                mod2 = mods2[:, l, :, :]

                def gains(name, s0):
                    for v in range(2):
                        stt(gain2[:, :, v], mod2[:, s0:s0 + 8, v], 1.0, cols[:, COL[name] + 8 * l:COL[name] + 8 * l + 8], ALU.add, ALU.mult)
                    dve.drain()

                gains("norm_mix_g_2", 8)
                if l == 1:
                    dve.memset(ones_g, 1.0 / 512)
                rms_norm(rms, both)
                rms += 1
                if l == 0:
                    ml_rows()
                    for c in range(KD):
                        dve.wait_ge(S("ml_raw"), c + 1)
                        outer_taps(mqk[:, c, :], mqk_raw[:, c, :], "ml_conv_w_2", c, 8, 2).then_inc(S("ml_conv"), 1)
                    dve.wait_ge(S("ml_bcol"), 1)
                    for t in range(4):
                        dve.eng.tensor_tensor(dcol[:, 8 * t:8 * t + 8].rearrange("p (d w) -> p d w", d=2),
                                              mix[:, 0, 64 + 16 * t:80 + 16 * t].rearrange("p (d w) -> p d w", d=2)[:, :, 0:4],
                                              bcol[:, t, :].rearrange("p (d w) -> p d w", d=2)[:, :, 4:8], ALU.subtract)
                    dve.drain()
                    stage_end(dve, count)
                    gla()
                    mlstm()
                    stage_end(dve, count)
                    add_branch(G["evenout"], mod2[:, 16:24, :], (0, 1))
                else:
                    ssd_rates()
                    stage_end(dve, count)
                    for q in range(6):
                        ssd_conv(0, q)
                    for g in range(4):
                        ssd_group(g)
                    stage_end(dve, count)
                    add_branch(G["ssdout"], mod2[:, 16:24, :], (0,))
                gains("norm_ffn_g_2", 32)
                streams = (0, 1) if l == 0 else (0,)
                rms_norm(rms, both if l == 0 else lat)
                rms += 1
                ffn_up(l)
                add_branch(G[f"down{l}"], mod2[:, 40:48, :], streams)
            rms_norm(rms, lat)


def bucket_of(dist):
    if dist < 16:
        return dist
    large = 16 + int(np.float32(np.log(np.float32(dist) / np.float32(16)) / np.log(128 / 16)) * np.float32(16))
    return min(large, 31)


def constants():
    c = np.zeros((P, NCST), np.float32)

    def put(name, v, off=0):
        c[:v.shape[0], CST[name] + off:CST[name] + off + v.shape[1]] = v

    i = np.arange(P)
    s, t = i[:, None], i[None, :]
    put("ident", (s == t).astype(np.float32))
    put("flip", (s + t == P - 1).astype(np.float32))
    for lv in range(NLEV):
        m = 1 << lv
        f = ((s // (2 * m) == t // (2 * m)) & (s // m % 2 == 0) & (t // m % 2 == 1)).astype(np.float32)
        put("tree_f", f, lv * P)
        put("tree_b", f.T, lv * P)
    j = np.arange(T)[None, :]
    put("causal", np.where(P + s - j < 0, NEG, 0).astype(np.float32))
    for d in range(2):
        for par in range(2):
            ok = j <= P * par + s if d == 0 else j >= P * par + s
            put("mneg", np.where(ok, 0, MASKED).astype(np.float32), (2 * d + par) * T)
    put("tri", (t >= s).astype(np.float32))
    put("tri", (t <= s).astype(np.float32), P)
    for c_ in range(2):
        w = np.array([POOL_WINDOWS[2 * c_ + h] for h in range(2)]).repeat(64)[:, None]
        put("invcnt", (1.0 / np.minimum(j + 1, w)).astype(np.float32), c_ * T)
    dist = np.maximum(T - 1 - np.arange(384), 0)
    put("onehot", (np.arange(32)[:, None] == np.array([bucket_of(int(x)) for x in dist])[None, :]).astype(np.float32))
    put("eps", np.array([[LN_EPS, RMS_EPS, 1.0]], np.float32).repeat(P, 0))
    put("eps", ((i >= 8) & (i < 16)).astype(np.float32)[:, None], 3)
    return c


def panels(w, starts):
    k = w.shape[0]
    out = np.zeros((len(starts), P, k // P, PANEL), w.dtype)
    for n, a in enumerate(starts):
        b = w[:, a:a + PANEL]
        out[n, :, :, :b.shape[1]] = b.reshape(k // P, P, -1).transpose(1, 0, 2)
    return out.reshape(len(starts), P, -1)


def down_panels(w, rows):
    out = [panels(w[r:r + rows], [a]) for a in range(0, w.shape[1], PANEL) for r in range(0, w.shape[0], rows)]
    return np.concatenate(out)


def custom_panel(pieces):
    out = np.zeros((1, P, KD, PANEL), np.float32)
    for w, at in pieces:
        out[0, :, :, at:at + w.shape[1]] = w.reshape(KD, P, -1).transpose(1, 0, 2)
    return out.reshape(1, P, -1)


def weight_stream(x):
    w8, w11, wc = [], [], []
    step = lambda a, n: [a + PANEL * i for i in range(n)]
    for l in range(DEPTH):
        wc.append(panels(x["w_ada"][l], step(0, ADA)))
        pairs = [c for i in range(11) for c in (PANEL * i, D_FF + PANEL * i)]
        m = x["mix_w_in"][l]
        for f in range(2):
            if f == 1:
                w8.append(panels(m, [0, 256, 512, 1024, 1280]))
                w8.append(custom_panel([(m[:, 1536:1600], 0), (m[:, 1536:1600], 64), (m[:, 1600:1608], 128)]))
                w8.append(panels(m, [768, 2632, 2888, 1608, 1864, 3144, 3400, 2120, 2376] + step(3656, 12)))
                w8.append(panels(x["w_branch"][l], step(0, 4)))
                w8.append(panels(x["w_out"][l], step(0, 4)))
            w8.append(panels(x["ffn_w_in"][l, f], pairs))
            w11.append(down_panels(x["ffn_w_out"][l, f], KSPLIT * P))
    for l in range(DEPTH):
        wc.append(panels(x["mod_w_2"][l], step(0, MOD)))
        if l == 0:
            e = x["even_w_in_2"][0]
            w8.append(custom_panel([(e[:, 3584:3600], 0), (x["gla_a1_2"][0, 0], 32), (x["gla_a1_2"][0, 1], 64)]))
            w8.append(panels(e, step(0, 14)))
            w8.append(panels(x["even_w_out_2"][0], step(0, 4)))
        else:
            o = x["ssd_w_in_2"][0]
            w8.append(custom_panel([(o[:, 5120:5184], 0)]))
            for g in range(4):
                w8.append(panels(o, step(2048 + 512 * g, 2)))
                w8.append(custom_panel([(o[:, 4096 + P * g:4096 + P * g + P], 0), (o[:, 4608 + P * g:4608 + P * g + P], P)]))
                w8.append(panels(o, step(512 * g, 2)))
            w8.append(down_panels(x["ssd_w_out_2"][0], KD * P))
        w8.append(panels(x["ffn_w_up_2"][l], pairs))
        w11.append(down_panels(x["ffn_w_down_2"][l], KSPLIT * P))
    return np.concatenate(w8), np.concatenate(w11), np.concatenate(wc)


def vectors(x):
    c = np.zeros((P, NCOL), np.float32)
    for name, n in COL_SPEC:
        v = x[name].reshape(-1)
        if name == "ssd_d_2":
            v = v.repeat(64)
        if n == 1:
            c[:v.size, COL[name]] = v
        else:
            c[:, COL[name]:COL[name] + n] = v.reshape(n, P).T
    return c


def kernel(**inputs):
    import concourse.bacc as bacc
    from concourse.bass_utils import run_bass_kernel_spmd

    x = {k: np.asarray(v) for k, v in inputs.items()}
    arrays = {}
    arrays["w8"], arrays["w11"], arrays["wc"] = weight_stream(x)
    arrays["consts"] = constants()
    arrays["cols"] = vectors(x)
    arrays["xs"] = np.ascontiguousarray(np.concatenate([x["ctx_2"][0].T, x["x"][0].T], axis=1))
    pw = np.zeros((P, DEPTH, 2, P), np.float32)
    for g in range(4):
        r = slice(64 * (g % 2), 64 * (g % 2) + 64)
        pw[r, :, g // 2, r] = x["pool_w"][:, g].transpose(1, 0, 2)
    arrays["poolw"] = pw
    a2 = np.zeros((64, T), np.float32)
    a2[0:16], a2[32:48] = x["gla_a2_2"][0, 0], x["gla_a2_2"][0, 1]
    arrays["a2w"] = a2
    arrays["rel_bias"] = np.ascontiguousarray(x["rel_bias"][:, [0, 2, 1, 3]])
    nc = bacc.Bacc("TRN2", target_bir_lowering=False, num_devices=1)
    io = {}
    for name, a in arrays.items():
        io[name] = nc.dram_tensor(name, a.shape, mybir.dt.from_np(a.dtype), kind="ExternalInput").ap()
    io["out"] = nc.dram_tensor("out", (D, T), F32, kind="ExternalOutput").ap()
    program(nc, io)
    r = run_bass_kernel_spmd(nc, [arrays], core_ids=[0])
    return np.ascontiguousarray(r.results[0]["out"].T)[None]
```
